# Optimizing a Trainium2 kernel written in Bass

```python
import jax, jax.numpy as jnp
from jax import lax
import numpy as np

D_MODEL = 1024
BATCH = 1
SEQ = 1024
DEPTH = 2
DEC_BATCH = 8
DEC_SEQ = 8
PAST_LEN = 512
PAGE_SIZE = 128

N_META = 16
N_EVEN = (DEPTH + 1) // 2
N_ODD = DEPTH // 2
CONV_A_CH = D_MODEL // 2
CONV_A_WIDTH = 31
N_HEADS_B = 8
HEAD_DIM_B = (D_MODEL // 2) // N_HEADS_B
ATT_B_CH = N_HEADS_B * HEAD_DIM_B
Q_BLOCK = 128
FORGET_BIAS_INIT = 3.0
SCONV_CH = D_MODEL // 2
SCONV_WIDTH = 3
POOL_CH = D_MODEL // 2
POOL_WINDOWS = (2, 4, 8, 16)
N_POOL_GROUPS = len(POOL_WINDOWS)
POOL_GROUP_CH = POOL_CH // N_POOL_GROUPS
POOL_HIST = max(POOL_WINDOWS) - 1
D_FF = ((8 * D_MODEL // 3 + 255) // 256) * 256
EVEN_IN = 2 * CONV_A_CH + 3 * ATT_B_CH + N_HEADS_B
EVEN_MIX = CONV_A_CH + ATT_B_CH
ODD_IN = 3 * SCONV_CH + POOL_CH
ODD_MIX = SCONV_CH + POOL_CH
DEEPNORM_ALPHA = float((2 * DEPTH) ** 0.25)
DEEPNORM_BETA = float((8 * DEPTH) ** -0.25)
LN_EPS = 1e-5

kernel_name = "hybrid_conformer_fox_shortconv_pool_step"

def layer_norm(x, g, b):
    xf = x.astype(jnp.float32)
    mu = xf.mean(-1, keepdims=True)
    var = jnp.square(xf - mu).mean(-1, keepdims=True)
    return ((xf - mu) * lax.rsqrt(var + LN_EPS) * g.astype(jnp.float32) + b.astype(jnp.float32)).astype(x.dtype)

def depthwise_causal(x_ext, w):
    c = x_ext.shape[-1]
    return lax.conv_general_dilated(x_ext, w[:, None, :].astype(x_ext.dtype), window_strides=(1,),
                                    padding='VALID', dimension_numbers=('NWC', 'WIO', 'NWC'),
                                    feature_group_count=c)

def fox_attend(q, c_q, pos_q, k, v, c_k, pos_k):
    s = jnp.einsum('bqhd,bkhd->bhqk', q, k).astype(jnp.float32) * (HEAD_DIM_B ** -0.5)
    bias = jnp.transpose(c_q, (0, 2, 1))[:, :, :, None] - jnp.transpose(c_k, (0, 2, 1))[:, :, None, :]
    mask = pos_k[None, :] <= pos_q[:, None]
    s = jnp.where(mask[None, None], s + bias, -jnp.inf)
    p = jax.nn.softmax(s, axis=-1)
    return jnp.einsum('bhqk,bkhd->bqhd', p.astype(v.dtype), v)

def fox_prompt(q, k, v, logf):
    b, s_tot = q.shape[:2]
    n_blocks = (s_tot - N_META) // Q_BLOCK
    c = jnp.cumsum(logf.astype(jnp.float32), axis=1)
    pos = jnp.arange(s_tot)
    meta_out = fox_attend(q[:, :N_META], c[:, :N_META], pos[:N_META],
                          k[:, :N_META], v[:, :N_META], c[:, :N_META], pos[:N_META])
    qb = q[:, N_META:].reshape(b, n_blocks, Q_BLOCK, N_HEADS_B, HEAD_DIM_B).swapaxes(0, 1)
    cb = c[:, N_META:].reshape(b, n_blocks, Q_BLOCK, N_HEADS_B).swapaxes(0, 1)
    pb = pos[N_META:].reshape(n_blocks, Q_BLOCK)
    out = lax.map(lambda a: fox_attend(a[0], a[1], a[2], k, v, c, pos), (qb, cb, pb))
    out = out.swapaxes(0, 1).reshape(b, s_tot - N_META, N_HEADS_B, HEAD_DIM_B)
    return jnp.concatenate([meta_out, out], axis=1)

def even_projections(x, w_in, b_f):
    b, t = x.shape[:2]
    h = x @ w_in
    cuts = [CONV_A_CH, 2 * CONV_A_CH, 2 * CONV_A_CH + ATT_B_CH,
            2 * CONV_A_CH + 2 * ATT_B_CH, 2 * CONV_A_CH + 3 * ATT_B_CH]
    u, g, q, k, v, f = jnp.split(h, cuts, axis=-1)
    a = u * jax.nn.sigmoid(g)
    q = q.reshape(b, t, N_HEADS_B, HEAD_DIM_B)
    k = k.reshape(b, t, N_HEADS_B, HEAD_DIM_B)
    v = v.reshape(b, t, N_HEADS_B, HEAD_DIM_B)
    logf = jax.nn.log_sigmoid((f + b_f).astype(jnp.float32)).astype(x.dtype)
    return a, q, k, v, logf

def conformer_tail(a_ext, w_dw, b_dw, g, b):
    y = depthwise_causal(a_ext, w_dw) + b_dw
    return jax.nn.silu(layer_norm(y, g, b))

def multiscale_pool(p_ext, hist_valid, w_mix, scale):
    b = p_ext.shape[0]
    t_len = p_ext.shape[1] - POOL_HIST
    cs = jnp.cumsum(p_ext.astype(jnp.float32), axis=1)
    cs = jnp.concatenate([jnp.zeros_like(cs[:, :1]), cs], axis=1)
    cur = p_ext[:, POOL_HIST:].astype(jnp.float32)
    t = jnp.arange(t_len)
    outs = []
    for gi, w in enumerate(POOL_WINDOWS):
        sl = slice(gi * POOL_GROUP_CH, (gi + 1) * POOL_GROUP_CH)
        win_sum = cs[:, POOL_HIST + 1:, sl] - cs[:, POOL_HIST + 1 - w:POOL_HIST + 1 - w + t_len, sl]
        count = jnp.minimum(w, hist_valid + t + 1).astype(jnp.float32)
        outs.append(win_sum / count[None, :, None] - cur[:, :, sl])
    d = jnp.stack(outs, axis=2).astype(p_ext.dtype)
    d = jnp.einsum('btgc,gcd->btgd', d, w_mix).reshape(b, t_len, POOL_CH)
    return d * scale

def odd_mixer(x, hist_s, hist_p, hist_valid, w_in, w_sc, w_mix, scale, w_out):
    h = x @ w_in
    hc, bg, cg, pd = jnp.split(h, [SCONV_CH, 2 * SCONV_CH, 3 * SCONV_CH], axis=-1)
    y_ext = jnp.concatenate([hist_s, cg * hc], axis=1)
    out_c = bg * depthwise_causal(y_ext, w_sc)
    p_ext = jnp.concatenate([hist_p, pd], axis=1)
    out_d = multiscale_pool(p_ext, hist_valid, w_mix, scale)
    mix = jnp.concatenate([out_c, out_d], axis=-1) @ w_out
    return mix, y_ext[:, -(SCONV_WIDTH - 1):], p_ext[:, -POOL_HIST:]

def swiglu(x, wg, wu, wd):
    return (jax.nn.silu(x @ wg) * (x @ wu)) @ wd

def setup_inputs(seed: int = 0) -> dict:
    key = jax.random.key(seed)
    ks = iter(jax.random.split(key, 40))

    def nrm(shape, scale=1.0):
        return jax.random.normal(next(ks), shape, jnp.float32) * scale

    n_pages = PAST_LEN // PAGE_SIZE
    n_used = DEC_BATCH * n_pages
    n_phys = n_used + max(1, n_used // 4)
    page_table = jax.random.permutation(next(ks), n_phys)[:n_used].reshape(DEC_BATCH, n_pages).astype(jnp.int32)
    d_in = D_MODEL ** -0.5
    return {
        "x_prompt": nrm((BATCH, SEQ, D_MODEL)),
        "x_sample": nrm((DEC_BATCH, DEC_SEQ, D_MODEL)),
        "cache_k": nrm((n_phys, N_EVEN, PAGE_SIZE, N_HEADS_B, HEAD_DIM_B)),
        "cache_v": nrm((n_phys, N_EVEN, PAGE_SIZE, N_HEADS_B, HEAD_DIM_B)),
        "cache_logf": jax.nn.log_sigmoid(FORGET_BIAS_INIT + nrm((n_phys, N_EVEN, PAGE_SIZE, N_HEADS_B))),
        "page_table": page_table,
        "state_conv_a": nrm((DEC_BATCH, N_EVEN, CONV_A_WIDTH - 1, CONV_A_CH)),
        "state_sconv": nrm((DEC_BATCH, N_ODD, SCONV_WIDTH - 1, SCONV_CH)),
        "state_pool": nrm((DEC_BATCH, N_ODD, POOL_HIST, POOL_CH)),
        "meta_tokens": nrm((N_META, D_MODEL)),
        "w_in_even": nrm((N_EVEN, D_MODEL, EVEN_IN), d_in),
        "b_forget": FORGET_BIAS_INIT + nrm((N_EVEN, N_HEADS_B), 0.5),
        "w_dw_a": nrm((N_EVEN, CONV_A_WIDTH, CONV_A_CH), CONV_A_WIDTH ** -0.5),
        "b_dw_a": nrm((N_EVEN, CONV_A_CH), 0.02),
        "ln_a_g": 1.0 + nrm((N_EVEN, CONV_A_CH), 0.02),
        "ln_a_b": nrm((N_EVEN, CONV_A_CH), 0.02),
        "w_out_even": nrm((N_EVEN, EVEN_MIX, D_MODEL), EVEN_MIX ** -0.5 * DEEPNORM_BETA),
        "w_in_odd": nrm((N_ODD, D_MODEL, ODD_IN), d_in),
        "w_sconv": nrm((N_ODD, SCONV_WIDTH, SCONV_CH), SCONV_WIDTH ** -0.5),
        "w_pool_mix": nrm((N_ODD, N_POOL_GROUPS, POOL_GROUP_CH, POOL_GROUP_CH), POOL_GROUP_CH ** -0.5),
        "pool_scale": 1.0 + nrm((N_ODD, POOL_CH), 0.1),
        "w_out_odd": nrm((N_ODD, ODD_MIX, D_MODEL), ODD_MIX ** -0.5 * DEEPNORM_BETA),
        "ln_mix_g": 1.0 + nrm((DEPTH, D_MODEL), 0.02),
        "ln_mix_b": nrm((DEPTH, D_MODEL), 0.02),
        "w_ffn_gate": nrm((DEPTH, D_MODEL, D_FF), d_in),
        "w_ffn_up": nrm((DEPTH, D_MODEL, D_FF), d_in),
        "w_ffn_down": nrm((DEPTH, D_FF, D_MODEL), D_FF ** -0.5 * DEEPNORM_BETA),
        "ln_ffn_g": 1.0 + nrm((DEPTH, D_MODEL), 0.02),
        "ln_ffn_b": nrm((DEPTH, D_MODEL), 0.02),
    }

def reference(x_prompt, x_sample, cache_k, cache_v, cache_logf, page_table, state_conv_a, state_sconv,
              state_pool, meta_tokens, w_in_even, b_forget, w_dw_a, b_dw_a, ln_a_g, ln_a_b, w_out_even,
              w_in_odd, w_sconv, w_pool_mix, pool_scale, w_out_odd, ln_mix_g, ln_mix_b, w_ffn_gate,
              w_ffn_up, w_ffn_down, ln_ffn_g, ln_ffn_b):
    b = x_prompt.shape[0]
    db, ds = x_sample.shape[:2]
    n_pages = page_table.shape[1]
    past = n_pages * cache_k.shape[2]
    xp = jnp.concatenate([jnp.broadcast_to(meta_tokens[None].astype(x_prompt.dtype), (b, N_META, D_MODEL)),
                          x_prompt], axis=1)
    xs = x_sample
    pos_s_q = past + jnp.arange(ds)
    pos_s_k = jnp.arange(past + ds)

    kp, vp, lfp, cap, scp, plp = [], [], [], [], [], []
    ks_, vs_, lfs, cas, scs, pls = [], [], [], [], [], []
    for layer in range(DEPTH):
        if layer % 2 == 0:
            i = layer // 2
            a, q, k, v, lf = even_projections(xp, w_in_even[i], b_forget[i])
            a_ext = jnp.concatenate([jnp.zeros((b, CONV_A_WIDTH - 1, CONV_A_CH), a.dtype), a], axis=1)
            conv_out = conformer_tail(a_ext, w_dw_a[i], b_dw_a[i], ln_a_g[i], ln_a_b[i])
            att = fox_prompt(q, k, v, lf)
            mix_p = jnp.concatenate([conv_out, att.reshape(b, -1, ATT_B_CH)], axis=-1) @ w_out_even[i]
            kp.append(k); vp.append(v); lfp.append(lf); cap.append(a_ext[:, -(CONV_A_WIDTH - 1):])
            a, q, k, v, lf = even_projections(xs, w_in_even[i], b_forget[i])
            a_ext = jnp.concatenate([state_conv_a[:, i].astype(a.dtype), a], axis=1)
            conv_out = conformer_tail(a_ext, w_dw_a[i], b_dw_a[i], ln_a_g[i], ln_a_b[i])
            k_past = cache_k[page_table, i].reshape(db, past, N_HEADS_B, HEAD_DIM_B)
            v_past = cache_v[page_table, i].reshape(db, past, N_HEADS_B, HEAD_DIM_B)
            lf_past = cache_logf[page_table, i].reshape(db, past, N_HEADS_B)
            k_all = jnp.concatenate([k_past.astype(k.dtype), k], axis=1)
            v_all = jnp.concatenate([v_past.astype(v.dtype), v], axis=1)
            c_all = jnp.cumsum(jnp.concatenate([lf_past.astype(jnp.float32), lf.astype(jnp.float32)], axis=1), axis=1)
            att = fox_attend(q, c_all[:, past:], pos_s_q, k_all, v_all, c_all, pos_s_k)
            mix_s = jnp.concatenate([conv_out, att.reshape(db, ds, ATT_B_CH)], axis=-1) @ w_out_even[i]
            ks_.append(k); vs_.append(v); lfs.append(lf); cas.append(a_ext[:, -(CONV_A_WIDTH - 1):])
        else:
            i = layer // 2
            zs = jnp.zeros((b, SCONV_WIDTH - 1, SCONV_CH), xp.dtype)
            zp = jnp.zeros((b, POOL_HIST, POOL_CH), xp.dtype)
            mix_p, s_new, p_new = odd_mixer(xp, zs, zp, 0, w_in_odd[i], w_sconv[i], w_pool_mix[i],
                                            pool_scale[i], w_out_odd[i])
            scp.append(s_new); plp.append(p_new)
            mix_s, s_new, p_new = odd_mixer(xs, state_sconv[:, i].astype(xs.dtype), state_pool[:, i].astype(xs.dtype),
                                            POOL_HIST, w_in_odd[i], w_sconv[i], w_pool_mix[i],
                                            pool_scale[i], w_out_odd[i])
            scs.append(s_new); pls.append(p_new)
        xp = layer_norm(DEEPNORM_ALPHA * xp + mix_p, ln_mix_g[layer], ln_mix_b[layer])
        xs = layer_norm(DEEPNORM_ALPHA * xs + mix_s, ln_mix_g[layer], ln_mix_b[layer])
        xp = layer_norm(DEEPNORM_ALPHA * xp + swiglu(xp, w_ffn_gate[layer], w_ffn_up[layer], w_ffn_down[layer]),
                        ln_ffn_g[layer], ln_ffn_b[layer])
        xs = layer_norm(DEEPNORM_ALPHA * xs + swiglu(xs, w_ffn_gate[layer], w_ffn_up[layer], w_ffn_down[layer]),
                        ln_ffn_g[layer], ln_ffn_b[layer])

    y_prompt = xp[:, N_META:]
    y_sample = xs
    k_prompt = jnp.stack(kp, axis=1)
    v_prompt = jnp.stack(vp, axis=1)
    logf_prompt = jnp.stack(lfp, axis=1)
    conv_a_prompt = jnp.stack(cap, axis=1)
    sconv_prompt = jnp.stack(scp, axis=1)
    pool_prompt = jnp.stack(plp, axis=1)
    k_sample = jnp.stack(ks_, axis=1)
    v_sample = jnp.stack(vs_, axis=1)
    logf_sample = jnp.stack(lfs, axis=1)
    conv_a_sample = jnp.stack(cas, axis=1)
    sconv_sample = jnp.stack(scs, axis=1)
    pool_sample = jnp.stack(pls, axis=1)
    return (y_prompt, y_sample, k_prompt, v_prompt, logf_prompt, conv_a_prompt, sconv_prompt, pool_prompt,
            k_sample, v_sample, logf_sample, conv_a_sample, sconv_sample, pool_sample)


_drawn_inputs = setup_inputs


def setup_inputs(seed=0):
    import zlib

    import numpy as np

    out = dict(_drawn_inputs(seed))
    spreads = {}
    factors = {'cache_logf': 4.135, 'b_dw_a': 6.636, 'ln_a_g': 8.0, 'ln_a_b': 8.0, 'pool_scale': 2.761}
    for name, (base, spread) in spreads.items():
        noise = np.random.default_rng([zlib.crc32(name.encode()), seed]).standard_normal(out[name].shape)
        drawn = base * np.exp(spread * noise) if base else spread * noise
        out[name] = __import__('jax').numpy.asarray(drawn.astype(out[name].dtype))
    for name, factor in factors.items():
        out[name] = (out[name] * factor).astype(out[name].dtype)
    return out
```

```python
from contextlib import ExitStack

import numpy as np

import concourse.bass as bass
from concourse import mybir

F32 = mybir.dt.float32
F32R = mybir.dt.float32r
I32 = mybir.dt.int32
ALU = mybir.AluOpType
ACT = mybir.ActivationFunctionType
AX_X = mybir.AxisListType.X

P = 128
D = 1024
KT = D // P
META, SEQ = 16, 1024
TP = META + SEQ
NS, NQ = 8, 8
T = TP + NS * NQ
NC = 3
C = T // NC
HALF = D // 2
HT = HALF // P
NH, HD = 8, 64
CW, SW, PW = 31, 3, 16
HA, HS, HP = CW - 1, SW - 1, PW - 1
FF = 2816
NG = FF // P // 2
PAGE, NPAGE = 128, 4
PAST = PAGE * NPAGE
KS = PAST + NQ
ALPHA = float(4 ** 0.25)
EPS = 1e-5
NEG = -float(2 ** 100)
NTT = (T + P - 1) // P
EA, ES, EP = HA + TP + NS * (HA + NQ), HS + TP + NS * (HS + NQ), HP + TP + NS * (HP + NQ)

R_DW, R_BDW, R_LAG, R_LAB, R_SC, R_PS = 0, 31, 32, 33, 34, 37
R_MG, R_MB, R_FG, R_FB, R_ALL = 38, 42, 46, 50, 54

K_ID, K_O1024, K_O512, K_MASK, K_MS, K_MSK, K_CNT, K_ONE, K_SEL, K_ALL = 0, 128, 256, 384, 512, 520, 528, 592, 600, 1112

ST_UG, ST_QKV, ST_OUT0, ST_FF0 = 0, 4, 10, 14
ST_ODD = ST_FF0 + 3 * NG
ST_OUT1 = ST_ODD + 8
ST_FF1 = ST_OUT1 + 4
ST_END = ST_FF1 + 3 * NG
GU_UG, GU_QKV, GU_FF0 = 0, 12, 30
GU_ODD = GU_FF0 + 6 * NG
GU_FF1 = GU_ODD + 24
DN_OUT0, DN_FF0 = 0, 24
DN_OUT1 = DN_FF0 + 24 * NG
DN_FF1 = DN_OUT1 + 24
TU_X, TU_PAR, TU_SA, TU_A, TU_KV, TU_LF, TU_LFS, TU_ST, TU_Y = 0, 18, 19, 21, 23, 41, 42, 43, 45
TAPS = 7
ORDER = (tuple(range(9)), (0, 8, 1, 2, 3, 4, 5, 6, 7))


def constants():
    k = np.zeros((P, K_ALL), np.float32)
    k[:, K_ID:K_ID + P] = np.eye(P)
    k[:, K_O1024:K_O1024 + P] = 1.0 / D
    k[:, K_O512:K_O512 + P] = 1.0 / HALF
    i = np.arange(P)
    k[:, K_MASK:K_MASK + P] = np.where(i[None, :] > i[:, None], NEG, 0.0)
    q = np.arange(64) % NQ
    k[:64, K_MS:K_MS + NQ] = np.where(np.arange(NQ)[None, :] > q[:, None], NEG, 0.0)
    k[:32, K_MSK:K_MSK + NH] = np.arange(NH)[None, :] == (np.arange(32) % NH)[:, None]
    for g, w in enumerate((2, 4, 8, 16)):
        k[:, K_CNT + PW * g:K_CNT + PW * (g + 1)] = 1.0 / np.minimum(w, np.arange(PW) + 1.0)
    k[:, K_ONE] = 1.0
    sel = np.zeros((NS, NH, NS, NH, NQ), np.float32)
    for s in range(NS):
        for h in range(NH):
            sel[s, h, s, h, :] = 1.0
    sel = sel.reshape(64, NS * 64)
    k[:64, K_SEL:] = -sel
    k[64:, K_SEL:] = sel
    return k


def build(nc, t):
    ctx = ExitStack()
    with ctx:
        def at(name, off, shape, dt=F32):
            n = int(np.prod(shape[1:])) * 4
            assert off % 32 == 0 and off + n <= 229344, (name, off, n)
            return nc.alloc_sbuf_tensor_at(name, shape, dt, offset=off), (off + n + 31) // 32 * 32

        def sem(name):
            return ctx.enter_context(nc.semaphore(name))

        CST, o = at("CST", 16512, [P, K_SEL])
        PRT, o = at("PRT", o, [P, HT, R_ALL])
        PTB, o = at("PTB", o, [1, NS * NPAGE], I32)
        BF, o = at("BF", o, [NH, 8])
        assert o <= 21120
        RAW, o = at("RAW", 21120, [P, 4, D])
        WHI, o = at("WHI", o, [P, 4, D], F32R)
        WLO, A0 = at("WLO", o, [P, 4, D], F32R)
        AH, o = at("AH", A0, [P, KT, T], F32R)
        AL, B0 = at("AL", o, [P, KT, T], F32R)
        R0 = B0 + 12 * T * 4
        QKV, _ = at("QKV", B0, [P, 12, T])
        AEXT, o = at("AEXT", R0, [P, HT, EA])
        CACC, _ = at("CACC", o, [P, T])
        STA, _ = at("STA", o, [HA, HALF])
        STB, o = at("STB", o + 2048, [NS * NQ, HALF])
        S, o = at("S", R0 + 26400, [P, 2, C])
        HF, _ = at("HF", o, [P, 2, C])
        ACMP, _ = at("ACMP", o, [P, HT, NS, NQ])
        SELC, _ = at("SELC", o, [P, NS, NH, NQ])
        WFR, o = at("WFR", R0 + 32288, [P, KT, NH])
        WFH, o = at("WFH", o, [P, KT, NH], F32R)
        WFL, o = at("WFL", o, [P, KT, NH], F32R)
        LFR, o = at("LFR", o, [P, NPAGE, NS, NH])
        HH, o = at("HH", B0, [P, 2, T], F32R)
        HL, o = at("HL", o, [P, 2, T], F32R)
        Y, o = at("Y", o, [P, KT, T])
        YC, o = at("YC", R0, [P, KT, C])
        XF, o = at("XF", o, [P, KT, C])
        RSD, o = at("RSD", o, [P, C])
        YS, _ = at("YS", R0 + 32288, [P, 2, C])
        YCA, o = at("YCA", B0 + 4 * T * 4, [P, HT, C])
        SQA, o = at("SQA", o, [P, HT, C])
        YSA, o = at("YSA", o, [P, 2, C])
        RSA, o = at("RSA", o, [P, C])
        XIN, o = at("XIN", B0, [P, 3, D])
        XTT, o = at("XTT", o, [P, 2, KT, P])
        PIN, o = at("PIN", o, [R_ALL, HALF])
        SIN, o = at("SIN", o, [P, 2, HALF])
        STG, o = at("STG", A0, [P, 4, HALF])
        LFZ, o = at("LFZ", o, [NH, 3, T])
        LFC, o = at("LFC", o, [NH, TP])
        LCH, o = at("LCH", o, [NH, TP], F32R)
        LCL, o = at("LCL", o, [NH, TP], F32R)
        LFO, o = at("LFO", o, [P, NTT, NH])
        stage_end = o
        QP, o = at("QP", A0, [P, 2, TP])
        KP, o = at("KP", o, [P, 2, TP])
        VP, o = at("VP", o, [P, 2, NTT, P])
        PB, o = at("PB", o, [P, 3, TP])
        PT, o = at("PT", o, [P, 2, NTT, P])
        assert o >= stage_end
        QB, o = at("QB", o, [32, 2, TP], F32R)
        QBA, o = at("QBA", o, [32, TP])
        KB, o = at("KB", o, [32, TP], F32R)
        IDR, o = at("IDR", o, [P, P], F32R)
        MKR, o = at("MKR", o, [P, P], F32R)
        ST4, o = at("ST4", o, [P, 3, 36])
        assert o <= B0
        KR, o = at("KR", A0, [P, 2, NPAGE, HALF])
        VR, o = at("VR", o, [P, 2, NPAGE + 1, HALF])
        KTS, o = at("KTS", o, [P, 2, HT, KS])
        PSA, o = at("PSA", o, [64, 2, KS])
        PTS, o = at("PTS", o, [P, 2, NPAGE + 1, 64])
        QBD, o = at("QBD", o, [P, 2, 328])
        LFS, o = at("LFS", o, [64, KS])
        KBS, o = at("KBS", o, [P, KS])
        SLS, o = at("SLS", o, [P, 2, 64])
        CQ2, o = at("CQ2", o, [P, NQ])
        ST5, o = at("ST5", o, [64, 2, 8])
        assert o <= B0
        YEXT, o = at("YEXT", B0, [P, HT, ES])
        BG, o = at("BG", o, [P, HT, T])
        PEXT, o = at("PEXT", o, [P, HT, EP])
        T1, o = at("T1", o, [P, EP + 1])
        T2, o = at("T2", o, [P, EP + 1])
        DH, o = at("DH", o, [P, T], F32R)
        DL, o = at("DL", o, [P, T], F32R)
        S1, o = at("S1", o, [P, 2, C])
        WMR, o = at("WMR", o, [P, HT, P])
        WMH, o = at("WMH", o, [P, HT, P], F32R)
        WML, o = at("WML", o, [P, HT, P], F32R)
        OSA, o = at("OSA", o, [P, HALF])
        OSB, o = at("OSB", o, [NS * HS, HALF])
        CMP, o = at("CMP", o, [P, NS * HS + NS * NQ])
        DF = (T1, T2, T1, T2)
        YO, _ = at("YO", A0, [P, 4, D])
        PS = ctx.enter_context(nc.psum_tensor("PS", [P, 8, 512], F32))
        XT = nc.dram_tensor("x_spill", [P, KT, T], F32, kind="Internal").ap()
        LFD = nc.dram_tensor("lf_spill", [NS * NH, NQ], F32, kind="Internal").ap()
        IDN = CST[:, K_ID:K_ID + P]
        ONES_D, ONES_H = CST[:, K_O1024:K_O1024 + P], CST[:, K_O512:K_O512 + P]

        def prompt_cols(tile, h, k, lo, hi, shift=0):
            return tile[:, k, h + lo - shift:h + hi - shift]

        def sample_cols(tile, h, k, shift=0):
            v = tile[:, k, h + TP:h + TP + NS * (h + NQ)].rearrange("p (s e) -> p s e", s=NS)
            return v[:, :, h - shift:h - shift + NQ]

        def history(tile, h, k, s0, n):
            v = tile[:, k, h + TP:h + TP + NS * (h + NQ)].rearrange("p (s e) -> p s e", s=NS)
            return v[:, s0:s0 + n, 0:h]

        def by_seq(ap):
            return ap.rearrange("p (s e) -> p s e", s=NS)

        def row(k, r):
            return PRT[:, k % HT, r + k // HT:r + k // HT + 1]

        s_cst, s_par, s_xin = sem("s_cst"), sem("s_par"), [sem(f"s_xin{i}") for i in range(3)]
        s_sin, s_bf, s_wf, s_ptb, ext_zero = sem("s_sin"), sem("s_bf"), sem("s_wf"), sem("s_ptb"), sem("ext_zero")
        w_loaded = [sem(f"w_loaded{i}") for i in range(4)]
        w_hi, w_lo = sem("w_hi"), sem("w_lo")
        t_done, t_free = sem("t_done"), sem("t_free")
        x_hi, x0_ready, xt_copy = sem("x_hi"), sem("x0_ready"), sem("xt_copy")
        xt_sent = [sem("xt_sent0"), sem("xt_sent1")]
        gu_done, s_ready, gu_free = sem("gu_done"), sem("s_ready"), sem("gu_free")
        hh_ready, h_ready = sem("hh_ready"), sem("h_ready")
        d_done, d_free = sem("d_done"), sem("d_free")
        acmp_ready, sta_sent, acc_step, acc_done, conv_done = (sem("acmp_ready"), sem("sta_sent"), sem("acc_step"),
                                                              sem("acc_done"), sem("conv_done"))
        wf_hi, wf_lo, f_done, f_act, lf_ready, lfo_ready = (sem("wf_hi"), sem("wf_lo"), sem("f_done"), sem("f_act"),
                                                            sem("lf_ready"), sem("lfo_ready"))
        c_ready, c_hi, c_lo, kb_sent, kb_zero, lfd_sent = (sem("c_ready"), sem("c_hi"), sem("c_lo"), sem("kb_sent"),
                                                           sem("kb_zero"), sem("lfd_sent"))
        stg_ready, stg_sent, ab_open = sem("stg_ready"), [sem(f"stg_sent{i}") for i in range(4)], sem("ab_open")
        idr_ready, qp_ready, kp_ready, qb_ready = sem("idr_ready"), sem("qp_ready"), sem("kp_ready"), sem("qb_ready")
        vp_ready = [sem("vp_ready0"), sem("vp_ready1")]
        qk_done, nm_ready, exp_done, rc_ready, pn_ready = (sem("qk_done"), sem("nm_ready"), sem("exp_done"),
                                                           sem("rc_ready"), sem("pn_ready"))
        ta_done, tb_done, pta_ready, ptb_ready = sem("ta_done"), sem("tb_done"), sem("pta_ready"), sem("ptb_ready")
        pv_done, att_evac = sem("pv_done"), sem("att_evac")
        lfr_in, lfs_page, lfs_in, sel_in, cs_ready, cq_ready, sel_ready = (
            sem("lfr_in"), sem("lfs_page"), sem("lfs_in"), sem("sel_in"), sem("cs_ready"), sem("cq_ready"), sem("sel_ready"))
        kr_in, vr_in = [sem("kr_in0"), sem("kr_in1")], [sem("vr_in0"), sem("vr_in1")]
        sk_done, kt_ready, kt_new, qbd_zero, qbd_ready, sls_ready = (sem("sk_done"), sem("kt_ready"), sem("kt_new"),
                                                                     sem("qbd_zero"), sem("qbd_ready"), sem("sls_ready"))
        sqk_done, snm, sexp, src_, spn = sem("sqk_done"), sem("snm"), sem("sexp"), sem("src_"), sem("spn")
        spt_done, spt_ready, spv_done, satt = sem("spt_done"), sem("spt_ready"), sem("spv_done"), sem("satt")
        la_sum, la_mean, la_cen, la_sq, la_sum2, la_var, la_sd, la_rs, la_nrm, la_act, la_hi = (
            sem("la_sum"), sem("la_mean"), sem("la_cen"), sem("la_sq"), sem("la_sum2"), sem("la_var"), sem("la_sd"),
            sem("la_rs"), sem("la_nrm"), sem("la_act"), sem("la_hi"))
        m_ready, y_in = sem("m_ready"), [sem(f"y_in{i}") for i in range(KT)]
        ln_part, ln_sum, ln_mean, ln_cen, ln_sq, ln_sum2, ln_var, ln_sd, ln_rs, ln_nrm = (
            sem("ln_part"), sem("ln_sum"), sem("ln_mean"), sem("ln_cen"), sem("ln_sq"), sem("ln_sum2"), sem("ln_var"),
            sem("ln_sd"), sem("ln_rs"), sem("ln_nrm"))
        ln_xf, ln_hi, x_ready, y_init, xt_spill = sem("ln_xf"), sem("ln_hi"), sem("x_ready"), sem("y_init"), sem("xt_spill")
        od_in, od_zero, wm_in, wm_hi, wm_lo, od_t = (sem("od_in"), sem("od_zero"), sem("wm_in"), sem("wm_hi"),
                                                     sem("wm_lo"), sem("od_t"))
        cmp_ready, ot_done, ot_free, os_sent, df_ready, dh_ready, dl_ready, mix_done, mix_evac, tap = (
            sem("cmp_ready"), sem("ot_done"), sem("ot_free"), sem("os_sent"), sem("df_ready"), sem("dh_ready"),
            sem("dl_ready"), sem("mix_done"), sem("mix_evac"), sem("tap"))
        oc_done = sem("oc_done")
        yo_sent, pool_out = [sem("yo_sent0"), sem("yo_sent1"), sem("yo_sent2"), sem("yo_sent3")], sem("pool_out")

        w_ug = t["w_in_even"][0].rearrange("(k p) n -> p k n", p=P)
        w_odd = t["w_in_odd"][0].rearrange("(k p) n -> p k n", p=P)
        w_out = [t[n][0].rearrange("(k p) n -> p k n", p=P) for n in ("w_out_even", "w_out_odd")]
        w_g = [t["w_ffn_gate"][i].rearrange("(k p) n -> p k n", p=P) for i in range(2)]
        w_u = [t["w_ffn_up"][i].rearrange("(k p) n -> p k n", p=P) for i in range(2)]
        w_d = [t["w_ffn_down"][i] for i in range(2)]

        def raw_cols(pos):
            return RAW[:, pos, :].rearrange("p (k m) -> p k m", k=KT)

        def token_pieces(i):
            lo, hi = i * P, min((i + 1) * P, T)
            spans = [(0, META, "meta_tokens"), (META, TP, "x_prompt"), (TP, T, "x_sample")]
            return [(max(lo, a) - lo, min(hi, b) - max(lo, a), n, max(lo, a) - a)
                    for a, b, n in spans if max(lo, a) < min(hi, b)]

        xsrc = {"meta_tokens": t["meta_tokens"], "x_prompt": t["x_prompt"][0],
                "x_sample": t["x_sample"].rearrange("s q d -> (s q) d")}
        xin_count = [16 * sum(len(token_pieces(j)) for j in range(i % 3, i + 1, 3)) for i in range(NTT)]
        tw = [min(P, T - i * P) for i in range(NTT)]
        YPIECES = [[(16, 112), (128, 128), (256, 112)], [(368, 128), (496, 128), (624, 112)],
                   [(736, 128), (864, 128), (992, 48), (1040, 64)]]
        STG_ALL = (6, 6, 4, 4)

        def att_units():
            na = nb = 0
            for a in range(36):
                i = ORDER[(a // 9) % 2][a % 9]
                groups = (i + 4) // 4
                yield a, (a // 9) % 2, a // 18, i, (P if i < 8 else META), min(P * (i + 1), TP), na, nb
                na += 1 + (groups > 2)
                nb += groups > 1

        ATT = list(att_units())
        NA = ATT[-1][6] + 1 + (ATT[-1][3] == 8)
        NB = ATT[-1][7] + (ATT[-1][3] > 3)

        def chunk(c):
            return slice(c * C, (c + 1) * C)

        def ffn_units(f):
            return (ST_FF0, GU_FF0, DN_FF0) if f == 0 else (ST_FF1, GU_FF1, DN_FF1)

        LN_DONE = [[3 + b + 18 + 2 * c + 2 for c in range(NC)] if f is None else
                   [3 + b + 24 * (NG - 1) + 8 * (c + 1) for c in range(NC)]
                   for b, f in ((DN_OUT0, None), (DN_FF0, 0), (DN_OUT1, None), (DN_FF1, 1))]
        POOL_OUT_ALL = 16 * (2 + NS + 3)
        block = ctx.enter_context(nc.Block())

        @block.sync
        def _(sp):
            def load(n, pos, src):
                sp.wait_ge(w_lo, n - 3)
                sp.dma_start(raw_cols(pos) if len(src.shape) == 3 else RAW[:, pos, :], src).then_inc(w_loaded[pos], 16)

            def cols(w, m):
                return w[:, :, bass.ds(m * P, P)]

            sp.dma_start(CST[:], t["consts"][:, 0:K_SEL]).then_inc(s_cst, 16)
            for i in range(NTT):
                if i >= 3:
                    sp.wait_ge(t_done, 2 * (i - 2))
                for r, n, name, first in token_pieces(i):
                    sp.dma_start(XIN[r:r + n, i % 3, :], xsrc[name][first:first + n, :]).then_inc(s_xin[i % 3], 16)
                if i == 2:
                    for n in range(4):
                        sp.dma_start(raw_cols(n), cols(w_ug, (1 - n % 2) * HT + n // 2)).then_inc(w_loaded[n], 16)
            for n in range(4, 8):
                load(n, n % 4, cols(w_ug, (1 - n % 2) * HT + n // 2))
            with sp.Fori(0, 3) as it:
                for n in range(4):
                    load(2 * ST_QKV + 4 * it + n, n, cols(w_ug, 4 * it + n + 2 * HT))
            for n in range(4):
                load(2 * ST_OUT0 + n, (2 * ST_OUT0 + n) % 4, w_out[0][:, :, n * P:(n + 1) * P])
            vd = t["v_prompt"][0, 0].rearrange("t h d -> t (h d)")
            sp.wait_ge(ab_open, 1)
            with sp.Fori(0, 2) as it:
                sp.wait_ge(pv_done, 1 + 36 * it)
                for j in range(2):
                    c = bass.ds((2 * it + j) * P, P)
                    sp.dma_start(VP[:, j, 0:8, :], vd[0:8 * P].rearrange("(b p) n -> p b n", p=P)[:, :, c]).then_inc(vp_ready[j], 16)
                    sp.dma_start(VP[0:META, j, 8, :], vd[8 * P:TP, c]).then_inc(vp_ready[j], 16)
            sp.wait_ge(s_ptb, 16)
            sp.wait_ge(att_evac, 1 + 72)
            vs = t["v_sample"].rearrange("s a q h d -> (s a) q (h d)")
            with sp.Fori(0, NS // 2) as it:
                for j in range(2):
                    sp.wait_ge(spv_done, 1 + 2 * it)
                    for g in range(NPAGE):
                        r = sp.value_load(PTB[0:1, bass.ds((2 * it + j) * NPAGE + g, 1)], min_val=0,
                                          max_val=t["cache_k"].shape[0] - 1)
                        sp.dma_start(KR[:, j, g, :], t["cache_k"][bass.ds(r, 1)].rearrange("a e p h d -> (a e p) (h d)")).then_inc(kr_in[j], 16)
                        sp.dma_start(VR[:, j, g, :], t["cache_v"][bass.ds(r, 1)].rearrange("a e p h d -> (a e p) (h d)")).then_inc(vr_in[j], 16)
                    sp.dma_start(VR[0:NQ, j, NPAGE, :], vs[bass.ds(2 * it + j, 1)].rearrange("s q n -> (s q) n")).then_inc(vr_in[j], 16)

            def residual(layer):
                sp.wait_ge(m_ready, 12 * (layer + 1))
                for k in range(KT):
                    sp.dma_start(Y[:, k, :], XT[:, k, :]).then_inc(y_in[k], 16)

            def ffn_weights(f):
                st = ffn_units(f)[0]

                def group(n, g, par):
                    for j in range(2):
                        load(n + 2 * j, (par + 2 * j) % 4, cols(w_g[f], 2 * g + j))
                        load(n + 2 * j + 1, (par + 2 * j + 1) % 4, cols(w_u[f], 2 * g + j))
                    for j in range(2):
                        load(n + 4 + j, (par + j) % 4, w_d[f][bass.ds((2 * g + j) * P, P), :])

                with sp.Fori(0, NG // 2) as it:
                    group(2 * st + 12 * it, 2 * it, 2 * st)
                    group(2 * st + 12 * it + 6, 2 * it + 1, 2 * st + 6)
                group(2 * st + 6 * (NG - 1), NG - 1, 2 * st + 6 * (NG - 1))

            sp.wait_ge(xt_sent[0], 16 * 5)
            sp.wait_ge(xt_sent[1], 16 * 4)
            residual(0)
            for n in range(4, 8):
                load(2 * ST_OUT0 + n, (2 * ST_OUT0 + n) % 4, w_out[0][:, :, n * P:(n + 1) * P])
            ffn_weights(0)
            for i in range(HT):
                for j, m in enumerate((2 * HT + i, i, HT + i, 3 * HT + i)):
                    load(2 * ST_ODD + 4 * i + j, (2 * ST_ODD + j) % 4, w_odd[:, :, m * P:(m + 1) * P])
            for n in range(4):
                load(2 * ST_OUT1 + n, (2 * ST_OUT1 + n) % 4, w_out[1][:, :, n * P:(n + 1) * P])
            residual(1)
            for n in range(4, 8):
                load(2 * ST_OUT1 + n, (2 * ST_OUT1 + n) % 4, w_out[1][:, :, n * P:(n + 1) * P])
            ffn_weights(1)

        @block.gpsimd
        def _(gp):
            for r, name, n in ((R_DW, "w_dw_a", CW), (R_BDW, "b_dw_a", 1), (R_LAG, "ln_a_g", 1), (R_LAB, "ln_a_b", 1),
                               (R_SC, "w_sconv", SW), (R_PS, "pool_scale", 1)):
                gp.dma_start(PIN[r:r + n, :], t[name][0] if n > 1 else t[name]).then_inc(s_par, 16)
            for r, name in ((R_MG, "ln_mix_g"), (R_MB, "ln_mix_b"), (R_FG, "ln_ffn_g"), (R_FB, "ln_ffn_b")):
                gp.dma_start(PIN[r:r + 4, :], t[name].rearrange("l (a n) -> (l a) n", a=2)).then_inc(s_par, 16)
            sca = t["state_conv_a"].rearrange("s a e n -> (s a e) n")
            for i in range(2):
                gp.dma_start(SIN[0:4 * HA, i, :], sca[4 * HA * i:4 * HA * (i + 1), :]).then_inc(s_sin, 16)
            gp.dma_start(PTB[:], t["page_table"].rearrange("(a s) g -> a (s g)", a=1)).then_inc(s_ptb, 16)
            with nc.allow_non_contiguous_dma(reason="eight biases, one per partition"):
                gp.dma_start(BF[:, 0:1], t["b_forget"].rearrange("a h -> h a")).then_inc(s_bf, 16)
            gp.dma_start(WFR[:], w_ug[:, :, 5 * HALF:5 * HALF + NH]).then_inc(s_wf, 16)
            gp.memset(AEXT[:, :, 0:HA], 0.0).then_inc(ext_zero, 1)
            gp.dma_start(t["conv_a_sample"][:, 0, 0:HA - NQ, :], t["state_conv_a"][:, 0, NQ:HA, :]).then_inc(pool_out, 16)
            gp.dma_start(t["pool_sample"][:, 0, 0:HP - NQ, :], t["state_pool"][:, 0, NQ:HP, :]).then_inc(pool_out, 16)
            for i in range(NTT):
                gp.wait_ge(xt_copy, 2 * (i + 1))
                gp.dma_start(XT[:, :, i * P:i * P + tw[i]], XTT[:, i % 2, :, 0:tw[i]]).then_inc(xt_sent[i % 2], 16)
            gp.wait_ge(s_ptb, 16)
            with gp.Fori(0, NS) as s:
                for g in range(NPAGE):
                    r = gp.value_load(PTB[0:1, bass.ds(s * NPAGE + g, 1)], min_val=0, max_val=t["cache_logf"].shape[0] - 1)
                    gp.dma_start(LFR[:, g, bass.ds(s, 1), :].rearrange("p a h -> p (a h)"),
                                 t["cache_logf"][bass.ds(r, 1)].rearrange("a e p h -> (a e p) h")).then_inc(lfr_in, 16)
            gp.wait_ge(gu_free, 2 + GU_QKV)
            for k in range(HT):
                gp.tensor_copy(ACMP[:, k, :, :], sample_cols(AEXT, HA, k)).then_inc(acmp_ready, 1)
            gp.wait_ge(t_free, 4 + TU_A + 1)
            gp.dma_start(t["conv_a_prompt"][0, 0], STA[:]).then_inc(sta_sent, 16)
            gp.wait_ge(t_free, 4 + TU_A + 2)
            for s in range(NS):
                gp.dma_start(t["conv_a_sample"][s, 0, HA - NQ:HA, :], STB[s * NQ:(s + 1) * NQ, :]).then_inc(sta_sent, 16)
            for k in range(HT):
                gp.wait_ge(acc_done, k + 1)
                gp.tensor_copy(AEXT[:, k, 0:T], CACC[:]).then_inc(conv_done, 1)
            kv = [t[n][0, 0].rearrange("t h d -> t (h d)") for n in ("k_prompt", "v_prompt")]
            kvs = [t[n].rearrange("s a q h d -> (s a q) (h d)") for n in ("k_sample", "v_sample")]
            for i in range(NTT):
                for j in range(2):
                    u = 2 * i + j
                    gp.wait_ge(t_free, 4 + TU_KV + u + 1)
                    if i < 8:
                        gp.dma_start(kv[j][i * P:(i + 1) * P, :], STG[:, u % 4, :]).then_inc(stg_sent[u % 4], 16)
                    else:
                        gp.dma_start(kv[j][i * P:TP, :], STG[0:META, u % 4, :]).then_inc(stg_sent[u % 4], 16)
                        gp.dma_start(kvs[j], STG[META:META + NS * NQ, u % 4, :]).then_inc(stg_sent[u % 4], 16)
            gp.wait_ge(t_free, 4 + TU_LF + 1)
            gp.dma_start(t["logf_prompt"][0, 0, 0:8 * P].rearrange("(b p) h -> p b h", p=P), LFO[:, 0:8, :]).then_inc(pool_out, 16)
            gp.dma_start(t["logf_prompt"][0, 0, 8 * P:TP], LFO[0:META, 8, :]).then_inc(pool_out, 16)
            gp.dma_start(t["logf_sample"].rearrange("s a q h -> (s a q) h"), LFO[META:META + NS * NQ, 8, :]).then_inc(pool_out, 16)
            for s in range(NS):
                gp.dma_start(LFD[s * NH:(s + 1) * NH, :], LFZ[:, 2, TP + s * NQ:TP + (s + 1) * NQ]).then_inc(lfd_sent, 16)
            gp.memset(KB[:].bitcast(F32), 1.0).then_inc(kb_zero, 1)
            gp.memset(QBA[:], -1.0).then_inc(kb_zero, 1)
            gp.wait_ge(kb_zero, 2)
            gp.wait_ge(c_lo, 1)
            gp.dma_start(KB[0:8, :], LCH[:]).then_inc(kb_sent, 16)
            gp.dma_start(KB[8:16, :], LCL[:]).then_inc(kb_sent, 16)
            gp.dma_start(QBA[16:24, :], LCH[:].bitcast(F32)).then_inc(kb_sent, 16)
            gp.dma_start(QBA[24:32, :], LCL[:].bitcast(F32)).then_inc(kb_sent, 16)
            gp.wait_ge(kb_sent, 64)
            gp.wait_ge(lfd_sent, 16 * NS)
            gp.wait_ge(pool_out, 16 * 5)
            for i in range(4):
                gp.wait_ge(stg_sent[i], 16 * STG_ALL[i])
            gp.sem_inc(ab_open, 1)

            with gp.Fori(0, 2) as it:
                gp.wait_ge(pv_done, 1 + 36 * it)
                for j in range(2):
                    gp.tensor_copy(KP[:, j, :], QKV[:, bass.ds(2 * it + j + HT, 1), 0:TP].rearrange("p a n -> p (a n)")).then_inc(kp_ready, 1)
                for a, h2, j, i, m, n, _, _ in ATT:
                    gp.wait_ge(rc_ready, 36 * it + a + 1)
                    gp.nop(nofuse=True)
                    gp.tensor_scalar(PB[0:m, a % 3, 0:n], PB[0:m, a % 3, 0:n], ST4[0:m, 2, a:a + 1], 1.0,
                                     ALU.mult, ALU.mult).then_inc(pn_ready, 1)
            gp.wait_ge(att_evac, 1 + 72)
            gp.dma_start(SELC[:].rearrange("p s h q -> p (s h q)"), t["consts"][:, K_SEL:K_ALL]).then_inc(sel_in, 16)
            gp.dma_start(LFS[:, PAST:KS], LFD).then_inc(lfs_in, 16)
            gp.memset(QBD[:], 0.0).then_inc(qbd_zero, 1)
            gp.wait_ge(qbd_zero, 1)
            gp.memset(KBS[64:128, :], 1.0).then_inc(qbd_zero, 1)
            gp.wait_ge(qbd_zero, 2)
            gp.wait_ge(sel_ready, 1)
            with gp.Fori(0, NS // 2) as it:
                gp.wait_ge(spv_done, 1 + 2 * it)
                for j in range(2):
                    s = 2 * it + j
                    gp.tensor_copy(SLS[:, j, :], SELC[:, bass.ds(s, 1), :, :].rearrange("p a h q -> p (a h q)")).then_inc(sls_ready, 1)
                    gp.tensor_copy(KTS[:, j, :, PAST:KS], QKV[:, HT:2 * HT, bass.ds(TP + s * NQ, NQ)]).then_inc(kt_new, 1)

            gp.wait_ge(satt, 1 + NS)
            gp.wait_ge(conv_done, HT)
            for c in range(NC):
                if c:
                    gp.wait_ge(la_var, c)
                gp.tensor_tensor(YSA[:], AEXT[:, 0:2, chunk(c)], AEXT[:, 2:4, chunk(c)], ALU.add).then_inc(la_sum, 1)
                gp.wait_ge(la_mean, c + 1)
                gp.wait_ge(la_sq, 2 * (c + 1))
                gp.tensor_tensor(YSA[:], SQA[:, 0:2, :], SQA[:, 2:4, :], ALU.add).then_inc(la_sum2, 1)

            parts = [0]

            def partial(ins):
                parts[0] += 1
                ins.then_inc(ln_part, 1)
                gp.wait_ge(ln_part, parts[0])

            def layer_norm(ln, after=lambda c: None):
                for c in range(NC):
                    cc, k = chunk(c), 3 * ln + c
                    gp.wait_ge(d_free, LN_DONE[ln][c])
                    if k:
                        gp.wait_ge(ln_var, k)
                    partial(gp.tensor_tensor(YS[:], Y[:, 0:2, cc], Y[:, 2:4, cc], ALU.add))
                    partial(gp.tensor_tensor(YS[:], YS[:], Y[:, 4:6, cc], ALU.add))
                    gp.tensor_tensor(YS[:], YS[:], Y[:, 6:8, cc], ALU.add).then_inc(ln_sum, 1)
                    gp.wait_ge(ln_mean, k + 1)
                    gp.wait_ge(ln_sq, 4 * k + 2)
                    partial(gp.tensor_tensor(YS[:], XF[:, 0:2, :], XF[:, 2:4, :], ALU.add))
                    gp.wait_ge(ln_sq, 4 * k + 4)
                    partial(gp.tensor_tensor(YS[:], YS[:], XF[:, 4:6, :], ALU.add))
                    gp.tensor_tensor(YS[:], YS[:], XF[:, 6:8, :], ALU.add).then_inc(ln_sum2, 1)
                    if ln % 2 == 0:
                        for q in range(4):
                            gp.wait_ge(ln_xf, 4 * k + q + 1)
                            gp.tensor_scalar(Y[:, 2 * q:2 * q + 2, cc], XF[:, 2 * q:2 * q + 2, :], ALPHA, 1.0,
                                             ALU.mult, ALU.mult).then_inc(y_init, 1)
                    elif ln == 1:
                        gp.wait_ge(ln_xf, 4 * k + 4)
                        gp.dma_start(XT[:, :, cc], XF[:]).then_inc(xt_spill, 16)
                    after(c)

            layer_norm(0)
            layer_norm(1)
            gp.wait_ge(xt_spill, 48)
            gp.wait_ge(x_ready, 24)
            gp.dma_start(OSB[:], t["state_sconv"].rearrange("s a e n -> (s a e) n")).then_inc(od_in, 16)
            gp.dma_start(OSA[0:NS * HP, :], t["state_pool"].rearrange("s a e n -> (s a e) n")).then_inc(od_in, 16)
            gp.dma_start(WMR[:], t["w_pool_mix"][0].rearrange("g c d -> c g d")).then_inc(wm_in, 16)
            gp.memset(YEXT[:, :, 0:HS], 0.0).then_inc(od_zero, 1)
            gp.memset(PEXT[:, :, 0:HP], 0.0).then_inc(od_zero, 1)
            gp.wait_ge(ot_free, 1 + HT)
            gp.dma_start(t["sconv_prompt"][0, 0], OSA[64:64 + HS, :]).then_inc(os_sent, 16)
            gp.dma_start(t["pool_prompt"][0, 0], OSA[96:96 + HP, :]).then_inc(os_sent, 16)
            gp.dma_start(t["sconv_sample"].rearrange("s a e n -> (s a e) n"), OSB[:]).then_inc(os_sent, 16)
            for s in range(NS):
                gp.dma_start(t["pool_sample"][s, 0, HP - NQ:HP, :], OSA[s * NQ:(s + 1) * NQ, :]).then_inc(os_sent, 16)
            gp.wait_ge(os_sent, 16 * (3 + NS))
            layer_norm(2)

            def store_y(c):
                n = sum(len(YPIECES[x]) for x in range(c))
                for a, w in YPIECES[c]:
                    gp.wait_ge(t_free, 4 + TU_Y + 2 * (n + 1))
                    dst = t["y_prompt"][0, a - META:a - META + w, :] if a < TP else t["y_sample"].rearrange("s q d -> (s q) d")
                    gp.dma_start(dst, YO[0:w, n % 4, :]).then_inc(yo_sent[n % 4], 16)
                    n += 1

            layer_norm(3, store_y)
            for i in range(4):
                gp.wait_ge(yo_sent[i], 16 * len(range(i, sum(map(len, YPIECES)), 4)))
            gp.wait_ge(sta_sent, 16 * (1 + NS))

        @block.tensor
        def _(pe):
            pe.sem_inc(pv_done, 1)
            pe.sem_inc(spv_done, 1)

            def mm3(out, wh, wl, xh, xl, first, last):
                pe.matmul(out, wh, xh, start=first, stop=False)
                pe.matmul(out, wh, xl, start=False, stop=False)
                return pe.matmul(out, wl, xh, start=False, stop=last)

            def transposes(u, bank, pieces):
                pe.wait_ge(t_free, u + 1)
                for out, src, idn in pieces:
                    m = pe.transpose(out, src, idn)
                m.then_inc(t_done, 1)

            def gu_stage(stage, pos, unit, par, before=None):
                pe.wait_ge(w_lo, 2 * stage + 2)
                for c in range(NC):
                    if before:
                        before(c)
                    pe.wait_ge(gu_free, unit + c + 1)
                    for w in range(2):
                        out = PS[:, 2 * ((par + c) % 2) + w, 0:C]
                        for k in range(KT):
                            ks = slice(k * P, (k + 1) * P)
                            m = mm3(out, WHI[:, pos + w, ks], WLO[:, pos + w, ks], AH[:, k, chunk(c)], AL[:, k, chunk(c)],
                                    k == 0, k == KT - 1)
                    m.then_inc(gu_done, 1)

            def ln_products(ln, c, s_sum, s_mean, s_sum2, s_var, s_sd, ones, ys, k):
                if k:
                    pe.wait_ge(s_sd, k)
                for s_in, s_res in ((s_sum, s_mean), (s_sum2, s_var)):
                    pe.wait_ge(s_in, k + 1)
                    pe.matmul(PS[:, 7, 0:C], ones, ys[:, 0, :], start=True, stop=False)
                    pe.matmul(PS[:, 7, 0:C], ones, ys[:, 1, :], start=False, stop=True).then_inc(s_res, 1)

            def ln_mm(ln):
                return lambda c: ln_products(ln, c, ln_sum, ln_mean, ln_sum2, ln_var, ln_sd, ONES_D, YS, 3 * ln + c)

            def with_norm(ln):
                def before(c):
                    ln_mm(ln)(c)
                    pe.wait_ge(x_ready, 12 * ln + 4 * (c + 1))
                return before

            pe.wait_ge(s_cst, 16)
            for i in range(NTT):
                pe.wait_ge(s_xin[i % 3], xin_count[i])
                for h in range(2):
                    u = 2 * i + h
                    transposes(u, 4 + u % 4, [(PS[:, 4 + u % 4, P * j:P * j + tw[i]], XIN[0:tw[i], i % 3, (4 * h + j) * P:(4 * h + j + 1) * P],
                                               IDN[0:tw[i], 0:tw[i]]) for j in range(4)])
            pe.wait_ge(s_par, 160)
            u = TU_PAR
            transposes(u, 4 + u % 4, [(PS[:, 4 + u % 4, R_ALL * j:R_ALL * (j + 1)], PIN[:, j * P:(j + 1) * P], IDN[0:R_ALL, 0:R_ALL])
                                      for j in range(HT)])
            pe.wait_ge(s_sin, 32)
            for i in range(2):
                u, n = TU_SA + i, 4 * HA
                transposes(u, 4 + u % 4, [(PS[:, 4 + u % 4, n * j:n * (j + 1)], SIN[0:n, i, j * P:(j + 1) * P], IDN[0:n, 0:n])
                                          for j in range(HT)])
            with pe.Fori(0, 2) as it:
                for j in range(2):
                    def x_split(c):
                        pe.wait_ge(t_free, 4 + 6 * (c + 1))
                    gu_stage(2 * it + j, 2 * j, 6 * it + 3 * j, 3 * j, x_split)
            pe.wait_ge(gu_free, 2 + GU_QKV)
            u = TU_A
            transposes(u, 4 + u % 4, [(PS[0:HA, 4 + u % 4, k * P:(k + 1) * P], AEXT[:, k, TP:HA + TP], IDN) for k in range(HT)])
            pe.wait_ge(acmp_ready, HT)
            u = TU_A + 1
            transposes(u, 4 + u % 4, [(PS[0:NS * NQ, 4 + u % 4, k * P:(k + 1) * P], ACMP[:, k, :, :].rearrange("p s e -> p (s e)"), IDN)
                                      for k in range(HT)])
            with pe.Fori(0, 3) as it:
                for j in range(2):
                    gu_stage(ST_QKV + 2 * it + j, 2 * j, GU_QKV + 6 * it + 3 * j, 3 * j)
            pe.wait_ge(wf_lo, 1)
            pe.wait_ge(t_free, 4 + TU_KV)
            for c in range(NC):
                for k in range(KT):
                    m = mm3(PS[0:NH, 4 + c, 0:C], WFH[:, k, :], WFL[:, k, :], AH[:, k, chunk(c)], AL[:, k, chunk(c)], k == 0, k == KT - 1)
                m.then_inc(f_done, 1)
            pe.wait_ge(gu_free, 2 + GU_FF0)
            pe.wait_ge(f_act, NC)
            for i in range(NTT):
                for j in range(2):
                    u = TU_KV + 2 * i + j
                    transposes(u, 4 + u % 4, [(PS[0:tw[i], 4 + u % 4, k * P:(k + 1) * P], QKV[:, HT * (1 + j) + k, i * P:i * P + tw[i]], IDN)
                                              for k in range(HT)])
            pe.wait_ge(lf_ready, 1)
            u = TU_LF
            transposes(u, 4 + u % 4, [(PS[0:tw[i], 4 + u % 4, NH * i:NH * (i + 1)], LFZ[:, 2, i * P:i * P + tw[i]], IDN[0:NH, 0:NH])
                                      for i in range(NTT)])

            pe.wait_ge(t_free, 4 + TU_LF + 1)
            pe.wait_ge(idr_ready, 2)

            def scores(it, a, h2, j, i, m, n, na, nb):
                if a % 18 == 0:
                    pe.wait_ge(qp_ready, 2 * it + j + 1)
                    pe.wait_ge(kp_ready, 2 * it + j + 1)
                if a % 9 == 0:
                    pe.wait_ge(qb_ready, 4 * it + a // 9 + 1)
                pe.wait_ge(exp_done, 36 * it + a + 1)
                if i == 8:
                    pe.nop(nofuse=True)
                base, hs, ms = (0, 3)[a % 2], slice(HD * h2, HD * (h2 + 1)), slice(i * P, i * P + m)
                for b in range((n + 511) // 512):
                    lo, hi = 512 * b, min(n, 512 * (b + 1))
                    diag = i * P >= lo and i * P < hi
                    out = PS[0:m, base + b, 0:hi - lo]
                    pe.matmul(out, QP[hs, j, ms], KP[hs, j, lo:hi], start=True, stop=False)
                    if diag:
                        pe.matmul(PS[0:m, base + b, i * P - lo:i * P - lo + m], IDR[:, 0:m], MKR[:, 0:m], start=False, stop=False,
                                  skip_group_check=True)
                    mm = pe.matmul(out, QB[:, h2, ms], KB[:, lo:hi], start=False, stop=True)
                mm.then_inc(qk_done, 1)

            def turn(it, a, h2, j, i, m, n, na, nb):
                pe.wait_ge(pn_ready, 36 * it + a + 1)
                for g in range((i + 4) // 4):
                    if g == 1:
                        pe.wait_ge(ptb_ready, NB * it + nb + 1)
                    else:
                        pe.wait_ge(pta_ready, NA * it + na + g // 2 + 1)
                    if i == 8:
                        pe.nop(nofuse=True)
                    for jt in range(4 * g, min(4 * g + 4, i + 1)):
                        kw = min(P, TP - jt * P)
                        mm = pe.transpose(PS[0:kw, 5 + g % 2, (jt - 4 * g) * P:(jt - 4 * g) * P + m], PB[0:m, a % 3, jt * P:jt * P + kw],
                                          IDN[0:m, 0:m])
                    mm.then_inc(tb_done if g == 1 else ta_done, 1)

            def values(it, a, h2, j, i, m, n, na, nb):
                if a % 18 == 0:
                    pe.wait_ge(vp_ready[j], 32 * it + 32)
                pe.wait_ge(pta_ready, NA * it + na + (2 if i == 8 else 1) + 1)
                if i > 3:
                    pe.wait_ge(ptb_ready, NB * it + nb + 2)
                pe.wait_ge(att_evac, 36 * it + a + 1)
                for jt in range(i + 1):
                    kw = min(P, TP - jt * P)
                    mm = pe.matmul(PS[0:HD, 7, 0:m], VP[0:kw, j, jt, HD * h2:HD * (h2 + 1)], PT[0:kw, a % 2, jt, 0:m],
                                   start=(jt == 0), stop=(jt == i))
                mm.then_inc(pv_done, 1)

            with pe.Fori(0, 2) as it:
                for n in range(36 + 3):
                    if n < 36:
                        scores(it, *ATT[n])
                    if 2 <= n < 38:
                        turn(it, *ATT[n - 2])
                    if n >= 3:
                        values(it, *ATT[n - 3])

            pe.wait_ge(att_evac, 1 + 72)
            pe.wait_ge(lfr_in, 16 * NS * NPAGE)
            u = TU_LFS
            transposes(u, 6, [(PS[0:64, 6, g * P:(g + 1) * P], LFR[:, g, :, :].rearrange("p s h -> p (s h)"), IDN) for g in range(NPAGE)])
            pe.wait_ge(t_free, 4 + TU_LFS + 1)
            pe.wait_ge(qbd_zero, 2)
            with pe.Fori(0, NS // 2) as it:
                for j in range(2):
                    s = 2 * it + j
                    pe.wait_ge(kr_in[j], 64 * it + 64)
                    for c in range(HT):
                        pe.wait_ge(kt_ready, 4 * s + c + 1)
                        for g in range(NPAGE):
                            mm = pe.transpose(PS[:, c, g * P:(g + 1) * P], KR[:, j, g, c * P:(c + 1) * P], IDN)
                        mm.then_inc(sk_done, 1)
                    pe.wait_ge(kt_ready, 4 * s + 8)
                    pe.wait_ge(kt_new, s + 1)
                    pe.wait_ge(qbd_ready, 2 * s + 2)
                    pe.wait_ge(sls_ready, s + 1)
                    pe.wait_ge(sexp, s + 1)
                    for b, lo, hi in ((4, 0, PAST), (5, PAST, KS)):
                        out = PS[0:64, b, 0:hi - lo]
                        for c in range(HT):
                            pe.matmul(out, QBD[:, j, 64 * c:64 * c + 64], KTS[:, j, c, lo:hi], start=(c == 0), stop=False)
                        mm = pe.matmul(out, SLS[:, j, :], KBS[:, lo:hi], start=False, stop=(b == 4))
                    mm = pe.matmul(PS[0:64, 5, 0:NQ], IDN[0:64, 0:64], CST[0:64, K_MS:K_MS + NQ], start=False, stop=True)
                    mm.then_inc(sqk_done, 1)
                for j in range(2):
                    s = 2 * it + j
                    pe.wait_ge(spn, s + 1)
                    pe.wait_ge(spt_ready, s + 1)
                    pe.nop(nofuse=True)
                    for g in range(NPAGE + 1):
                        kw = P if g < NPAGE else NQ
                        mm = pe.transpose(PS[0:kw, 6, 64 * g:64 * g + 64], PSA[:, j, g * P:g * P + kw], IDN[0:64, 0:64])
                    mm.then_inc(spt_done, 1)
                    pe.wait_ge(spt_ready, s + 2)
                    pe.wait_ge(vr_in[j], 80 * it + 80)
                    pe.wait_ge(satt, s + 1)
                    for c in range(HT):
                        for g in range(NPAGE + 1):
                            kw = P if g < NPAGE else NQ
                            mm = pe.matmul(PS[:, 7, 16 * c:16 * c + 16], VR[0:kw, j, g, c * P:(c + 1) * P], PTS[0:kw, j, g, 16 * c:16 * c + 16],
                                           start=(g == 0), stop=(g == NPAGE))
                    mm.then_inc(spv_done, 1)

            pe.wait_ge(satt, 1 + NS)
            for c in range(NC):
                ln_products(0, c, la_sum, la_mean, la_sum2, la_var, la_sd, ONES_H, YSA, c)

            def out_product(layer, st, dn):
                with pe.Fori(0, 2) as it:
                    for j in range(2):
                        pos = 2 * (st + j) % 4
                        pe.wait_ge(w_lo, 2 * (st + 2 * it + j) + 2)
                        for c in range(NC):
                            pe.wait_ge(m_ready, 12 * layer + 4 * (c + 1))
                            for w in range(2):
                                n = 6 * j + 2 * c + w
                                pe.wait_ge(d_free, dn + 12 * it + n + 1)
                                for k in range(KT):
                                    ks = slice(k * P, (k + 1) * P)
                                    m = mm3(PS[:, 4 + n % 3, 0:C], WHI[:, pos + w, ks], WLO[:, pos + w, ks], AH[:, k, chunk(c)],
                                            AL[:, k, chunk(c)], k == 0, k == KT - 1)
                                m.then_inc(d_done, 1)

            def ffn(f):
                st, gu, dn = ffn_units(f)

                def group(g, par, before=None):
                    stage, unit = st + 3 * g, gu + 6 * g
                    for j in range(2):
                        gu_stage(stage + j, 2 * (st + 3 * par + j) % 4, unit + 3 * j, 3 * j, before if j == 0 else None)
                    pos = 2 * (st + 3 * par + 2) % 4
                    pe.wait_ge(w_lo, 2 * stage + 6)
                    for c in range(NC):
                        pe.wait_ge(h_ready, 66 * f + 6 * g + 3 + c + 1)
                        for o in range(KT):
                            n = 8 * c + o
                            pe.wait_ge(d_free, dn + 24 * g + n + 1)
                            for w in range(2):
                                os = slice(o * P, (o + 1) * P)
                                m = mm3(PS[:, 4 + n % 3, 0:C], WHI[:, pos + w, os], WLO[:, pos + w, os], HH[:, w, chunk(c)], HL[:, w, chunk(c)],
                                        w == 0, w == 1)
                            m.then_inc(d_done, 1)

                group(0, 0, with_norm(2 * f))
                with pe.Fori(0, NG // 2) as it:
                    group(2 * it + 1, 1)
                    group(2 * it + 2, 0)

            out_product(0, ST_OUT0, DN_OUT0)
            ffn(0)
            def mix(i):
                pe.wait_ge(gu_free, 2 + GU_ODD + 6 * (i + 1))
                pe.wait_ge(cmp_ready, i + 1)
                pe.wait_ge(ot_free, i + 1)
                pe.transpose(PS[0:NS * NQ, 7, 0:P], CMP[:, NS * HS:], IDN)
                pe.transpose(PS[0:HS, 7, P:2 * P], prompt_cols(YEXT, HS, i, TP - HS, TP), IDN)
                pe.transpose(PS[0:HP, 7, 2 * P:3 * P], prompt_cols(PEXT, HP, i, TP - HP, TP), IDN)
                pe.transpose(PS[0:NS * HS, 7, 3 * P:4 * P], CMP[:, 0:NS * HS], IDN).then_inc(ot_done, 1)
                pe.wait_ge(dl_ready, i + 1)
                for c in range(NC):
                    pe.wait_ge(mix_evac, 3 * i + c + 1)
                    mm3(PS[:, 4 + c, 0:C], WMH[:, i, :], WML[:, i, :], DH[:, chunk(c)], DL[:, chunk(c)], True, True).then_inc(mix_done, 1)

            for i in range(HT):
                gu_stage(ST_ODD + 2 * i, 2 * ST_ODD % 4, GU_ODD + 6 * i, 0, with_norm(1) if i == 0 else None)
                if i == 0:
                    pe.wait_ge(ln_sd, 6)
                    pe.wait_ge(d_free, 3 + DN_OUT1)
                    pe.wait_ge(od_in, 32)
                    transposes(TU_ST, 7, [(PS[:, 7, NS * HS * k:NS * HS * (k + 1)], OSB[:, k * P:(k + 1) * P], IDN[0:NS * HS, 0:NS * HS])
                                          for k in range(HT)])
                    n = NS * HP
                    transposes(TU_ST + 1, 4, [(PS[:, 4, n * k:n * (k + 1)], OSA[0:n, k * P:(k + 1) * P], IDN[0:n, 0:n])
                                              for k in range(HT)])
                gu_stage(ST_ODD + 2 * i + 1, (2 * ST_ODD + 2) % 4, GU_ODD + 6 * i + 3, 1)
                if i == 0:
                    pe.wait_ge(wm_lo, 1)
                    pe.wait_ge(t_free, 4 + TU_ST + 2)
                if i:
                    mix(i - 1)
            mix(HT - 1)
            pe.wait_ge(mix_evac, 3 + 3 * HT)
            out_product(1, ST_OUT1, DN_OUT1)
            ffn(1)
            pe.wait_ge(gu_free, 2 + GU_FF1 + 6 * NG)
            u = TU_Y
            for c in range(NC):
                ln_mm(3)(c)
                pe.wait_ge(ln_xf, 4 * (9 + c) + 4)
                for a, w in YPIECES[c]:
                    for h in range(2):
                        transposes(u, (u - TU_Y) % 4, [(PS[0:w, (u - TU_Y) % 4, k * P:(k + 1) * P], XF[:, 4 * h + k, a - c * C:a - c * C + w], IDN)
                                                       for k in range(4)])
                        u += 1

        @block.scalar
        def _(act):
            act.sem_inc(exp_done, 2)
            act.sem_inc(ptb_ready, 1)
            act.sem_inc(att_evac, 1)
            act.sem_inc(kt_ready, 4)
            act.sem_inc(sexp, 1)
            act.sem_inc(spt_ready, 1)
            act.sem_inc(satt, 1)
            act.sem_inc(mix_evac, 3)

            def split(stage, pos, it2=None):
                for j in range(2):
                    n = 2 * stage + j
                    act.wait_ge(w_loaded[pos + j], 16 * it2 if it2 is not None else 16 * (n // 4 + 1))
                    act.copy(WHI[:, pos + j, :], RAW[:, pos + j, :]).then_inc(w_hi, 1)

            def loads(stage_base, it):
                return stage_base // 2 + it + 1

            def x_tile(i):
                for h in range(2):
                    u = 2 * i + h
                    act.wait_ge(t_done, u + 1)
                    src = PS[:, 4 + u % 4, :].rearrange("p (k n) -> p k n", k=4)[:, :, 0:tw[i]]
                    act.copy(AH[:, 4 * h:4 * h + 4, i * P:i * P + tw[i]], src).then_inc(x_hi, 1)
                    if i >= 2:
                        act.wait_ge(xt_sent[i % 2], 16 * (i // 2))
                    act.copy(XTT[:, i % 2, 4 * h:4 * h + 4, 0:tw[i]], src).then_inc(xt_copy, 1)

            for i in range(3):
                x_tile(i)
            split(0, 0)
            for i in range(3, NTT):
                x_tile(i)

            def gated(unit, par, func, s_tile, bank0_to=None):
                act.wait_ge(gu_done, unit + 1)
                act.activation(s_tile[:, par, :] if bank0_to is None else bank0_to, PS[:, 2 * par, 0:C], func).then_inc(s_ready, 1)

            with act.Fori(0, 2) as it:
                for j in range(2):
                    split(2 * it + j + 1, 2 * (1 - j), loads(0, it) if j == 0 else loads(2, it))
                    for c in range(NC):
                        gated(6 * it + 3 * j + c, (3 * j + c) % 2, ACT.Sigmoid, S)
            act.wait_ge(s_wf, 16)
            act.copy(WFH[:], WFR[:]).then_inc(wf_hi, 1)
            act.wait_ge(xt_sent[0], 16 * 5)
            act.wait_ge(xt_sent[1], 16 * 4)
            act.wait_ge(t_free, 4 + TU_A)
            for it in range(3):
                for j in range(2):
                    st = ST_QKV + 2 * it + j
                    split(st + 1, 2 * (1 - j))
                    for c in range(NC):
                        gated(GU_QKV + 6 * it + 3 * j + c, (3 * j + c) % 2, ACT.Copy, S, QKV[:, 4 * it + 2 * j, chunk(c)])
            act.wait_ge(f_done, NC)
            act.wait_ge(s_bf, 16)
            for c in range(NC):
                act.activation(LFZ[:, 0, chunk(c)], PS[0:NH, 4 + c, 0:C], ACT.Identity, bias=BF[:, 0:1]).then_inc(f_act, 1)
            act.wait_ge(f_act, NC)
            act.activation(LFZ[:, 1, :], LFZ[:, 0, :], ACT.Abs).then_inc(f_act, 1)
            act.wait_ge(f_act, NC + 1)
            act.activation(LFZ[:, 1, :], LFZ[:, 1, :], ACT.Exp, scale=-1.0).then_inc(f_act, 1)
            act.wait_ge(f_act, NC + 2)
            act.activation(LFZ[:, 1, :], LFZ[:, 1, :], ACT.Ln, bias=1.0).then_inc(f_act, 1)
            act.wait_ge(c_ready, 1)
            act.copy(LCH[:], LFC[:]).then_inc(c_hi, 1)

            act.wait_ge(ab_open, 1)
            act.copy(IDR[:], IDN).then_inc(idr_ready, 1)
            act.copy(MKR[:], CST[:, K_MASK:K_MASK + P]).then_inc(idr_ready, 1)

            def expo(it, a, h2, j, i, m, n, na, nb):
                base = (0, 3)[a % 2]
                act.wait_ge(nm_ready, 36 * it + a + 1)
                src = PS[0:m, base:base + (n + 511) // 512, :].rearrange("p b n -> p (b n)")[:, 0:n]
                act.activation(PB[0:m, a % 3, 0:n], src, ACT.Exp, bias=ST4[0:m, 0, a:a + 1],
                               accum_out=ST4[0:m, 1, a:a + 1]).then_inc(exp_done, 1)

            def turned(it, a, h2, j, i, m, n, na, nb):
                if i > 3:
                    act.wait_ge(tb_done, NB * it + nb + 1)
                    w = min(i + 1, 8) - 4
                    act.copy(PT[:, a % 2, 4:4 + w, 0:m], PS[:, 6, :].rearrange("p (k n) -> p k n", k=4)[:, 0:w, 0:m]).then_inc(ptb_ready, 1)

            def result(it, a, h2, j, i, m, n, na, nb):
                act.wait_ge(pv_done, 36 * it + a + 2)
                act.nop(nofuse=True)
                act.activation(QKV[HD * h2:HD * (h2 + 1), bass.ds(2 * it + j, 1), i * P:i * P + m].rearrange("p a n -> p (a n)"),
                               PS[0:HD, 7, 0:m], ACT.Copy).then_inc(att_evac, 1)

            with act.Fori(0, 2) as it:
                act.wait_ge(pv_done, 1 + 36 * it)
                act.nop(nofuse=True)
                for j in range(2):
                    act.mul(QP[:, j, :], QKV[:, bass.ds(2 * it + j, 1), 0:TP].rearrange("p a n -> p (a n)"), HD ** -0.5).then_inc(qp_ready, 1)
                for n in range(36 + 3):
                    if n < 36:
                        expo(it, *ATT[n])
                    if 2 <= n < 38:
                        turned(it, *ATT[n - 2])
                    if n >= 3:
                        result(it, *ATT[n - 3])

            act.wait_ge(cs_ready, 1)
            act.copy(CQ2[64:128, :], KBS[0:64, PAST:KS]).then_inc(cq_ready, 1)
            act.wait_ge(qbd_zero, 1)
            with act.Fori(0, NS // 2) as it:
                act.wait_ge(spv_done, 1 + 2 * it)
                act.nop(nofuse=True)
                for j in range(2):
                    s = 2 * it + j
                    for h2 in range(2):
                        dst = QBD[HD * h2:HD * (h2 + 1), j, 8 * h2:8 * h2 + 320].rearrange("p (c x) -> p c x", x=80)[:, :, 0:NQ]
                        act.mul(dst, QKV[HD * h2:HD * (h2 + 1), 0:HT, bass.ds(TP + s * NQ, NQ)], HD ** -0.5).then_inc(qbd_ready, 1)
                    for c in range(HT):
                        act.wait_ge(sk_done, 4 * s + c + 1)
                        act.copy(KTS[:, j, c, 0:PAST], PS[:, c, :]).then_inc(kt_ready, 1)
                for j in range(2):
                    s = 2 * it + j
                    act.wait_ge(snm, s + 1)
                    act.activation(PSA[:, j, :], PS[0:64, 4:6, :].rearrange("p b n -> p (b n)")[:, 0:KS], ACT.Exp,
                                   bias=ST5[:, j, 0:1], accum_out=ST5[:, j, 1:2]).then_inc(sexp, 1)
                for j in range(2):
                    s = 2 * it + j
                    act.wait_ge(spt_done, s + 1)
                    act.copy(PTS[:, j, 0:NPAGE, :], PS[:, 6, 0:256].rearrange("p (g n) -> p g n", g=NPAGE))
                    act.copy(PTS[0:NQ, j, NPAGE, :], PS[0:NQ, 6, 256:320]).then_inc(spt_ready, 1)
                    act.wait_ge(spv_done, s + 2)
                    act.nop(nofuse=True)
                    for h2 in range(2):
                        src = PS[HD * h2:HD * (h2 + 1), 7, 0:64].rearrange("p (c x) -> p c x", x=16)[:, :, 8 * h2:8 * h2 + NQ]
                        mm = act.activation(QKV[HD * h2:HD * (h2 + 1), 0:HT, bass.ds(TP + s * NQ, NQ)], src, ACT.Copy)
                    mm.then_inc(satt, 1)

            for c in range(NC):
                if c:
                    act.wait_ge(m_ready, 4 * c)
                for q in range(2):
                    act.wait_ge(la_cen, 2 * c + q + 1)
                    act.activation(SQA[:, 2 * q:2 * q + 2, :], YCA[:, 2 * q:2 * q + 2, :], ACT.Square).then_inc(la_sq, 1)
                act.wait_ge(la_var, c + 1)
                act.activation(RSA[:], PS[:, 7, 0:C], ACT.Sqrt, bias=EPS).then_inc(la_sd, 1)
                if c == 0:
                    act.wait_ge(satt, 1 + NS)
                for q in range(2):
                    act.copy(AH[:, HT + 2 * q:HT + 2 * q + 2, chunk(c)], QKV[:, 2 * q:2 * q + 2, chunk(c)]).then_inc(la_hi, 1)
                for k in range(HT):
                    act.wait_ge(la_nrm, 2 * c + k // 2 + 1)
                    act.activation(SQA[:, k, :], YCA[:, k, :], ACT.Silu, bias=row(k, R_LAB), scale=row(k, R_LAG)).then_inc(la_act, 1)
                for q in range(2):
                    act.wait_ge(la_act, 4 * c + 2 * q + 2)
                    act.copy(AH[:, 2 * q:2 * q + 2, chunk(c)], SQA[:, 2 * q:2 * q + 2, :]).then_inc(la_hi, 1)

            def layer_norm(ln, c):
                k = 3 * ln + c
                if k:
                    act.wait_ge(x_ready, min(4 * k, 36))
                if ln % 2 == 0 and c:
                    act.wait_ge(y_init, 12 * (ln // 2) + 4 * c)
                if ln == 1 and c:
                    act.wait_ge(xt_spill, 16 * c)
                if ln == 3 and c:
                    act.wait_ge(t_done, TU_Y + 2 * sum(len(YPIECES[x]) for x in range(c)))
                for q in range(4):
                    act.wait_ge(ln_cen, 4 * k + q + 1)
                    act.activation(XF[:, 2 * q:2 * q + 2, :], YC[:, 2 * q:2 * q + 2, :], ACT.Square).then_inc(ln_sq, 1)
                act.wait_ge(ln_var, k + 1)
                act.activation(RSD[:], PS[:, 7, 0:C], ACT.Sqrt, bias=EPS).then_inc(ln_sd, 1)
                if ln < 3:
                    for q in range(4):
                        act.wait_ge(ln_xf, 4 * k + q + 1)
                        act.copy(AH[:, 2 * q:2 * q + 2, chunk(c)], XF[:, 2 * q:2 * q + 2, :]).then_inc(ln_hi, 1)

            def out_product(st, dn):
                for q in range(4):
                    if q:
                        act.wait_ge(d_done, dn + 6 * q)
                    split(st + q + 1, 2 * (st + q + 1) % 4)

            def hidden(g, f, gu, j, c):
                v, par = 66 * f + 6 * g + 3 * j + c, (3 * j + c) % 2
                gated(gu + 6 * g + 3 * j + c, par, ACT.Silu, S)
                act.wait_ge(gu_free, 2 + gu + 6 * g + 3 * j + c + 1)
                act.copy(HH[:, j, chunk(c)], HF[:, par, :]).then_inc(hh_ready, 1)

            def ffn(f):
                st, gu, dn = ffn_units(f)
                act.wait_ge(d_done, dn)
                split(st + 1, 2 * (st + 1) % 4)
                layer_norm(2 * f, 0)
                layer_norm(2 * f, 1)
                hidden(0, f, gu, 0, 0)
                layer_norm(2 * f, 2)
                hidden(0, f, gu, 0, 1)
                hidden(0, f, gu, 0, 2)
                split(st + 2, 2 * (st + 2) % 4)
                for c in range(NC):
                    hidden(0, f, gu, 1, c)
                split(st + 3, 2 * (st + 3) % 4)

                def group(it, par, last=False):
                    g = 2 * it + (1 if par else 2)
                    for j in range(3):
                        s1 = st + (3 if par else 6) + j + 1
                        if j == 0:
                            act.wait_ge(d_done, dn + 24 * g)
                        for e in range(0 if last and j == 2 else 2):
                            act.wait_ge(w_loaded[2 * s1 % 4 + e], 16 * (s1 // 2 + 1) + 48 * it)
                            act.copy(WHI[:, 2 * s1 % 4 + e, :], RAW[:, 2 * s1 % 4 + e, :]).then_inc(w_hi, 1)
                        if j < 2:
                            for c in range(NC):
                                hidden(g, f, gu, j, c)

                with act.Fori(0, NG // 2 - f) as it:
                    group(it, 1)
                    group(it, 0)
                if f == 1:
                    group(NG // 2 - 1, 1)
                    group(NG // 2 - 1, 0, last=True)

            def mixed(i):
                for c in range(NC):
                    act.wait_ge(mix_done, 3 * i + c + 1)
                    act.activation(YEXT[:, i, chunk(c)], PS[:, 4 + c, 0:C], ACT.Identity, scale=row(i, R_PS)).then_inc(mix_evac, 1)

            out_product(ST_OUT0, DN_OUT0)
            ffn(0)
            act.wait_ge(d_done, DN_OUT1)
            split(ST_ODD + 1, (2 * ST_ODD + 2) % 4)
            for i in range(HT):
                for j in range(2):
                    if i or j:
                        split(ST_ODD + 2 * i + j + 1, 2 * (ST_ODD + j + 1) % 4)
                    else:
                        layer_norm(1, 0)
                        layer_norm(1, 1)
                        layer_norm(1, 2)
                        act.wait_ge(x_ready, 24)
                        act.wait_ge(xt_spill, 48)
                    for c in range(NC):
                        if j == 0:
                            gated(GU_ODD + 6 * i + c, c % 2, ACT.Copy, S1)
                        else:
                            gated(GU_ODD + 6 * i + 3 + c, (3 + c) % 2, ACT.Copy, S1, BG[:, i, chunk(c)])
                if i == 0:
                    act.wait_ge(wm_in, 16)
                    act.copy(WMH[:], WMR[:]).then_inc(wm_hi, 1)
                act.wait_ge(df_ready, i + 1)
                if i:
                    act.wait_ge(mix_done, 3 * i)
                act.copy(DH[:], DF[i][:, 0:T]).then_inc(dh_ready, 1)
                if i:
                    mixed(i - 1)
            mixed(HT - 1)
            act.wait_ge(gu_done, GU_FF1)
            act.wait_ge(mix_evac, 3 + 3 * HT)
            act.wait_ge(oc_done, HT)
            for c in range(NC):
                for q in range(4):
                    src = BG if q < 2 else YEXT
                    act.copy(AH[:, 2 * q:2 * q + 2, chunk(c)], src[:, 2 * q % 4:2 * q % 4 + 2, chunk(c)]).then_inc(la_hi, 1)
            out_product(ST_OUT1, DN_OUT1)
            ffn(1)
            for c in range(NC):
                layer_norm(3, c)

        @block.vector
        def _(dve):
            dve.sem_inc(t_free, 4)
            dve.sem_inc(gu_free, 2)
            dve.sem_inc(d_free, 3)
            dve.sem_inc(pta_ready, 1)
            dve.sem_inc(ot_free, 1)

            def f32(ap):
                return ap.bitcast(F32)

            def two(ap):
                return ap.unsqueeze(1).to_broadcast([P, 2, C])

            def low(out, x, hi):
                return dve.tensor_tensor(out, x, f32(hi), ALU.subtract)

            def split(n, pos):
                for j in range(2):
                    dve.wait_ge(w_hi, n + j + 1)
                    low(WLO[:, pos + j, :], RAW[:, pos + j, :], WHI[:, pos + j, :]).then_inc(w_lo, 1)

            def split_stage(s):
                split(2 * s, 2 * s % 4)

            def x_tile(i):
                for h in range(2):
                    u, cols = 2 * i + h, slice(i * P, i * P + tw[i])
                    dve.wait_ge(xt_copy, u + 1)
                    src = PS[:, 4 + u % 4, :].rearrange("p (k n) -> p k n", k=4)[:, :, 0:tw[i]]
                    low(AL[:, 4 * h:4 * h + 4, cols], src, AH[:, 4 * h:4 * h + 4, cols]).then_inc(t_free, 1)

            for i in range(3):
                x_tile(i)
            split_stage(0)
            for i in range(3, NTT):
                x_tile(i)
            u = TU_PAR
            dve.wait_ge(t_done, u + 1)
            dve.tensor_copy(PRT[:], PS[:, 4 + u % 4, 0:HT * R_ALL].rearrange("p (k n) -> p k n", k=HT)).then_inc(t_free, 1)
            for i in range(2):
                u = TU_SA + i
                dve.wait_ge(t_done, u + 1)
                for k in range(HT):
                    src = PS[:, 4 + u % 4, 4 * HA * k:4 * HA * (k + 1)].rearrange("p (s e) -> p s e", s=4)
                    last = dve.tensor_copy(history(AEXT, HA, k, 4 * i, 4), src)
                last.then_inc(t_free, 1)

            def to_ext(tile, h, k, c, op):
                lo, hi = c * C, min((c + 1) * C, TP)
                last = op(prompt_cols(tile, h, k, lo, hi), slice(0, hi - lo), False)
                if (c + 1) * C > TP:
                    last = op(sample_cols(tile, h, k), slice(TP - lo, C), True)
                return last

            def product(par, s_tile):
                def op(out, cols, seq):
                    a, b = PS[:, 2 * par + 1, cols], s_tile[:, par, cols]
                    return dve.tensor_tensor(out, by_seq(a) if seq else a, by_seq(b) if seq else b, ALU.mult)
                return op

            def plain(par):
                def op(out, cols, seq):
                    a = PS[:, 2 * par + 1, cols]
                    return dve.tensor_copy(out, by_seq(a) if seq else a)
                return op

            for k in range(HT):
                split_stage(k + 1)
                for c in range(NC):
                    n = 3 * k + c
                    dve.wait_ge(s_ready, n + 1)
                    to_ext(AEXT, HA, k, c, product(n % 2, S)).then_inc(gu_free, 1)
            dve.wait_ge(wf_hi, 1)
            low(WFL[:], WFR[:], WFH[:]).then_inc(wf_lo, 1)
            for u, tile, rows in ((TU_A, STA, HA), (TU_A + 1, STB, NS * NQ)):
                dve.wait_ge(t_done, u + 1)
                dve.tensor_copy(tile[:], PS[0:rows, 4 + u % 4, :]).then_inc(t_free, 1)

            def taps():
                steps = 0
                for k in range(HT):
                    dve.wait_ge(ext_zero, 1)
                    if k:
                        dve.wait_ge(conv_done, k)
                    for j in range(CW):
                        dve.wait_ge(acc_step, steps) if steps else dve.wait_ge(sta_sent, 16 * (1 + NS))
                        acc_p, acc_s = CACC[:, 0:TP], by_seq(CACC[:, TP:T])
                        in_p, in_s = prompt_cols(AEXT, HA, k, 0, TP, HA - j), sample_cols(AEXT, HA, k, HA - j)
                        if j == 0:
                            for acc, src in ((acc_p, in_p), (acc_s, in_s)):
                                dve.tensor_scalar(acc, src, row(k, R_DW), row(k, R_BDW), ALU.mult, ALU.add).then_inc(acc_step, 1)
                            steps += 2
                        elif j < CW - 1:
                            for acc, src in ((acc_p, in_p), (acc_s, in_s)):
                                dve.scalar_tensor_tensor(acc, src, row(k, R_DW + j), acc, ALU.mult, ALU.add).then_inc(acc_step, 1)
                            steps += 2
                        else:
                            dve.scalar_tensor_tensor(acc_p, in_p, row(k, R_DW + j), acc_p, ALU.mult, ALU.add)
                            dve.scalar_tensor_tensor(acc_s, in_s, row(k, R_DW + j), acc_s, ALU.mult, ALU.add).then_inc(acc_done, 1)
                        yield

            conv = taps()
            for q in range(6):
                split_stage(ST_QKV + q + 1)
                for c in range(NC):
                    n = 3 * q + c
                    dve.wait_ge(s_ready, GU_QKV + n + 1)
                    dve.tensor_copy(QKV[:, 2 * q + 1, chunk(c)], PS[:, 2 * (n % 2) + 1, 0:C]).then_inc(gu_free, 1)
                    for _ in range(TAPS):
                        next(conv, None)
            for _ in conv:
                pass
            dve.wait_ge(f_act, NC + 3)
            dve.scalar_tensor_tensor(LFZ[:, 2, :], LFZ[:, 0, :], 0.0, LFZ[:, 1, :], ALU.min, ALU.subtract).then_inc(lf_ready, 1)
            dve.wait_ge(lf_ready, 1)
            dve.tensor_tensor_scan(LFC[:], CST[0:NH, K_ONE:K_ONE + 1].to_broadcast([NH, TP]), LFZ[:, 2, 0:TP], 0.0,
                                   ALU.mult, ALU.add).then_inc(c_ready, 1)
            dve.wait_ge(c_hi, 1)
            low(LCL[:], LFC[:], LCH[:]).then_inc(c_lo, 1)
            for n in range(2 * NTT):
                u = TU_KV + n
                dve.wait_ge(t_done, u + 1)
                if n >= 4:
                    dve.wait_ge(stg_sent[n % 4], 16 * (n // 4))
                rows = tw[n // 2]
                dve.tensor_copy(STG[0:rows, n % 4, :], PS[0:rows, 4 + u % 4, :]).then_inc(t_free, 1)
            u = TU_LF
            dve.wait_ge(t_done, u + 1)
            dve.tensor_copy(LFO[:, 0:8, :], PS[:, 4 + u % 4, 0:8 * NH].rearrange("p (b h) -> p b h", b=8))
            dve.tensor_copy(LFO[0:tw[8], 8, :], PS[0:tw[8], 4 + u % 4, 8 * NH:9 * NH]).then_inc(t_free, 1)

            def peak(it, a, h2, j, i, m, n, na, nb):
                base = (0, 3)[a % 2]
                dve.wait_ge(qk_done, 36 * it + a + 1)
                src = PS[0:m, base:base + (n + 511) // 512, :].rearrange("p b n -> p (b n)")[:, 0:n]
                dve.tensor_reduce(ST4[0:m, 0, a:a + 1], src, AX_X, ALU.max, negate=True).then_inc(nm_ready, 1)

            def inverse(it, a, h2, j, i, m, n, na, nb):
                dve.wait_ge(exp_done, 36 * it + a + 3)
                dve.reciprocal(ST4[0:m, 2, a:a + 1], ST4[0:m, 1, a:a + 1]).then_inc(rc_ready, 1)

            def turned(it, a, h2, j, i, m, n, na, nb):
                bank = PS[:, 5, :].rearrange("p (k n) -> p k n", k=4)
                dve.wait_ge(ta_done, NA * it + na + 1)
                w = min(4, i + 1)
                dve.tensor_copy(PT[:, a % 2, 0:w, 0:m], bank[:, 0:w, 0:m]).then_inc(pta_ready, 1)
                if i == 8:
                    dve.wait_ge(ta_done, NA * it + na + 2)
                    dve.tensor_copy(PT[0:META, a % 2, 8, 0:m], PS[0:META, 5, 0:m]).then_inc(pta_ready, 1)

            dve.wait_ge(ab_open, 1)
            with dve.Fori(0, 2) as it:
                for n in range(36 + 2):
                    if n < 36 and n % 18 == 0:
                        for h2 in range(2):
                            head = 4 * it + 2 * (n // 18) + h2
                            dve.tensor_scalar(QB[:, h2, :], QBA[:], CST[0:32, bass.ds(K_MSK + head, 1)], None, ALU.mult).then_inc(qb_ready, 1)
                    if 1 <= n < 37:
                        inverse(it, *ATT[n - 1])
                    if n < 36:
                        peak(it, *ATT[n])
                    if n >= 2:
                        turned(it, *ATT[n - 2])

            dve.wait_ge(t_done, TU_LFS + 1)
            dve.tensor_copy(LFS[:, 0:PAST], PS[0:64, 6, :]).then_inc(t_free, 1)
            dve.wait_ge(t_free, 4 + TU_LFS + 1)
            dve.wait_ge(lfs_in, 16)
            dve.tensor_tensor_scan(KBS[0:64, :], CST[0:64, K_ONE:K_ONE + 1].to_broadcast([64, KS]), LFS[:], 0.0,
                                   ALU.mult, ALU.add).then_inc(cs_ready, 1)
            dve.wait_ge(sel_in, 16)
            dve.wait_ge(cq_ready, 1)
            half = SELC[64:128].rearrange("p s h q -> p (s h) q")
            dve.tensor_tensor(half, half, CQ2[64:128, :].unsqueeze(1).to_broadcast([64, NS * NH, NQ]), ALU.mult).then_inc(sel_ready, 1)
            with dve.Fori(0, NS // 2) as it:
                for j in range(2):
                    s = 2 * it + j
                    dve.wait_ge(sqk_done, s + 1)
                    dve.tensor_reduce(ST5[:, j, 0:1], PS[0:64, 4:6, :].rearrange("p b n -> p (b n)")[:, 0:KS], AX_X, ALU.max,
                                      negate=True).then_inc(snm, 1)
                    dve.wait_ge(sexp, s + 2)
                    dve.reciprocal(ST5[:, j, 2:3], ST5[:, j, 1:2]).then_inc(src_, 1)
                    dve.wait_ge(src_, s + 1)
                    dve.tensor_scalar(PSA[:, j, :], PSA[:, j, :], ST5[:, j, 2:3], None, ALU.mult).then_inc(spn, 1)

            for c in range(NC):
                cc = chunk(c)
                dve.wait_ge(la_mean, c + 1)
                for q in range(2):
                    qs = slice(2 * q, 2 * q + 2)
                    dve.tensor_tensor(YCA[:, qs, :], AEXT[:, qs, cc], two(PS[:, 7, 0:C]), ALU.subtract).then_inc(la_cen, 1)
                dve.wait_ge(la_sd, c + 1)
                dve.reciprocal(RSA[:], RSA[:]).then_inc(la_rs, 1)
                dve.wait_ge(la_rs, c + 1)
                for q in range(2):
                    qs = slice(2 * q, 2 * q + 2)
                    dve.tensor_tensor(YCA[:, qs, :], YCA[:, qs, :], two(RSA[:]), ALU.mult).then_inc(la_nrm, 1)
                for q in range(2):
                    qs, ks = slice(2 * q, 2 * q + 2), slice(HT + 2 * q, HT + 2 * q + 2)
                    dve.wait_ge(la_hi, 4 * c + q + 1)
                    low(AL[:, ks, cc], QKV[:, qs, cc], AH[:, ks, cc]).then_inc(m_ready, 1)
                for q in range(2):
                    qs = slice(2 * q, 2 * q + 2)
                    dve.wait_ge(la_hi, 4 * c + 2 + q + 1)
                    low(AL[:, qs, cc], SQA[:, qs, :], AH[:, qs, cc]).then_inc(m_ready, 1)

            def layer_norm(ln, c):
                k, cc, layer = 3 * ln + c, chunk(c), ln // 2
                g, b = ((R_MG, R_MB), (R_FG, R_FB))[ln % 2]
                dve.wait_ge(ln_mean, k + 1)
                for q in range(4):
                    qs = slice(2 * q, 2 * q + 2)
                    dve.tensor_tensor(YC[:, qs, :], Y[:, qs, cc], two(PS[:, 7, 0:C]), ALU.subtract).then_inc(ln_cen, 1)
                dve.wait_ge(ln_sd, k + 1)
                dve.reciprocal(RSD[:], RSD[:]).then_inc(ln_rs, 1)
                dve.wait_ge(ln_rs, k + 1)
                for q in range(4):
                    qs = slice(2 * q, 2 * q + 2)
                    dve.tensor_tensor(YC[:, qs, :], YC[:, qs, :], two(RSD[:]), ALU.mult).then_inc(ln_nrm, 1)
                for q in range(4):
                    dve.wait_ge(ln_nrm, 4 * k + q + 1)
                    for o in (2 * q, 2 * q + 1):
                        last = dve.tensor_scalar(XF[:, o, :], YC[:, o, :], row(o, g + 2 * layer), row(o, b + 2 * layer), ALU.mult, ALU.add)
                    last.then_inc(ln_xf, 1)
                if ln < 3:
                    for q in range(4):
                        qs = slice(2 * q, 2 * q + 2)
                        dve.wait_ge(ln_hi, 4 * k + q + 1)
                        low(AL[:, qs, cc], XF[:, qs, :], AH[:, qs, cc]).then_inc(x_ready, 1)

            def out_product(layer, st, dn):
                for q in range(4):
                    split_stage(st + q + 1)
                    for c in range(NC):
                        for w in range(2):
                            n, o = 6 * q + 2 * c + w, 2 * q + w
                            if c == 0:
                                dve.wait_ge(y_in[o], 16 * (layer + 1))
                            dve.wait_ge(d_done, dn + n + 1)
                            y = Y[:, o, chunk(c)]
                            dve.scalar_tensor_tensor(y, y, ALPHA, PS[:, 4 + n % 3, 0:C], ALU.mult, ALU.add).then_inc(d_free, 1)

            def hidden(g, f, gu, j, c):
                unit, v, par = gu + 6 * g + 3 * j + c, 66 * f + 6 * g + 3 * j + c, (3 * j + c) % 2
                dve.wait_ge(s_ready, unit + 1)
                dve.tensor_tensor(HF[:, par, :], S[:, par, :], PS[:, 2 * par + 1, 0:C], ALU.mult).then_inc(gu_free, 1)
                dve.wait_ge(hh_ready, v + 1)
                low(HL[:, j, chunk(c)], HF[:, par, :], HH[:, j, chunk(c)]).then_inc(h_ready, 1)

            def down(g, f, dn, first=False):
                for c in range(NC):
                    if first:
                        dve.wait_ge(y_init, 12 * f + 4 * (c + 1))
                    for o in range(KT):
                        n = 8 * c + o
                        dve.wait_ge(d_done, dn + 24 * g + n + 1)
                        y = Y[:, o, chunk(c)]
                        dve.tensor_tensor(y, y, PS[:, 4 + n % 3, 0:C], ALU.add).then_inc(d_free, 1)

            def ffn(f):
                st, gu, dn = ffn_units(f)
                split_stage(st + 1)
                layer_norm(2 * f, 0)
                layer_norm(2 * f, 1)
                hidden(0, f, gu, 0, 0)
                layer_norm(2 * f, 2)
                hidden(0, f, gu, 0, 1)
                hidden(0, f, gu, 0, 2)
                split_stage(st + 2)
                for c in range(NC):
                    hidden(0, f, gu, 1, c)
                split_stage(st + 3)
                down(0, f, dn, first=True)

                def group(it, par, last=False):
                    g = 2 * it + (1 if par else 2)
                    for j in range(3):
                        s1 = st + (3 if par else 6) + j + 1
                        if not (last and j == 2):
                            split(2 * s1 + 12 * it, 2 * s1 % 4)
                        if j < 2:
                            for c in range(NC):
                                hidden(g, f, gu, j, c)
                    down(g, f, dn)

                with dve.Fori(0, NG // 2 - f) as it:
                    group(it, 1)
                    group(it, 0)
                if f == 1:
                    group(NG // 2 - 1, 1)
                    group(NG // 2 - 1, 0, last=True)

            out_product(0, ST_OUT0, DN_OUT0)
            ffn(0)

            steps = [0]

            def step(ins):
                steps[0] += 1
                ins.then_inc(tap, 1)
                dve.wait_ge(tap, steps[0])

            def new_rows(i):
                dve.wait_ge(ot_done, i + 1)
                cs = slice(i * P, (i + 1) * P)
                dve.tensor_copy(OSA[0:NS * NQ, cs], PS[0:NS * NQ, 7, 0:P])
                dve.tensor_copy(OSA[64:64 + HS, cs], PS[0:HS, 7, P:2 * P])
                dve.tensor_copy(OSA[96:96 + HP, cs], PS[0:HP, 7, 2 * P:3 * P])
                dve.tensor_copy(OSB[:, cs], PS[0:NS * HS, 7, 3 * P:4 * P]).then_inc(ot_free, 1)

            split_stage(ST_ODD + 1)
            for c in range(NC):
                layer_norm(1, c)
            dve.wait_ge(xt_spill, 48)
            for i in range(HT):
                for j in range(2):
                    if i or j:
                        split_stage(ST_ODD + 2 * i + j + 1)
                    for c in range(NC):
                        n = 6 * i + 3 * j + c
                        dve.wait_ge(s_ready, GU_ODD + n + 1)
                        if j == 0:
                            to_ext(YEXT, HS, i, c, product(n % 2, S1)).then_inc(gu_free, 1)
                        else:
                            to_ext(PEXT, HP, i, c, plain(n % 2)).then_inc(gu_free, 1)
                    if i == 0 and j == 0:
                        for u, bank, tile, h in ((TU_ST, 7, YEXT, HS), (TU_ST + 1, 4, PEXT, HP)):
                            dve.wait_ge(t_done, u + 1)
                            for k in range(HT):
                                last = dve.tensor_copy(history(tile, h, k, 0, NS), by_seq(PS[:, bank, NS * h * k:NS * h * (k + 1)]))
                            last.then_inc(t_free, 1)
                        dve.wait_ge(od_zero, 2)
                if i == 0:
                    dve.wait_ge(wm_hi, 1)
                    low(WML[:], WMR[:], WMH[:]).then_inc(wm_lo, 1)
                    dve.wait_ge(t_free, 4 + TU_ST + 2)
                if i:
                    dve.wait_ge(ot_done, i)
                dve.wait_ge(gu_free, 2 + GU_ODD + 6 * (i + 1))
                y_new, p_new = sample_cols(YEXT, HS, i), sample_cols(PEXT, HP, i)
                dve.tensor_copy(by_seq(CMP[:, 0:NS * HS]), y_new[:, :, NQ - HS:])
                dve.tensor_copy(by_seq(CMP[:, NS * HS:]), p_new).then_inc(cmp_ready, 1)
                if i:
                    dve.wait_ge(dh_ready, i)
                    new_rows(i - 1)
                for j in range(SW):
                    for acc, src in ((T1[:, 0:TP], prompt_cols(YEXT, HS, i, 0, TP, HS - j)),
                                     (by_seq(T1[:, TP:T]), sample_cols(YEXT, HS, i, HS - j))):
                        if j == 0:
                            step(dve.tensor_scalar(acc, src, row(i, R_SC), None, ALU.mult))
                        else:
                            step(dve.scalar_tensor_tensor(acc, src, row(i, R_SC + j), acc, ALU.mult, ALU.add))
                dve.tensor_tensor(BG[:, i, :], BG[:, i, :], T1[:, 0:T], ALU.mult).then_inc(oc_done, 1)
                src, lo = PEXT[:, i, :], 0
                for d in range(i + 1):
                    w, dst = 1 << d, (T2, T1)[d % 2]
                    step(dve.tensor_tensor(dst[:, lo + w:EP], src[:, lo + w:EP], src[:, lo:EP - w], ALU.add))
                    src, lo = dst, lo + w
                w, df = 2 << i, DF[i]
                first = src[:, HP:HP + PW]
                step(dve.tensor_tensor(first, first, CST[:, K_CNT + PW * i:K_CNT + PW * (i + 1)], ALU.mult))
                dve.tensor_tensor(df[:, 0:PW], first, PEXT[:, i, HP:HP + PW], ALU.subtract)
                dve.scalar_tensor_tensor(df[:, PW:TP], src[:, HP + PW:HP + TP], 1.0 / w, PEXT[:, i, HP + PW:HP + TP], ALU.mult, ALU.subtract)
                sums = src[:, HP + TP:EP].rearrange("p (s e) -> p s e", s=NS)[:, :, HP:]
                dve.scalar_tensor_tensor(by_seq(df[:, TP:T]), sums, 1.0 / w, p_new, ALU.mult, ALU.subtract).then_inc(df_ready, 1)
                dve.wait_ge(dh_ready, i + 1)
                if i:
                    dve.wait_ge(mix_done, 3 * i)
                low(DL[:], df[:, 0:T], DH[:]).then_inc(dl_ready, 1)
            new_rows(HT - 1)
            for c in range(NC):
                for q in range(4):
                    src = BG if q < 2 else YEXT
                    dve.wait_ge(la_hi, 12 + 4 * c + q + 1)
                    qs = slice(2 * q, 2 * q + 2)
                    low(AL[:, qs, chunk(c)], src[:, 2 * q % 4:2 * q % 4 + 2, chunk(c)], AH[:, qs, chunk(c)]).then_inc(m_ready, 1)
            out_product(1, ST_OUT1, DN_OUT1)
            ffn(1)
            n = 0
            for c in range(NC):
                layer_norm(3, c)
                for a, w in YPIECES[c]:
                    for h in range(2):
                        u = 2 * n + h
                        dve.wait_ge(t_done, TU_Y + u + 1)
                        if n >= 4:
                            dve.wait_ge(yo_sent[n % 4], 16 * (n // 4))
                        dve.tensor_copy(YO[0:w, n % 4, h * HALF:(h + 1) * HALF], PS[0:w, u % 4, :]).then_inc(t_free, 1)
                    n += 1


_INS = ["x_prompt", "x_sample", "cache_k", "cache_v", "cache_logf", "page_table", "state_conv_a", "state_sconv", "state_pool",
        "meta_tokens", "w_in_even", "b_forget", "w_dw_a", "b_dw_a", "ln_a_g", "ln_a_b", "w_out_even", "w_in_odd", "w_sconv",
        "w_pool_mix", "pool_scale", "w_out_odd", "ln_mix_g", "ln_mix_b", "w_ffn_gate", "w_ffn_up", "w_ffn_down", "ln_ffn_g",
        "ln_ffn_b"]
_OUTS = [("y_prompt", (1, SEQ, D)), ("y_sample", (NS, NQ, D)), ("k_prompt", (1, 1, TP, NH, HD)), ("v_prompt", (1, 1, TP, NH, HD)),
         ("logf_prompt", (1, 1, TP, NH)), ("conv_a_prompt", (1, 1, HA, HALF)), ("sconv_prompt", (1, 1, HS, HALF)),
         ("pool_prompt", (1, 1, HP, HALF)), ("k_sample", (NS, 1, NQ, NH, HD)), ("v_sample", (NS, 1, NQ, NH, HD)),
         ("logf_sample", (NS, 1, NQ, NH)), ("conv_a_sample", (NS, 1, HA, HALF)), ("sconv_sample", (NS, 1, HS, HALF)),
         ("pool_sample", (NS, 1, HP, HALF))]


def kernel(**inputs):
    import concourse.bacc as bacc
    from concourse.bass_utils import run_bass_kernel_spmd

    nc = bacc.Bacc("TRN2", target_bir_lowering=False, num_devices=1)
    arrays, aps = {}, {}
    for name in _INS + ["consts"]:
        a = constants() if name == "consts" else np.ascontiguousarray(inputs[name])
        arrays[f"in_{name}"] = a
        aps[name] = nc.dram_tensor(f"in_{name}", a.shape, mybir.dt.from_np(a.dtype), kind="ExternalInput").ap()
    for name, shape in _OUTS:
        aps[name] = nc.dram_tensor(f"out_{name}", shape, F32, kind="ExternalOutput").ap()
    build(nc, aps)
    r = run_bass_kernel_spmd(nc, [arrays], core_ids=[0])
    return tuple(r.results[0][f"out_{name}"] for name, _ in _OUTS)
```

```python
from contextlib import ExitStack

import numpy as np

import concourse.bass as bass
from concourse import mybir

F32 = mybir.dt.float32
F32R = mybir.dt.float32r
I32 = mybir.dt.int32
ALU = mybir.AluOpType
ACT = mybir.ActivationFunctionType
AX_X = mybir.AxisListType.X

P = 128
D = 1024
KT = D // P
META, SEQ = 16, 1024
TP = META + SEQ
NS, NQ = 8, 8
T = TP + NS * NQ
NC = 3
C = T // NC
HALF = D // 2
HT = HALF // P
NH, HD = 8, 64
CW, SW, PW = 31, 3, 16
HA, HS, HP = CW - 1, SW - 1, PW - 1
FF = 2816
NG = FF // P // 2
PAGE, NPAGE = 128, 4
PAST = PAGE * NPAGE
KS = PAST + NQ
ALPHA = float(4 ** 0.25)
EPS = 1e-5
NEG = -float(2 ** 100)
NTT = (T + P - 1) // P
EA, ES, EP = HA + TP + NS * (HA + NQ), HS + TP + NS * (HS + NQ), HP + TP + NS * (HP + NQ)

R_DW, R_BDW, R_LAG, R_LAB, R_SC, R_PS = 0, 31, 32, 33, 34, 37
R_MG, R_MB, R_FG, R_FB, R_ALL = 38, 42, 46, 50, 54

K_ID, K_O1024, K_O512, K_MASK, K_MS, K_MSK, K_CNT, K_ONE, K_SEL, K_ALL = 0, 128, 256, 384, 512, 520, 528, 592, 600, 1112

ST_UG, ST_QKV, ST_OUT0, ST_FF0 = 0, 4, 10, 14
ST_ODD = ST_FF0 + 3 * NG
ST_OUT1 = ST_ODD + 8
ST_FF1 = ST_OUT1 + 4
ST_END = ST_FF1 + 3 * NG
GU_UG, GU_QKV, GU_FF0 = 0, 12, 30
GU_ODD = GU_FF0 + 6 * NG
GU_FF1 = GU_ODD + 24
DN_OUT0, DN_FF0 = 0, 24
DN_OUT1 = DN_FF0 + 24 * NG
DN_FF1 = DN_OUT1 + 24
TU_X, TU_PAR, TU_SA, TU_A, TU_KV, TU_LF, TU_LFS, TU_ST, TU_Y = 0, 18, 19, 21, 23, 41, 42, 43, 45
TAPS = 6
ORDER = (tuple(range(9)), (0, 8, 1, 2, 3, 4, 5, 6, 7))


def constants():
    k = np.zeros((P, K_ALL), np.float32)
    k[:, K_ID:K_ID + P] = np.eye(P)
    k[:, K_O1024:K_O1024 + P] = 1.0 / D
    k[:, K_O512:K_O512 + P] = 1.0 / HALF
    i = np.arange(P)
    k[:, K_MASK:K_MASK + P] = np.where(i[None, :] > i[:, None], NEG, 0.0)
    q = np.arange(64) % NQ
    k[:64, K_MS:K_MS + NQ] = np.where(np.arange(NQ)[None, :] > q[:, None], NEG, 0.0)
    k[:32, K_MSK:K_MSK + NH] = np.arange(NH)[None, :] == (np.arange(32) % NH)[:, None]
    for g, w in enumerate((2, 4, 8, 16)):
        k[:, K_CNT + PW * g:K_CNT + PW * (g + 1)] = 1.0 / np.minimum(w, np.arange(PW) + 1.0)
    k[:, K_ONE] = 1.0
    sel = np.zeros((NS, NH, NS, NH, NQ), np.float32)
    for s in range(NS):
        for h in range(NH):
            sel[s, h, s, h, :] = 1.0
    sel = sel.reshape(64, NS * 64)
    k[:64, K_SEL:] = -sel
    k[64:, K_SEL:] = sel
    return k


def build(nc, t):
    ctx = ExitStack()
    with ctx:
        def at(name, off, shape, dt=F32):
            n = int(np.prod(shape[1:])) * 4
            assert off % 32 == 0 and off + n <= 229344, (name, off, n)
            return nc.alloc_sbuf_tensor_at(name, shape, dt, offset=off), (off + n + 31) // 32 * 32

        def sem(name):
            return ctx.enter_context(nc.semaphore(name))

        CST, o = at("CST", 16512, [P, K_SEL])
        PRT, o = at("PRT", o, [P, HT, R_ALL])
        PTB, o = at("PTB", o, [1, NS * NPAGE], I32)
        BF, o = at("BF", o, [NH, 8])
        assert o <= 21120
        RAW, o = at("RAW", 21120, [P, 4, D])
        WHI, o = at("WHI", o, [P, 4, D], F32R)
        WLO, A0 = at("WLO", o, [P, 4, D], F32R)
        AH, o = at("AH", A0, [P, KT, T], F32R)
        AL, B0 = at("AL", o, [P, KT, T], F32R)
        R0 = B0 + 12 * T * 4
        QKV, _ = at("QKV", B0, [P, 12, T])
        AEXT, o = at("AEXT", R0, [P, HT, EA])
        CACC, _ = at("CACC", o, [P, T])
        STA, o = at("STA", B0 + 11 * T * 4, [HA, HALF])
        STB, _ = at("STB", o, [NS * NQ, HALF])
        S, o = at("S", R0 + 26400, [P, 2, C])
        HF, _ = at("HF", o, [P, 2, C])
        ACMP, _ = at("ACMP", o, [P, HT, NS, NQ])
        SELC, _ = at("SELC", o, [P, NS, NH, NQ])
        WFR, o = at("WFR", R0 + 32288, [P, KT, NH])
        WFH, o = at("WFH", o, [P, KT, NH], F32R)
        WFL, o = at("WFL", o, [P, KT, NH], F32R)
        LFR, o = at("LFR", o, [P, NPAGE, NS, NH])
        HH, o = at("HH", B0, [P, 2, T], F32R)
        HL, o = at("HL", o, [P, 2, T], F32R)
        Y, o = at("Y", o, [P, KT, T])
        SQ, o = at("SQ", R0, [P, KT, C])
        RSD, o = at("RSD", o, [P, 2, C])
        YSM, o = at("YSM", o, [P, 2, C])
        YSV, o = at("YSV", o, [P, 2, C])
        YCA, o = at("YCA", B0 + 4 * T * 4, [P, HT, C])
        SQA, o = at("SQA", o, [P, HT, C])
        YSA, o = at("YSA", o, [P, 2, C])
        RSA, o = at("RSA", o, [P, C])
        XIN, o = at("XIN", B0, [P, 3, D])
        XTT, o = at("XTT", o, [P, 2, KT, P])
        PIN, o = at("PIN", o, [R_ALL, HALF])
        SIN, o = at("SIN", o, [P, 2, HALF])
        STG, o = at("STG", A0, [P, 4, HALF])
        LFZ, o = at("LFZ", o, [NH, 3, T])
        LFC, o = at("LFC", o, [NH, TP])
        LCH, o = at("LCH", o, [NH, TP], F32R)
        LCL, o = at("LCL", o, [NH, TP], F32R)
        LFO, o = at("LFO", o, [P, NTT, NH])
        stage_end = o
        QS1, o = at("QS1", A0, [P, 2, TP], F32R)
        KS1, o = at("KS1", o, [P, 2, TP], F32R)
        QS2, o = at("QS2", o, [96, 2, TP], F32R)
        PB, o = at("PB", o, [P, 3, TP])
        assert o >= stage_end
        VP, o = at("VP", o, [P, 2, NTT, P])
        PT, o = at("PT", o, [P, 2, NTT, P])
        KS2, o = at("KS2", o, [96, 2, TP], F32R)
        QBA, o = at("QBA", o, [32, TP])
        IDR, o = at("IDR", o, [P, P], F32R)
        MKR, o = at("MKR", o, [P, P], F32R)
        ST4, o = at("ST4", o, [P, 3, 36])
        assert o <= B0
        KR, o = at("KR", A0, [P, 2, NPAGE, HALF])
        VR, o = at("VR", o, [P, 2, NPAGE + 1, HALF])
        KTS, o = at("KTS", o, [P, 2, HT, KS])
        PSA, o = at("PSA", o, [64, 2, KS])
        PTS, o = at("PTS", o, [P, 2, NPAGE + 1, 64])
        QBD, o = at("QBD", o, [P, 2, 328])
        LFS, o = at("LFS", o, [64, KS])
        KBS, o = at("KBS", o, [P, KS])
        SLS, o = at("SLS", o, [P, 2, 64])
        CQ2, o = at("CQ2", o, [P, NQ])
        ST5, o = at("ST5", o, [64, 2, 8])
        assert o <= B0
        MIX, o = at("MIX", B0, [P, HT, ES + T + EP])
        YEXT, BG, PEXT = MIX[:, :, 0:ES], MIX[:, :, ES:ES + T], MIX[:, :, ES + T:]
        assert (ES + T + EP) * 4 <= 4 * T * 4
        T1, o = at("T1", o, [P, EP + 1])
        T2, o = at("T2", o, [P, EP + 1])
        DH, o = at("DH", o, [P, T], F32R)
        WMR, _ = at("WMR", o, [P, HT, P])
        DL, o = at("DL", o, [P, T], F32R)
        OSA, o = at("OSA", o, [P, HALF])
        OSB, o = at("OSB", o, [NS * HS, HALF])
        CMP, o = at("CMP", o, [P, NS * HS + NS * NQ])
        assert o <= R0 + 26400
        WMH, o = at("WMH", R0 + 29344, [P, HT, P], F32R)
        WML, o = at("WML", o, [P, HT, P], F32R)
        DF = (T1, T2, T1, T2)
        YO, _ = at("YO", A0, [P, 4, D])
        PS = ctx.enter_context(nc.psum_tensor("PS", [P, 8, 512], F32))
        XT = nc.dram_tensor("x_spill", [P, KT, T], F32, kind="Internal").ap()
        LFD = nc.dram_tensor("lf_spill", [NS * NH, NQ], F32, kind="Internal").ap()
        IDN = CST[:, K_ID:K_ID + P]
        ONES_D, ONES_H = CST[:, K_O1024:K_O1024 + P], CST[:, K_O512:K_O512 + P]

        def prompt_cols(tile, h, k, lo, hi, shift=0):
            return tile[:, k, h + lo - shift:h + hi - shift]

        def sample_cols(tile, h, k, shift=0):
            v = tile[:, k, h + TP:h + TP + NS * (h + NQ)].rearrange("p (s e) -> p s e", s=NS)
            return v[:, :, h - shift:h - shift + NQ]

        def history(tile, h, k, s0, n):
            v = tile[:, k, h + TP:h + TP + NS * (h + NQ)].rearrange("p (s e) -> p s e", s=NS)
            return v[:, s0:s0 + n, 0:h]

        def by_seq(ap):
            return ap.rearrange("p (s e) -> p s e", s=NS)

        def row(k, r):
            return PRT[:, k % HT, r + k // HT:r + k // HT + 1]

        s_cst, s_par, s_xin = sem("s_cst"), sem("s_par"), [sem(f"s_xin{i}") for i in range(3)]
        s_sin, s_bf, s_wf, s_ptb, ext_zero = sem("s_sin"), sem("s_bf"), sem("s_wf"), sem("s_ptb"), sem("ext_zero")
        w_loaded = [sem(f"w_loaded{i}") for i in range(4)]
        w_hi, w_lo = sem("w_hi"), sem("w_lo")
        t_done, t_free = sem("t_done"), sem("t_free")
        x_hi, x0_ready, xt_copy = sem("x_hi"), sem("x0_ready"), sem("xt_copy")
        xt_sent = [sem("xt_sent0"), sem("xt_sent1")]
        gu_done, s_ready, gu_free = sem("gu_done"), sem("s_ready"), sem("gu_free")
        hh_ready, h_ready = sem("hh_ready"), sem("h_ready")
        d_done, d_free = sem("d_done"), sem("d_free")
        acmp_ready, sta_sent, acc_step, acc_done, conv_done = (sem("acmp_ready"), sem("sta_sent"), sem("acc_step"),
                                                              sem("acc_done"), sem("conv_done"))
        wf_hi, wf_lo, f_done, f_act, lf_ready, lfo_ready = (sem("wf_hi"), sem("wf_lo"), sem("f_done"), sem("f_act"),
                                                            sem("lf_ready"), sem("lfo_ready"))
        c_ready, c_hi, c_lo, kb_sent, kb_zero, lfd_sent = (sem("c_ready"), sem("c_hi"), sem("c_lo"), sem("kb_sent"),
                                                           sem("kb_zero"), sem("lfd_sent"))
        stg_ready, stg_sent, ab_open = sem("stg_ready"), [sem(f"stg_sent{i}") for i in range(4)], sem("ab_open")
        idr_ready, qk_hi, qk_lo = sem("idr_ready"), sem("qk_hi"), sem("qk_lo")
        vp_ready = [sem("vp_ready0"), sem("vp_ready1")]
        qk_done, nm_ready, exp_done, rc_ready, pn_ready = (sem("qk_done"), sem("nm_ready"), sem("exp_done"),
                                                           sem("rc_ready"), sem("pn_ready"))
        ta_done, tb_done, pta_ready, ptb_ready = sem("ta_done"), sem("tb_done"), sem("pta_ready"), sem("ptb_ready")
        pv_done, att_evac = sem("pv_done"), sem("att_evac")
        lfr_in, lfs_page, lfs_in, sel_in, cs_ready, cq_ready, sel_ready = (
            sem("lfr_in"), sem("lfs_page"), sem("lfs_in"), sem("sel_in"), sem("cs_ready"), sem("cq_ready"), sem("sel_ready"))
        kr_in, vr_in = [sem("kr_in0"), sem("kr_in1")], [sem("vr_in0"), sem("vr_in1")]
        sk_done, kt_ready, kt_new, qbd_zero, qbd_ready, sls_ready = (sem("sk_done"), sem("kt_ready"), sem("kt_new"),
                                                                     sem("qbd_zero"), sem("qbd_ready"), sem("sls_ready"))
        sqk_done, snm, sexp, src_, spn = sem("sqk_done"), sem("snm"), sem("sexp"), sem("src_"), sem("spn")
        spt_done, spt_ready, spv_done, satt = sem("spt_done"), sem("spt_ready"), sem("spv_done"), sem("satt")
        la_sum, la_mean, la_cen, la_sq, la_sum2, la_var, la_sd, la_rs, la_nrm, la_act, la_hi = (
            sem("la_sum"), sem("la_mean"), sem("la_cen"), sem("la_sq"), sem("la_sum2"), sem("la_var"), sem("la_sd"),
            sem("la_rs"), sem("la_nrm"), sem("la_act"), sem("la_hi"))
        m_ready, y_in = sem("m_ready"), [sem(f"y_in{i}") for i in range(KT)]
        ln_part, ln_sum, ln_mean, ln_cen, ln_sq, ln_sum2, ln_var, ln_sd, ln_rs, ln_nrm = (
            sem("ln_part"), sem("ln_sum"), sem("ln_mean"), sem("ln_cen"), sem("ln_sq"), sem("ln_sum2"), sem("ln_var"),
            sem("ln_sd"), sem("ln_rs"), sem("ln_nrm"))
        ln_xf, ln_hi, x_ready, xt_spill = sem("ln_xf"), sem("ln_hi"), sem("x_ready"), sem("xt_spill")
        od_in, od_zero, wm_in, wm_hi, wm_lo, od_t = (sem("od_in"), sem("od_zero"), sem("wm_in"), sem("wm_hi"),
                                                     sem("wm_lo"), sem("od_t"))
        cmp_ready, ot_done, ot_free, os_sent, df_ready, dh_ready, dl_ready, mix_done, mix_evac, tap = (
            sem("cmp_ready"), sem("ot_done"), sem("ot_free"), sem("os_sent"), sem("df_ready"), sem("dh_ready"),
            sem("dl_ready"), sem("mix_done"), sem("mix_evac"), sem("tap"))
        oc_done = sem("oc_done")
        yo_sent, pool_out = [sem("yo_sent0"), sem("yo_sent1"), sem("yo_sent2"), sem("yo_sent3")], sem("pool_out")

        w_ug = t["w_in_even"][0].rearrange("(k p) n -> p k n", p=P)
        w_odd = t["w_in_odd"][0].rearrange("(k p) n -> p k n", p=P)
        w_out = [t[n][0].rearrange("(k p) n -> p k n", p=P) for n in ("w_out_even", "w_out_odd")]
        w_g = [t["w_ffn_gate"][i].rearrange("(k p) n -> p k n", p=P) for i in range(2)]
        w_u = [t["w_ffn_up"][i].rearrange("(k p) n -> p k n", p=P) for i in range(2)]
        w_d = [t["w_ffn_down"][i] for i in range(2)]

        def raw_cols(pos):
            return RAW[:, pos, :].rearrange("p (k m) -> p k m", k=KT)

        def token_pieces(i):
            lo, hi = i * P, min((i + 1) * P, T)
            spans = [(0, META, "meta_tokens"), (META, TP, "x_prompt"), (TP, T, "x_sample")]
            return [(max(lo, a) - lo, min(hi, b) - max(lo, a), n, max(lo, a) - a)
                    for a, b, n in spans if max(lo, a) < min(hi, b)]

        xsrc = {"meta_tokens": t["meta_tokens"], "x_prompt": t["x_prompt"][0],
                "x_sample": t["x_sample"].rearrange("s q d -> (s q) d")}
        xin_count = [16 * sum(len(token_pieces(j)) for j in range(i % 3, i + 1, 3)) for i in range(NTT)]
        tw = [min(P, T - i * P) for i in range(NTT)]
        YPIECES = [[(16, 112), (128, 128), (256, 112)], [(368, 128), (496, 128), (624, 112)],
                   [(736, 128), (864, 128), (992, 48), (1040, 64)]]
        STG_ALL = (6, 6, 4, 4)

        def att_units():
            na = nb = 0
            for a in range(36):
                i = ORDER[(a // 9) % 2][a % 9]
                groups = (i + 4) // 4
                yield a, (a // 9) % 2, a // 18, i, (P if i < 8 else META), min(P * (i + 1), TP), na, nb
                na += 1 + (groups > 2)
                nb += groups > 1

        ATT = list(att_units())
        NA = ATT[-1][6] + 1 + (ATT[-1][3] == 8)
        NB = ATT[-1][7] + (ATT[-1][3] > 3)

        def chunk(c):
            return slice(c * C, (c + 1) * C)

        def ffn_units(f):
            return (ST_FF0, GU_FF0, DN_FF0) if f == 0 else (ST_FF1, GU_FF1, DN_FF1)

        LN_DONE = [[3 + b + 18 + 2 * c + 2 for c in range(NC)] if f is None else
                   [3 + b + 24 * (NG - 1) + 8 * (c + 1) for c in range(NC)]
                   for b, f in ((DN_OUT0, None), (DN_FF0, 0), (DN_OUT1, None), (DN_FF1, 1))]
        POOL_OUT_ALL = 16 * (2 + NS + 3)
        block = ctx.enter_context(nc.Block())

        @block.sync
        def _(sp):
            def load(n, pos, src):
                sp.wait_ge(w_lo, n - 3)
                sp.dma_start(raw_cols(pos) if len(src.shape) == 3 else RAW[:, pos, :], src).then_inc(w_loaded[pos], 16)

            def cols(w, m):
                return w[:, :, bass.ds(m * P, P)]

            sp.dma_start(CST[:], t["consts"][:, 0:K_SEL]).then_inc(s_cst, 16)
            for i in range(NTT):
                if i >= 3:
                    sp.wait_ge(t_done, 2 * (i - 2))
                for r, n, name, first in token_pieces(i):
                    sp.dma_start(XIN[r:r + n, i % 3, :], xsrc[name][first:first + n, :]).then_inc(s_xin[i % 3], 16)
                if i == 2:
                    for n in range(4):
                        sp.dma_start(raw_cols(n), cols(w_ug, (1 - n % 2) * HT + n // 2)).then_inc(w_loaded[n], 16)
            for n in range(4, 8):
                load(n, n % 4, cols(w_ug, (1 - n % 2) * HT + n // 2))
            with sp.Fori(0, 3) as it:
                for n in range(4):
                    load(2 * ST_QKV + 4 * it + n, n, cols(w_ug, 4 * it + n + 2 * HT))
            for n in range(4):
                load(2 * ST_OUT0 + n, (2 * ST_OUT0 + n) % 4, w_out[0][:, :, n * P:(n + 1) * P])
            kv = [t[n][0, 0].rearrange("t h d -> t (h d)") for n in ("k_prompt", "v_prompt")]
            kvs = [t[n].rearrange("s a q h d -> (s a q) (h d)") for n in ("k_sample", "v_sample")]
            for i in range(NTT):
                for j in range(2):
                    u = 2 * i + j
                    sp.wait_ge(t_free, 4 + TU_KV + u + 1)
                    if i < 8:
                        sp.dma_start(kv[j][i * P:(i + 1) * P, :], STG[:, u % 4, :]).then_inc(stg_sent[u % 4], 16)
                    else:
                        sp.dma_start(kv[j][i * P:TP, :], STG[0:META, u % 4, :]).then_inc(stg_sent[u % 4], 16)
                        sp.dma_start(kvs[j], STG[META:META + NS * NQ, u % 4, :]).then_inc(stg_sent[u % 4], 16)
            vd = t["v_prompt"][0, 0].rearrange("t h d -> t (h d)")
            for i in range(4):
                sp.wait_ge(stg_sent[i], 16 * STG_ALL[i])
            with sp.Fori(0, 2) as it:
                sp.wait_ge(pv_done, 1 + 36 * it)
                for j in range(2):
                    c = bass.ds((2 * it + j) * P, P)
                    sp.dma_start(VP[:, j, 0:8, :], vd[0:8 * P].rearrange("(b p) n -> p b n", p=P)[:, :, c]).then_inc(vp_ready[j], 16)
                    sp.dma_start(VP[0:META, j, 8, :], vd[8 * P:TP, c]).then_inc(vp_ready[j], 16)
            sp.wait_ge(s_ptb, 16)
            sp.wait_ge(att_evac, 1 + 72)
            vs = t["v_sample"].rearrange("s a q h d -> (s a) q (h d)")

            def pages(s, j, wait):
                rows = [sp.value_load(PTB[0:1, bass.ds(s * NPAGE + g, 1)], min_val=0, max_val=t["cache_k"].shape[0] - 1)
                        for g in range(NPAGE)]
                if wait:
                    sp.wait_ge(sk_done, 4 * s - 4)
                for g, r in enumerate(rows):
                    sp.dma_start(KR[:, j, g, :], t["cache_k"][bass.ds(r, 1)].rearrange("a e p h d -> (a e p) (h d)")).then_inc(kr_in[j], 16)
                if wait:
                    sp.wait_ge(spv_done, s)
                for g, r in enumerate(rows):
                    sp.dma_start(VR[:, j, g, :], t["cache_v"][bass.ds(r, 1)].rearrange("a e p h d -> (a e p) (h d)")).then_inc(vr_in[j], 16)
                sp.dma_start(VR[0:NQ, j, NPAGE, :], vs[bass.ds(s, 1)].rearrange("s q n -> (s q) n")).then_inc(vr_in[j], 16)

            for j in range(2):
                pages(j, j, False)
            with sp.Fori(0, NS // 2 - 1) as it:
                for j in range(2):
                    pages(2 * it + 2 + j, j, True)

            def residual(layer):
                sp.wait_ge(m_ready, 12 * (layer + 1))
                for k in range(KT):
                    sp.dma_start(Y[:, k, :], XT[:, k, :]).then_inc(y_in[k], 16)

            def ffn_weights(f):
                st = ffn_units(f)[0]

                def group(n, g, par):
                    for j in range(2):
                        load(n + 2 * j, (par + 2 * j) % 4, cols(w_g[f], 2 * g + j))
                        load(n + 2 * j + 1, (par + 2 * j + 1) % 4, cols(w_u[f], 2 * g + j))
                    for j in range(2):
                        load(n + 4 + j, (par + j) % 4, w_d[f][bass.ds((2 * g + j) * P, P), :])

                with sp.Fori(0, NG // 2) as it:
                    group(2 * st + 12 * it, 2 * it, 2 * st)
                    group(2 * st + 12 * it + 6, 2 * it + 1, 2 * st + 6)
                group(2 * st + 6 * (NG - 1), NG - 1, 2 * st + 6 * (NG - 1))

            sp.wait_ge(xt_sent[0], 16 * 5)
            sp.wait_ge(xt_sent[1], 16 * 4)
            residual(0)
            for n in range(4, 8):
                load(2 * ST_OUT0 + n, (2 * ST_OUT0 + n) % 4, w_out[0][:, :, n * P:(n + 1) * P])
            ffn_weights(0)
            for i in range(HT):
                for j, m in enumerate((2 * HT + i, i, HT + i, 3 * HT + i)):
                    load(2 * ST_ODD + 4 * i + j, (2 * ST_ODD + j) % 4, w_odd[:, :, m * P:(m + 1) * P])
            for n in range(4):
                load(2 * ST_OUT1 + n, (2 * ST_OUT1 + n) % 4, w_out[1][:, :, n * P:(n + 1) * P])
            residual(1)
            for n in range(4, 8):
                load(2 * ST_OUT1 + n, (2 * ST_OUT1 + n) % 4, w_out[1][:, :, n * P:(n + 1) * P])
            ffn_weights(1)

        @block.gpsimd
        def _(gp):
            for r, name, n in ((R_DW, "w_dw_a", CW), (R_BDW, "b_dw_a", 1), (R_LAG, "ln_a_g", 1), (R_LAB, "ln_a_b", 1),
                               (R_SC, "w_sconv", SW), (R_PS, "pool_scale", 1)):
                gp.dma_start(PIN[r:r + n, :], t[name][0] if n > 1 else t[name]).then_inc(s_par, 16)
            for r, name in ((R_MG, "ln_mix_g"), (R_MB, "ln_mix_b"), (R_FG, "ln_ffn_g"), (R_FB, "ln_ffn_b")):
                gp.dma_start(PIN[r:r + 4, :], t[name].rearrange("l (a n) -> (l a) n", a=2)).then_inc(s_par, 16)
            sca = t["state_conv_a"].rearrange("s a e n -> (s a e) n")
            for i in range(2):
                gp.dma_start(SIN[0:4 * HA, i, :], sca[4 * HA * i:4 * HA * (i + 1), :]).then_inc(s_sin, 16)
            gp.dma_start(PTB[:], t["page_table"].rearrange("(a s) g -> a (s g)", a=1)).then_inc(s_ptb, 16)
            with nc.allow_non_contiguous_dma(reason="eight biases, one per partition"):
                gp.dma_start(BF[:, 0:1], t["b_forget"].rearrange("a h -> h a")).then_inc(s_bf, 16)
            gp.dma_start(WFR[:], w_ug[:, :, 5 * HALF:5 * HALF + NH]).then_inc(s_wf, 16)
            gp.memset(AEXT[:, :, 0:HA], 0.0).then_inc(ext_zero, 1)
            gp.dma_start(t["conv_a_sample"][:, 0, 0:HA - NQ, :], t["state_conv_a"][:, 0, NQ:HA, :]).then_inc(pool_out, 16)
            gp.dma_start(t["pool_sample"][:, 0, 0:HP - NQ, :], t["state_pool"][:, 0, NQ:HP, :]).then_inc(pool_out, 16)
            for i in range(NTT):
                gp.wait_ge(xt_copy, 2 * (i + 1))
                gp.dma_start(XT[:, :, i * P:i * P + tw[i]], XTT[:, i % 2, :, 0:tw[i]]).then_inc(xt_sent[i % 2], 16)
            gp.wait_ge(s_ptb, 16)
            with gp.Fori(0, NS) as s:
                for g in range(NPAGE):
                    r = gp.value_load(PTB[0:1, bass.ds(s * NPAGE + g, 1)], min_val=0, max_val=t["cache_logf"].shape[0] - 1)
                    gp.dma_start(LFR[:, g, bass.ds(s, 1), :].rearrange("p a h -> p (a h)"),
                                 t["cache_logf"][bass.ds(r, 1)].rearrange("a e p h -> (a e p) h")).then_inc(lfr_in, 16)
            gp.wait_ge(gu_free, 2 + GU_QKV)
            for k in range(HT):
                gp.tensor_copy(ACMP[:, k, :, :], sample_cols(AEXT, HA, k)).then_inc(acmp_ready, 1)
            gp.wait_ge(t_free, 4 + TU_A + 1)
            gp.dma_start(t["conv_a_prompt"][0, 0], STA[:]).then_inc(sta_sent, 16)
            gp.wait_ge(t_free, 4 + TU_A + 2)
            for s in range(NS):
                gp.dma_start(t["conv_a_sample"][s, 0, HA - NQ:HA, :], STB[s * NQ:(s + 1) * NQ, :]).then_inc(sta_sent, 16)
            for k in range(HT):
                gp.wait_ge(acc_done, k + 1)
                gp.tensor_copy(AEXT[:, k, 0:T], CACC[:]).then_inc(conv_done, 1)
            gp.wait_ge(t_free, 4 + TU_LF + 1)
            gp.dma_start(t["logf_prompt"][0, 0, 0:8 * P].rearrange("(b p) h -> p b h", p=P), LFO[:, 0:8, :]).then_inc(pool_out, 16)
            gp.dma_start(t["logf_prompt"][0, 0, 8 * P:TP], LFO[0:META, 8, :]).then_inc(pool_out, 16)
            gp.dma_start(t["logf_sample"].rearrange("s a q h -> (s a q) h"), LFO[META:META + NS * NQ, 8, :]).then_inc(pool_out, 16)
            gp.dma_start(LFD.rearrange("(s h) q -> h s q", s=NS), by_seq(LFZ[:, 2, TP:T])).then_inc(lfd_sent, 16)
            gp.wait_ge(conv_done, HT)
            gp.memset(KS2[64:96, :, :].bitcast(F32), 1.0).then_inc(kb_zero, 1)
            gp.wait_ge(kb_zero, 1)
            gp.memset(QBA[:], -1.0).then_inc(kb_zero, 1)
            gp.wait_ge(kb_zero, 2)
            gp.wait_ge(c_lo, 1)
            for j in range(2):
                gp.dma_start(KS2[64:72, j, :], LCH[:]).then_inc(kb_sent, 16)
                gp.dma_start(KS2[72:80, j, :], LCL[:]).then_inc(kb_sent, 16)
            gp.dma_start(QBA[16:24, :], LCH[:].bitcast(F32)).then_inc(kb_sent, 16)
            gp.dma_start(QBA[24:32, :], LCL[:].bitcast(F32)).then_inc(kb_sent, 16)
            gp.wait_ge(kb_sent, 96)
            gp.wait_ge(lfd_sent, 16)
            gp.wait_ge(pool_out, 16 * 5)
            for i in range(4):
                gp.wait_ge(stg_sent[i], 16 * STG_ALL[i])
            gp.sem_inc(ab_open, 1)

            with gp.Fori(0, 2) as it:
                for a, h2, j, i, m, n, _, _ in ATT:
                    gp.wait_ge(rc_ready, 36 * it + a + 1)
                    gp.nop(nofuse=True)
                    gp.tensor_scalar(PB[0:m, a % 3, 0:n], PB[0:m, a % 3, 0:n], ST4[0:m, 2, a:a + 1], 1.0,
                                     ALU.mult, ALU.mult).then_inc(pn_ready, 1)
            gp.wait_ge(att_evac, 1 + 72)
            gp.dma_start(SELC[:].rearrange("p s h q -> p (s h q)"), t["consts"][:, K_SEL:K_ALL]).then_inc(sel_in, 16)
            gp.dma_start(LFS[:, PAST:KS], LFD).then_inc(lfs_in, 16)
            gp.memset(QBD[:], 0.0).then_inc(qbd_zero, 1)
            gp.wait_ge(qbd_zero, 1)
            gp.memset(KBS[64:128, :], 1.0).then_inc(qbd_zero, 1)
            gp.wait_ge(qbd_zero, 2)
            gp.wait_ge(sel_ready, 1)

            def new_keys(s, j):
                gp.tensor_copy(SLS[:, j, :], SELC[:, bass.ds(s, 1), :, :].rearrange("p a h q -> p (a h q)")).then_inc(sls_ready, 1)
                gp.tensor_copy(KTS[:, j, :, PAST:KS], QKV[:, HT:2 * HT, bass.ds(TP + s * NQ, NQ)]).then_inc(kt_new, 1)

            for j in range(2):
                new_keys(j, j)
            with gp.Fori(0, NS // 2 - 1) as it:
                for j in range(2):
                    gp.wait_ge(sqk_done, 2 * it + j + 1)
                    new_keys(2 * it + 2 + j, j)

            gp.wait_ge(satt, 1 + NS)
            gp.wait_ge(conv_done, HT)
            for c in range(NC):
                if c:
                    gp.wait_ge(la_var, c)
                gp.tensor_tensor(YSA[:], AEXT[:, 0:2, chunk(c)], AEXT[:, 2:4, chunk(c)], ALU.add).then_inc(la_sum, 1)
                gp.wait_ge(la_mean, c + 1)
                gp.wait_ge(la_sq, 2 * (c + 1))
                gp.tensor_tensor(YSA[:], SQA[:, 0:2, :], SQA[:, 2:4, :], ALU.add).then_inc(la_sum2, 1)

            parts = [0]

            def partial(ins):
                parts[0] += 1
                ins.then_inc(ln_part, 1)
                gp.wait_ge(ln_part, parts[0])

            def mean_sums(ln, c):
                cc, k = chunk(c), 3 * ln + c
                gp.wait_ge(d_free, LN_DONE[ln][c])
                if k:
                    gp.wait_ge(ln_mean, k)
                partial(gp.tensor_tensor(YSM[:], Y[:, 0:2, cc], Y[:, 2:4, cc], ALU.add))
                partial(gp.tensor_tensor(YSM[:], YSM[:], Y[:, 4:6, cc], ALU.add))
                gp.tensor_tensor(YSM[:], YSM[:], Y[:, 6:8, cc], ALU.add).then_inc(ln_sum, 1)

            def square_sums(ln, c):
                k = 3 * ln + c
                if k:
                    gp.wait_ge(ln_var, k)
                gp.wait_ge(ln_sq, 4 * k + 2)
                partial(gp.tensor_tensor(YSV[:], SQ[:, 0:2, :], SQ[:, 2:4, :], ALU.add))
                gp.wait_ge(ln_sq, 4 * k + 4)
                partial(gp.tensor_tensor(YSV[:], YSV[:], SQ[:, 4:6, :], ALU.add))
                gp.tensor_tensor(YSV[:], YSV[:], SQ[:, 6:8, :], ALU.add).then_inc(ln_sum2, 1)

            def spill(c):
                gp.wait_ge(ln_xf, 4 * (3 + c) + 4)
                gp.dma_start(XT[:, :, chunk(c)], Y[:, :, chunk(c)]).then_inc(xt_spill, 16)

            def layer_norm(ln, after=lambda c: None):
                mean_sums(ln, 0)
                mean_sums(ln, 1)
                square_sums(ln, 0)
                mean_sums(ln, 2)
                after(0)
                square_sums(ln, 1)
                after(1)
                square_sums(ln, 2)
                after(2)

            layer_norm(0)
            layer_norm(1, spill)
            gp.wait_ge(xt_spill, 48)
            gp.wait_ge(x_ready, 24)
            gp.dma_start(OSB[:], t["state_sconv"].rearrange("s a e n -> (s a e) n")).then_inc(od_in, 16)
            gp.dma_start(OSA[0:NS * HP, :], t["state_pool"].rearrange("s a e n -> (s a e) n")).then_inc(od_in, 16)
            gp.dma_start(WMR[:], t["w_pool_mix"][0].rearrange("g c d -> c g d")).then_inc(wm_in, 16)
            gp.memset(YEXT[:, :, 0:HS], 0.0).then_inc(od_zero, 1)
            gp.memset(PEXT[:, :, 0:HP], 0.0).then_inc(od_zero, 1)
            gp.wait_ge(ot_free, 1 + HT)
            gp.dma_start(t["sconv_prompt"][0, 0], OSA[64:64 + HS, :]).then_inc(os_sent, 16)
            gp.dma_start(t["pool_prompt"][0, 0], OSA[96:96 + HP, :]).then_inc(os_sent, 16)
            gp.dma_start(t["sconv_sample"].rearrange("s a e n -> (s a e) n"), OSB[:]).then_inc(os_sent, 16)
            for s in range(NS):
                gp.dma_start(t["pool_sample"][s, 0, HP - NQ:HP, :], OSA[s * NQ:(s + 1) * NQ, :]).then_inc(os_sent, 16)
            gp.wait_ge(os_sent, 16 * (3 + NS))
            layer_norm(2)

            def store_y(c):
                n = sum(len(YPIECES[x]) for x in range(c))
                for a, w in YPIECES[c]:
                    gp.wait_ge(t_free, 4 + TU_Y + 2 * (n + 1))
                    dst = t["y_prompt"][0, a - META:a - META + w, :] if a < TP else t["y_sample"].rearrange("s q d -> (s q) d")
                    gp.dma_start(dst, YO[0:w, n % 4, :]).then_inc(yo_sent[n % 4], 16)
                    n += 1

            layer_norm(3, store_y)
            for i in range(4):
                gp.wait_ge(yo_sent[i], 16 * len(range(i, sum(map(len, YPIECES)), 4)))
            gp.wait_ge(sta_sent, 16 * (1 + NS))

        @block.tensor
        def _(pe):
            pe.sem_inc(pv_done, 1)
            pe.sem_inc(spv_done, 1)

            def mm3(out, wh, wl, xh, xl, first, last):
                pe.matmul(out, wh, xh, start=first, stop=False)
                pe.matmul(out, wh, xl, start=False, stop=False)
                return pe.matmul(out, wl, xh, start=False, stop=last)

            def transposes(u, bank, pieces):
                pe.wait_ge(t_free, u + 1)
                for out, src, idn in pieces:
                    m = pe.transpose(out, src, idn)
                m.then_inc(t_done, 1)

            def gu_stage(stage, pos, unit, par, before=None):
                pe.wait_ge(w_lo, 2 * stage + 2)
                for c in range(NC):
                    if before:
                        before(c)
                    pe.wait_ge(gu_free, unit + c + 1)
                    for w in range(2):
                        out = PS[:, 2 * ((par + c) % 2) + w, 0:C]
                        for k in range(KT):
                            ks = slice(k * P, (k + 1) * P)
                            m = mm3(out, WHI[:, pos + w, ks], WLO[:, pos + w, ks], AH[:, k, chunk(c)], AL[:, k, chunk(c)],
                                    k == 0, k == KT - 1)
                    m.then_inc(gu_done, 1)

            def norm_product(ones, ys, s_in, s_res, k):
                pe.wait_ge(s_in, k + 1)
                pe.matmul(PS[:, 7, 0:C], ones, ys[:, 0, :], start=True, stop=False)
                pe.matmul(PS[:, 7, 0:C], ones, ys[:, 1, :], start=False, stop=True).then_inc(s_res, 1)

            def mean(ln, c):
                k = 3 * ln + c
                if k:
                    pe.wait_ge(ln_sd, k)
                norm_product(ONES_D, YSM, ln_sum, ln_mean, k)

            def variance(ln, c):
                norm_product(ONES_D, YSV, ln_sum2, ln_var, 3 * ln + c)

            def gu_unit(pos, unit, par, c):
                pe.wait_ge(gu_free, unit + 1)
                for w in range(2):
                    for k in range(KT):
                        ks = slice(k * P, (k + 1) * P)
                        m = mm3(PS[:, 2 * par + w, 0:C], WHI[:, pos + w, ks], WLO[:, pos + w, ks], AH[:, k, chunk(c)], AL[:, k, chunk(c)],
                                k == 0, k == KT - 1)
                m.then_inc(gu_done, 1)

            def gu_stage(stage, pos, unit, par, before=None):
                pe.wait_ge(w_lo, 2 * stage + 2)
                for c in range(NC):
                    if before:
                        before(c)
                    gu_unit(pos, unit + c, (par + c) % 2, c)

            def head(ln, st, unit):
                variance(ln, 0)
                mean(ln, 1)
                for c in range(NC):
                    pe.wait_ge(x_ready, 12 * ln + 4 * (c + 1))
                    for j in range(2):
                        pe.wait_ge(w_lo, 2 * (st + j) + 2)
                        gu_unit(2 * (st + j) % 4, unit + 2 * c + j, j, c)
                        if j == 0 and c < 2:
                            variance(ln, c + 1)
                        if j == 1 and c == 0:
                            mean(ln, 2)

            pe.wait_ge(s_cst, 16)
            for i in range(NTT):
                pe.wait_ge(s_xin[i % 3], xin_count[i])
                for h in range(2):
                    u = 2 * i + h
                    transposes(u, 4 + u % 4, [(PS[:, 4 + u % 4, P * j:P * j + tw[i]], XIN[0:tw[i], i % 3, (4 * h + j) * P:(4 * h + j + 1) * P],
                                               IDN[0:tw[i], 0:tw[i]]) for j in range(4)])
            pe.wait_ge(s_par, 160)
            u = TU_PAR
            transposes(u, 4 + u % 4, [(PS[:, 4 + u % 4, R_ALL * j:R_ALL * (j + 1)], PIN[:, j * P:(j + 1) * P], IDN[0:R_ALL, 0:R_ALL])
                                      for j in range(HT)])
            pe.wait_ge(s_sin, 32)
            for i in range(2):
                u, n = TU_SA + i, 4 * HA
                transposes(u, 4 + u % 4, [(PS[:, 4 + u % 4, n * j:n * (j + 1)], SIN[0:n, i, j * P:(j + 1) * P], IDN[0:n, 0:n])
                                          for j in range(HT)])
            with pe.Fori(0, 2) as it:
                for j in range(2):
                    def x_split(c):
                        pe.wait_ge(t_free, 4 + 6 * (c + 1))
                    gu_stage(2 * it + j, 2 * j, 6 * it + 3 * j, 3 * j, x_split)
            pe.wait_ge(gu_free, 2 + GU_QKV)
            u = TU_A
            transposes(u, 4 + u % 4, [(PS[0:HA, 4 + u % 4, k * P:(k + 1) * P], AEXT[:, k, TP:HA + TP], IDN) for k in range(HT)])
            pe.wait_ge(acmp_ready, HT)
            u = TU_A + 1
            transposes(u, 4 + u % 4, [(PS[0:NS * NQ, 4 + u % 4, k * P:(k + 1) * P], ACMP[:, k, :, :].rearrange("p s e -> p (s e)"), IDN)
                                      for k in range(HT)])
            with pe.Fori(0, 3) as it:
                for j in range(2):
                    gu_stage(ST_QKV + 2 * it + j, 2 * j, GU_QKV + 6 * it + 3 * j, 3 * j)
            pe.wait_ge(wf_lo, 1)
            pe.wait_ge(t_free, 4 + TU_KV)
            for c in range(NC):
                for k in range(KT):
                    m = mm3(PS[0:NH, 4 + c, 0:C], WFH[:, k, :], WFL[:, k, :], AH[:, k, chunk(c)], AL[:, k, chunk(c)], k == 0, k == KT - 1)
                m.then_inc(f_done, 1)
            pe.wait_ge(gu_free, 2 + GU_FF0)
            pe.wait_ge(f_act, NC)
            for i in range(NTT):
                for j in range(2):
                    u = TU_KV + 2 * i + j
                    transposes(u, 4 + u % 4, [(PS[0:tw[i], 4 + u % 4, k * P:(k + 1) * P], QKV[:, HT * (1 + j) + k, i * P:i * P + tw[i]], IDN)
                                              for k in range(HT)])
            pe.wait_ge(lf_ready, 1)
            u = TU_LF
            transposes(u, 4 + u % 4, [(PS[0:tw[i], 4 + u % 4, NH * i:NH * (i + 1)], LFZ[:, 2, i * P:i * P + tw[i]], IDN[0:NH, 0:NH])
                                      for i in range(NTT)])

            pe.wait_ge(t_free, 4 + TU_LF + 1)
            pe.wait_ge(idr_ready, 2)

            def scores(it, a, h2, j, i, m, n, na, nb):
                if a % 9 == 0:
                    pe.wait_ge(qk_hi, 16 * it + 4 * (a // 9) + 4)
                    pe.wait_ge(qk_lo, 12 * it + 3 * (a // 9) + 3)
                pe.wait_ge(exp_done, 36 * it + a + 1)
                if i == 8:
                    pe.nop(nofuse=True)
                base, ms = (0, 3)[a % 2], slice(i * P, i * P + m)
                for b in range((n + 511) // 512):
                    lo, hi = 512 * b, min(n, 512 * (b + 1))
                    diag = i * P >= lo and i * P < hi
                    out = PS[0:m, base + b, 0:hi - lo]
                    pe.matmul(out, QS1[:, h2, ms], KS1[:, h2, lo:hi], start=True, stop=False)
                    if diag:
                        pe.matmul(PS[0:m, base + b, i * P - lo:i * P - lo + m], IDR[:, 0:m], MKR[:, 0:m], start=False, stop=False,
                                  skip_group_check=True)
                    mm = pe.matmul(out, QS2[:, h2, ms], KS2[:, h2, lo:hi], start=False, stop=True)
                mm.then_inc(qk_done, 1)

            def turn(it, a, h2, j, i, m, n, na, nb):
                pe.wait_ge(pn_ready, 36 * it + a + 1)
                for g in range((i + 4) // 4):
                    if g == 1:
                        pe.wait_ge(ptb_ready, NB * it + nb + 1)
                    else:
                        pe.wait_ge(pta_ready, NA * it + na + g // 2 + 1)
                    if i == 8:
                        pe.nop(nofuse=True)
                    for jt in range(4 * g, min(4 * g + 4, i + 1)):
                        kw = min(P, TP - jt * P)
                        mm = pe.transpose(PS[0:kw, 5 + g % 2, (jt - 4 * g) * P:(jt - 4 * g) * P + m], PB[0:m, a % 3, jt * P:jt * P + kw],
                                          IDN[0:m, 0:m])
                    mm.then_inc(tb_done if g == 1 else ta_done, 1)

            def values(it, a, h2, j, i, m, n, na, nb):
                if a % 18 == 0:
                    pe.wait_ge(vp_ready[j], 32 * it + 32)
                pe.wait_ge(pta_ready, NA * it + na + (2 if i == 8 else 1) + 1)
                if i > 3:
                    pe.wait_ge(ptb_ready, NB * it + nb + 2)
                pe.wait_ge(att_evac, 36 * it + a + 1)
                for jt in range(i + 1):
                    kw = min(P, TP - jt * P)
                    mm = pe.matmul(PS[0:HD, 7, 0:m], VP[0:kw, j, jt, HD * h2:HD * (h2 + 1)], PT[0:kw, a % 2, jt, 0:m],
                                   start=(jt == 0), stop=(jt == i))
                mm.then_inc(pv_done, 1)

            with pe.Fori(0, 2) as it:
                for n in range(36 + 3):
                    if n < 36:
                        scores(it, *ATT[n])
                    if 2 <= n < 38:
                        turn(it, *ATT[n - 2])
                    if n >= 3:
                        values(it, *ATT[n - 3])

            pe.wait_ge(att_evac, 1 + 72)
            pe.wait_ge(lfr_in, 16 * NS * NPAGE)
            u = TU_LFS
            transposes(u, 6, [(PS[0:64, 6, g * P:(g + 1) * P], LFR[:, g, :, :].rearrange("p s h -> p (s h)"), IDN) for g in range(NPAGE)])
            pe.wait_ge(t_free, 4 + TU_LFS + 1)
            pe.wait_ge(qbd_zero, 2)

            def turn_keys(s, j, loads):
                pe.wait_ge(kr_in[j], 64 * loads)
                for c in range(HT):
                    pe.wait_ge(kt_ready, 4 * s + c + 1)
                    for g in range(NPAGE):
                        mm = pe.transpose(PS[:, c, g * P:(g + 1) * P], KR[:, j, g, c * P:(c + 1) * P], IDN)
                    mm.then_inc(sk_done, 1)

            def sample_scores(s, j):
                pe.wait_ge(kt_ready, 4 * s + 8)
                pe.wait_ge(kt_new, s + 1)
                pe.wait_ge(qbd_ready, 2 * s + 2)
                pe.wait_ge(sls_ready, s + 1)
                pe.wait_ge(sexp, s + 1)
                for b, lo, hi in ((4, 0, PAST), (5, PAST, KS)):
                    out = PS[0:64, b, 0:hi - lo]
                    for c in range(HT):
                        pe.matmul(out, QBD[:, j, 64 * c:64 * c + 64], KTS[:, j, c, lo:hi], start=(c == 0), stop=False)
                    mm = pe.matmul(out, SLS[:, j, :], KBS[:, lo:hi], start=False, stop=(b == 4))
                mm = pe.matmul(PS[0:64, 5, 0:NQ], IDN[0:64, 0:64], CST[0:64, K_MS:K_MS + NQ], start=False, stop=True)
                mm.then_inc(sqk_done, 1)

            def sample_values(s, j, loads):
                pe.wait_ge(spn, s + 1)
                pe.wait_ge(spt_ready, s + 1)
                pe.nop(nofuse=True)
                for g in range(NPAGE + 1):
                    kw = P if g < NPAGE else NQ
                    mm = pe.transpose(PS[0:kw, 6, 64 * g:64 * g + 64], PSA[:, j, g * P:g * P + kw], IDN[0:64, 0:64])
                mm.then_inc(spt_done, 1)
                pe.wait_ge(spt_ready, s + 2)
                pe.wait_ge(vr_in[j], 80 * loads)
                pe.wait_ge(satt, s + 1)
                for c in range(HT):
                    for g in range(NPAGE + 1):
                        kw = P if g < NPAGE else NQ
                        mm = pe.matmul(PS[:, 7, 16 * c:16 * c + 16], VR[0:kw, j, g, c * P:(c + 1) * P], PTS[0:kw, j, g, 16 * c:16 * c + 16],
                                       start=(g == 0), stop=(g == NPAGE))
                mm.then_inc(spv_done, 1)

            turn_keys(0, 0, 1)
            sample_scores(0, 0)
            def sequence(s, j, it):
                turn_keys(s + 1, 1 - j, it + 1 + j)
                sample_values(s, j, it + 1)
                sample_scores(s + 1, 1 - j)

            with pe.Fori(0, NS // 2 - 1) as it:
                for j in range(2):
                    sequence(2 * it + j, j, it)
            sequence(NS - 2, 0, NS // 2 - 1)
            sample_values(NS - 1, 1, NS // 2)

            pe.wait_ge(satt, 1 + NS)
            for c in range(NC):
                if c:
                    pe.wait_ge(la_sd, c)
                norm_product(ONES_H, YSA, la_sum, la_mean, c)
                norm_product(ONES_H, YSA, la_sum2, la_var, c)

            def out_product(layer, st, dn):
                for q in range(4):
                    pos = 2 * (st + q) % 4
                    pe.wait_ge(w_lo, 2 * (st + q) + 2)
                    for c in range(NC):
                        pe.wait_ge(m_ready, 12 * layer + 4 * (c + 1))
                        if q == 3 and c == 2:
                            mean(2 * layer, 0)
                        for w in range(2):
                            n = 6 * q + 2 * c + w
                            pe.wait_ge(d_free, dn + n + 1)
                            for k in range(KT):
                                ks = slice(k * P, (k + 1) * P)
                                m = mm3(PS[:, 4 + n % 3, 0:C], WHI[:, pos + w, ks], WLO[:, pos + w, ks], AH[:, k, chunk(c)],
                                        AL[:, k, chunk(c)], k == 0, k == KT - 1)
                            m.then_inc(d_done, 1)

            def ffn(f):
                st, gu, dn = ffn_units(f)

                def h_need(g, c):
                    return 2 * c + 2 if isinstance(g, int) and g == 0 else 6 * g + 3 + c + 1

                def down(g, par, last=False):
                    pos = 2 * (st + 3 * par + 2) % 4
                    pe.wait_ge(w_lo, 2 * (st + 3 * g) + 6)
                    for c in range(NC):
                        if last and c == 2:
                            mean(2 * f + 1, 0)
                        pe.wait_ge(h_ready, 66 * f + h_need(g, c))
                        for o in range(KT):
                            n = 8 * c + o
                            pe.wait_ge(d_free, dn + 24 * g + n + 1)
                            for w in range(2):
                                os = slice(o * P, (o + 1) * P)
                                m = mm3(PS[:, 4 + n % 3, 0:C], WHI[:, pos + w, os], WLO[:, pos + w, os], HH[:, w, chunk(c)], HL[:, w, chunk(c)],
                                        w == 0, w == 1)
                            m.then_inc(d_done, 1)

                def group(g, par, last=False):
                    for j in range(2):
                        gu_stage(st + 3 * g + j, 2 * (st + 3 * par + j) % 4, gu + 6 * g + 3 * j, 3 * j)
                    down(g, par, last)

                head(2 * f, st, gu)
                down(0, 0)
                with pe.Fori(0, NG // 2 - 1) as it:
                    group(2 * it + 1, 1)
                    group(2 * it + 2, 0)
                group(NG - 2, 1)
                group(NG - 1, 0, last=True)

            out_product(0, ST_OUT0, DN_OUT0)
            ffn(0)
            def mix(i):
                pe.wait_ge(gu_free, 2 + GU_ODD + 6 * (i + 1))
                pe.wait_ge(cmp_ready, i + 1)
                pe.wait_ge(ot_free, i + 1)
                pe.transpose(PS[0:NS * NQ, 7, 0:P], CMP[:, NS * HS:], IDN)
                pe.transpose(PS[0:HS, 7, P:2 * P], prompt_cols(YEXT, HS, i, TP - HS, TP), IDN)
                pe.transpose(PS[0:HP, 7, 2 * P:3 * P], prompt_cols(PEXT, HP, i, TP - HP, TP), IDN)
                pe.transpose(PS[0:NS * HS, 7, 3 * P:4 * P], CMP[:, 0:NS * HS], IDN).then_inc(ot_done, 1)
                pe.wait_ge(dl_ready, i + 1)
                for c in range(NC):
                    pe.wait_ge(mix_evac, 3 * i + c + 1)
                    mm3(PS[:, 4 + c, 0:C], WMH[:, i, :], WML[:, i, :], DH[:, chunk(c)], DL[:, chunk(c)], True, True).then_inc(mix_done, 1)

            for i in range(HT):
                if i:
                    gu_stage(ST_ODD + 2 * i, 2 * ST_ODD % 4, GU_ODD + 6 * i, 0)
                else:
                    head(1, ST_ODD, GU_ODD)
                    pe.wait_ge(ln_sd, 6)
                    pe.wait_ge(d_free, 3 + DN_OUT1)
                    pe.wait_ge(od_in, 32)
                    transposes(TU_ST, 7, [(PS[:, 7, NS * HS * k:NS * HS * (k + 1)], OSB[:, k * P:(k + 1) * P], IDN[0:NS * HS, 0:NS * HS])
                                          for k in range(HT)])
                    n = NS * HP
                    transposes(TU_ST + 1, 4, [(PS[:, 4, n * k:n * (k + 1)], OSA[0:n, k * P:(k + 1) * P], IDN[0:n, 0:n])
                                              for k in range(HT)])
                if i:
                    gu_stage(ST_ODD + 2 * i + 1, (2 * ST_ODD + 2) % 4, GU_ODD + 6 * i + 3, 1)
                if i == 0:
                    pe.wait_ge(wm_lo, 1)
                    pe.wait_ge(t_free, 4 + TU_ST + 2)
                if i:
                    mix(i - 1)
            mix(HT - 1)
            pe.wait_ge(mix_evac, 3 + 3 * HT)
            out_product(1, ST_OUT1, DN_OUT1)
            ffn(1)
            pe.wait_ge(gu_free, 2 + GU_FF1 + 6 * NG)
            u = TU_Y
            variance(3, 0)
            mean(3, 1)
            for c in range(NC):
                pe.wait_ge(ln_xf, 4 * (9 + c) + 4)
                for a, w in YPIECES[c]:
                    for h in range(2):
                        transposes(u, (u - TU_Y) % 4, [(PS[0:w, (u - TU_Y) % 4, k * P:(k + 1) * P], Y[:, 4 * h + k, a:a + w], IDN)
                                                       for k in range(4)])
                        u += 1
                if c < 2:
                    variance(3, c + 1)
                if c < 1:
                    mean(3, 2)

        @block.scalar
        def _(act):
            act.sem_inc(exp_done, 2)
            act.sem_inc(ptb_ready, 1)
            act.sem_inc(att_evac, 1)
            act.sem_inc(kt_ready, 4)
            act.sem_inc(sexp, 1)
            act.sem_inc(spt_ready, 1)
            act.sem_inc(satt, 1)
            act.sem_inc(mix_evac, 3)

            def split(stage, pos, it2=None):
                for j in range(2):
                    n = 2 * stage + j
                    act.wait_ge(w_loaded[pos + j], 16 * it2 if it2 is not None else 16 * (n // 4 + 1))
                    act.copy(WHI[:, pos + j, :], RAW[:, pos + j, :]).then_inc(w_hi, 1)

            def loads(stage_base, it):
                return stage_base // 2 + it + 1

            def x_tile(i):
                for h in range(2):
                    u = 2 * i + h
                    act.wait_ge(t_done, u + 1)
                    src = PS[:, 4 + u % 4, :].rearrange("p (k n) -> p k n", k=4)[:, :, 0:tw[i]]
                    act.copy(AH[:, 4 * h:4 * h + 4, i * P:i * P + tw[i]], src).then_inc(x_hi, 1)
                    if i >= 2:
                        act.wait_ge(xt_sent[i % 2], 16 * (i // 2))
                    act.copy(XTT[:, i % 2, 4 * h:4 * h + 4, 0:tw[i]], src).then_inc(xt_copy, 1)

            for i in range(3):
                x_tile(i)
            split(0, 0)
            for i in range(3, NTT):
                x_tile(i)

            def gated(unit, par, func, s_tile, bank0_to=None):
                act.wait_ge(gu_done, unit + 1)
                act.activation(s_tile[:, par, :] if bank0_to is None else bank0_to, PS[:, 2 * par, 0:C], func).then_inc(s_ready, 1)

            with act.Fori(0, 2) as it:
                for j in range(2):
                    split(2 * it + j + 1, 2 * (1 - j), loads(0, it) if j == 0 else loads(2, it))
                    for c in range(NC):
                        gated(6 * it + 3 * j + c, (3 * j + c) % 2, ACT.Sigmoid, S)
            act.wait_ge(s_wf, 16)
            act.copy(WFH[:], WFR[:]).then_inc(wf_hi, 1)
            act.wait_ge(xt_sent[0], 16 * 5)
            act.wait_ge(xt_sent[1], 16 * 4)
            act.wait_ge(t_free, 4 + TU_A)
            for it in range(3):
                for j in range(2):
                    st = ST_QKV + 2 * it + j
                    split(st + 1, 2 * (1 - j))
                    for c in range(NC):
                        gated(GU_QKV + 6 * it + 3 * j + c, (3 * j + c) % 2, ACT.Copy, S, QKV[:, 4 * it + 2 * j, chunk(c)])
            act.wait_ge(f_done, NC)
            act.wait_ge(s_bf, 16)
            for c in range(NC):
                act.activation(LFZ[:, 0, chunk(c)], PS[0:NH, 4 + c, 0:C], ACT.Identity, bias=BF[:, 0:1]).then_inc(f_act, 1)
            act.wait_ge(f_act, NC)
            act.activation(LFZ[:, 1, :], LFZ[:, 0, :], ACT.Abs).then_inc(f_act, 1)
            act.wait_ge(f_act, NC + 1)
            act.activation(LFZ[:, 1, :], LFZ[:, 1, :], ACT.Exp, scale=-1.0).then_inc(f_act, 1)
            act.wait_ge(f_act, NC + 2)
            act.activation(LFZ[:, 1, :], LFZ[:, 1, :], ACT.Ln, bias=1.0).then_inc(f_act, 1)
            act.wait_ge(c_ready, 1)
            act.copy(LCH[:], LFC[:]).then_inc(c_hi, 1)

            act.wait_ge(ab_open, 1)
            act.copy(IDR[:], IDN).then_inc(idr_ready, 1)
            act.copy(MKR[:], CST[:, K_MASK:K_MASK + P]).then_inc(idr_ready, 1)

            def expo(it, a, h2, j, i, m, n, na, nb):
                base = (0, 3)[a % 2]
                act.wait_ge(nm_ready, 36 * it + a + 1)
                src = PS[0:m, base:base + (n + 511) // 512, :].rearrange("p b n -> p (b n)")[:, 0:n]
                act.activation(PB[0:m, a % 3, 0:n], src, ACT.Exp, bias=ST4[0:m, 0, a:a + 1],
                               accum_out=ST4[0:m, 1, a:a + 1]).then_inc(exp_done, 1)

            def turned(it, a, h2, j, i, m, n, na, nb):
                if i > 3:
                    act.wait_ge(tb_done, NB * it + nb + 1)
                    w = min(i + 1, 8) - 4
                    act.copy(PT[:, a % 2, 4:4 + w, 0:m], PS[:, 6, :].rearrange("p (k n) -> p k n", k=4)[:, 0:w, 0:m]).then_inc(ptb_ready, 1)

            def result(it, a, h2, j, i, m, n, na, nb):
                act.wait_ge(pv_done, 36 * it + a + 2)
                act.nop(nofuse=True)
                act.activation(QKV[HD * h2:HD * (h2 + 1), bass.ds(2 * it + j, 1), i * P:i * P + m].rearrange("p a n -> p (a n)"),
                               PS[0:HD, 7, 0:m], ACT.Copy).then_inc(att_evac, 1)

            def head_high(it, x, part):
                h2 = x % 2
                if x >= 2 and part == 0:
                    act.wait_ge(qk_done, 36 * it + 9 * (x - 1))
                    act.nop(nofuse=True)
                own, other = slice(HD * h2, HD * (h2 + 1)), slice(HD * (1 - h2), HD * (2 - h2))
                tile, out, scale = ((HT, KS1[own, h2, :], 1.0), (0, QS1[own, h2, :], HD ** -0.5), (HT, KS1[other, h2, :], 1.0),
                                    (0, QS2[0:HD, h2, :], HD ** -0.5))[part]
                src = QKV[own, bass.ds(2 * it + x // 2 + tile, 1), 0:TP].rearrange("p a n -> p (a n)")
                act.activation(out, src, ACT.Copy, scale=scale).then_inc(qk_hi, 1)

            with act.Fori(0, 2) as it:
                act.wait_ge(pv_done, 1 + 36 * it)
                act.nop(nofuse=True)
                for part in range(4):
                    head_high(it, 0, part)
                for n in range(36 + 3):
                    if n < 36:
                        expo(it, *ATT[n])
                    if n < 27 and n % 9 in (2, 3, 4, 5):
                        head_high(it, n // 9 + 1, n % 9 - 2)
                    if 2 <= n < 38:
                        turned(it, *ATT[n - 2])
                    if n >= 3:
                        result(it, *ATT[n - 3])

            act.wait_ge(cs_ready, 1)
            act.copy(CQ2[64:128, :], KBS[0:64, PAST:KS]).then_inc(cq_ready, 1)
            act.wait_ge(qbd_zero, 1)

            def queries(s, j):
                act.nop(nofuse=True)
                for h2 in range(2):
                    dst = QBD[HD * h2:HD * (h2 + 1), j, 8 * h2:8 * h2 + 320].rearrange("p (c x) -> p c x", x=80)[:, :, 0:NQ]
                    act.mul(dst, QKV[HD * h2:HD * (h2 + 1), 0:HT, bass.ds(TP + s * NQ, NQ)], HD ** -0.5).then_inc(qbd_ready, 1)

            def keys(s, j, cs):
                for c in cs:
                    act.wait_ge(sk_done, 4 * s + c + 1)
                    act.copy(KTS[:, j, c, 0:PAST], PS[:, c, :]).then_inc(kt_ready, 1)

            def sample_exp(s, j):
                act.wait_ge(snm, s + 1)
                act.activation(PSA[:, j, :], PS[0:64, 4:6, :].rearrange("p b n -> p (b n)")[:, 0:KS], ACT.Exp,
                               bias=ST5[:, j, 0:1], accum_out=ST5[:, j, 1:2]).then_inc(sexp, 1)

            def sample_result(s, j):
                act.wait_ge(spt_done, s + 1)
                act.copy(PTS[:, j, 0:NPAGE, :], PS[:, 6, 0:256].rearrange("p (g n) -> p g n", g=NPAGE))
                act.copy(PTS[0:NQ, j, NPAGE, :], PS[0:NQ, 6, 256:320]).then_inc(spt_ready, 1)
                act.wait_ge(spv_done, s + 2)
                act.nop(nofuse=True)
                for h2 in range(2):
                    src = PS[HD * h2:HD * (h2 + 1), 7, 0:64].rearrange("p (c x) -> p c x", x=16)[:, :, 8 * h2:8 * h2 + NQ]
                    mm = act.activation(QKV[HD * h2:HD * (h2 + 1), 0:HT, bass.ds(TP + s * NQ, NQ)], src, ACT.Copy)
                mm.then_inc(satt, 1)

            def sequence(s, j):
                queries(s + 1, 1 - j)
                keys(s + 1, 1 - j, (0, 1))
                sample_exp(s, j)
                keys(s + 1, 1 - j, (2, 3))
                sample_result(s, j)

            queries(0, 0)
            keys(0, 0, range(HT))
            with act.Fori(0, NS // 2 - 1) as it:
                for j in range(2):
                    sequence(2 * it + j, j)
            sequence(NS - 2, 0)
            sample_exp(NS - 1, 1)
            sample_result(NS - 1, 1)

            for c in range(NC):
                if c:
                    act.wait_ge(m_ready, 4 * c)
                for q in range(2):
                    act.wait_ge(la_cen, 2 * c + q + 1)
                    act.activation(SQA[:, 2 * q:2 * q + 2, :], YCA[:, 2 * q:2 * q + 2, :], ACT.Square).then_inc(la_sq, 1)
                act.wait_ge(la_var, c + 1)
                act.activation(RSA[:], PS[:, 7, 0:C], ACT.Sqrt, bias=EPS).then_inc(la_sd, 1)
                if c == 0:
                    act.wait_ge(satt, 1 + NS)
                for q in range(2):
                    act.copy(AH[:, HT + 2 * q:HT + 2 * q + 2, chunk(c)], QKV[:, 2 * q:2 * q + 2, chunk(c)]).then_inc(la_hi, 1)
                for k in range(HT):
                    act.wait_ge(la_nrm, 2 * c + k // 2 + 1)
                    act.activation(SQA[:, k, :], YCA[:, k, :], ACT.Silu, bias=row(k, R_LAB), scale=row(k, R_LAG)).then_inc(la_act, 1)
                for q in range(2):
                    act.wait_ge(la_act, 4 * c + 2 * q + 2)
                    act.copy(AH[:, 2 * q:2 * q + 2, chunk(c)], SQA[:, 2 * q:2 * q + 2, :]).then_inc(la_hi, 1)

            def squares(ln, c):
                k = 3 * ln + c
                if k:
                    act.wait_ge(ln_sum2, k)
                for q in range(4):
                    act.wait_ge(ln_cen, 4 * k + q + 1)
                    act.activation(SQ[:, 2 * q:2 * q + 2, :], Y[:, 2 * q:2 * q + 2, chunk(c)], ACT.Square).then_inc(ln_sq, 1)

            def deviation(ln, c):
                k = 3 * ln + c
                act.wait_ge(ln_var, k + 1)
                act.activation(RSD[:, c % 2, :], PS[:, 7, 0:C], ACT.Sqrt, bias=EPS).then_inc(ln_sd, 1)

            def finish(ln, c):
                k, layer, cc = 3 * ln + c, ln // 2, chunk(c)
                g, b = ((R_MG, R_MB), (R_FG, R_FB))[ln % 2]
                for q in range(5):
                    if q < 4:
                        act.wait_ge(ln_nrm, 4 * k + q + 1)
                        for o in (2 * q, 2 * q + 1):
                            last = act.activation(Y[:, o, cc], Y[:, o, cc], ACT.Identity, bias=row(o, b + 2 * layer), scale=row(o, g + 2 * layer))
                        last.then_inc(ln_xf, 1)
                    if q and ln < 3:
                        act.wait_ge(ln_xf, 4 * k + q)
                        act.copy(AH[:, 2 * q - 2:2 * q, cc], Y[:, 2 * q - 2:2 * q, cc]).then_inc(ln_hi, 1)

            def head(ln, split_next, unit, split_after):
                squares(ln, 0)
                split_next()
                deviation(ln, 0)
                finish(ln, 0)
                squares(ln, 1)
                for c in range(NC):
                    unit(0, c)
                    if c == 2:
                        split_after()
                    if c < 2:
                        deviation(ln, c + 1)
                        finish(ln, c + 1)
                    unit(1, c)
                    if c == 0:
                        squares(ln, 2)

            def out_product(st, dn):
                for q in range(4):
                    if q:
                        act.wait_ge(d_done, dn + 6 * q)
                    split(st + q + 1, 2 * (st + q + 1) % 4)

            def hidden(g, f, gu, j, c, u=None):
                u = 3 * j + c if u is None else u
                v, par = 66 * f + 6 * g + u, u % 2
                gated(gu + 6 * g + u, par, ACT.Silu, S)
                act.wait_ge(gu_free, 2 + gu + 6 * g + u + 1)
                act.copy(HH[:, j, chunk(c)], HF[:, par, :]).then_inc(hh_ready, 1)

            def ffn(f):
                st, gu, dn = ffn_units(f)

                def split_next():
                    act.wait_ge(d_done, dn)
                    split(st + 1, 2 * (st + 1) % 4)

                head(2 * f, split_next, lambda j, c: hidden(0, f, gu, j, c, 2 * c + j), lambda: split(st + 2, 2 * (st + 2) % 4))
                split(st + 3, 2 * (st + 3) % 4)

                def group(it, par, last=False):
                    g = 2 * it + (1 if par else 2)
                    for j in range(3):
                        s1 = st + (3 if par else 6) + j + 1
                        if j == 0:
                            act.wait_ge(d_done, dn + 24 * g)
                        for e in range(0 if last and j == 2 else 2):
                            act.wait_ge(w_loaded[2 * s1 % 4 + e], 16 * (s1 // 2 + 1) + 48 * it)
                            act.copy(WHI[:, 2 * s1 % 4 + e, :], RAW[:, 2 * s1 % 4 + e, :]).then_inc(w_hi, 1)
                        if j < 2:
                            for c in range(NC):
                                hidden(g, f, gu, j, c)

                with act.Fori(0, NG // 2 - 1) as it:
                    group(it, 1)
                    group(it, 0)
                group(NG // 2 - 1, 1)
                group(NG // 2 - 1, 0, last=f == 1)

            def mixed(i):
                for c in range(NC):
                    act.wait_ge(mix_done, 3 * i + c + 1)
                    act.activation(YEXT[:, i, chunk(c)], PS[:, 4 + c, 0:C], ACT.Identity, scale=row(i, R_PS)).then_inc(mix_evac, 1)

            out_product(ST_OUT0, DN_OUT0)
            ffn(0)
            def odd_unit(i, n, j, c):
                if j == 0:
                    gated(GU_ODD + 6 * i + n, n % 2, ACT.Copy, S)
                else:
                    gated(GU_ODD + 6 * i + n, n % 2, ACT.Copy, S, BG[:, i, chunk(c)])

            def odd_next():
                act.wait_ge(d_done, DN_OUT1)
                split(ST_ODD + 1, (2 * ST_ODD + 2) % 4)

            head(1, odd_next, lambda j, c: odd_unit(0, 2 * c + j, j, c), lambda: split(ST_ODD + 2, 2 * ST_ODD % 4))
            act.wait_ge(xt_spill, 48)
            for i in range(HT):
                for j in range(2 if i else 0):
                    split(ST_ODD + 2 * i + j + 1, 2 * (ST_ODD + j + 1) % 4)
                    for c in range(NC):
                        odd_unit(i, 3 * j + c, j, c)
                if i == 0:
                    act.wait_ge(wm_in, 16)
                    act.copy(WMH[:], WMR[:]).then_inc(wm_hi, 1)
                act.wait_ge(df_ready, i + 1)
                if i:
                    act.wait_ge(mix_done, 3 * i)
                act.copy(DH[:], DF[i][:, 0:T]).then_inc(dh_ready, 1)
                if i:
                    mixed(i - 1)
            mixed(HT - 1)
            act.wait_ge(gu_done, GU_FF1)
            act.wait_ge(mix_evac, 3 + 3 * HT)
            act.wait_ge(oc_done, HT)
            for c in range(NC):
                for q in range(4):
                    src = BG if q < 2 else YEXT
                    act.copy(AH[:, 2 * q:2 * q + 2, chunk(c)], src[:, 2 * q % 4:2 * q % 4 + 2, chunk(c)]).then_inc(la_hi, 1)
            out_product(ST_OUT1, DN_OUT1)
            ffn(1)
            squares(3, 0)
            deviation(3, 0)
            finish(3, 0)
            squares(3, 1)
            deviation(3, 1)
            finish(3, 1)
            squares(3, 2)
            deviation(3, 2)
            finish(3, 2)

        @block.vector
        def _(dve):
            dve.sem_inc(t_free, 4)
            dve.sem_inc(gu_free, 2)
            dve.sem_inc(d_free, 3)
            dve.sem_inc(pta_ready, 1)
            dve.sem_inc(ot_free, 1)

            def f32(ap):
                return ap.bitcast(F32)

            def two(ap):
                return ap.unsqueeze(1).to_broadcast([P, 2, C])

            def low(out, x, hi):
                return dve.tensor_tensor(out, x, f32(hi), ALU.subtract)

            def split_slot(n, pos, j):
                dve.wait_ge(w_hi, n + j + 1)
                low(WLO[:, pos + j, :], RAW[:, pos + j, :], WHI[:, pos + j, :]).then_inc(w_lo, 1)

            def split(n, pos):
                for j in range(2):
                    split_slot(n, pos, j)

            def split_stage(s):
                split(2 * s, 2 * s % 4)

            def x_tile(i):
                for h in range(2):
                    u, cols = 2 * i + h, slice(i * P, i * P + tw[i])
                    dve.wait_ge(xt_copy, u + 1)
                    src = PS[:, 4 + u % 4, :].rearrange("p (k n) -> p k n", k=4)[:, :, 0:tw[i]]
                    low(AL[:, 4 * h:4 * h + 4, cols], src, AH[:, 4 * h:4 * h + 4, cols]).then_inc(t_free, 1)

            for i in range(3):
                x_tile(i)
            split_stage(0)
            for i in range(3, NTT):
                x_tile(i)
            u = TU_PAR
            dve.wait_ge(t_done, u + 1)
            dve.tensor_copy(PRT[:], PS[:, 4 + u % 4, 0:HT * R_ALL].rearrange("p (k n) -> p k n", k=HT)).then_inc(t_free, 1)
            for i in range(2):
                u = TU_SA + i
                dve.wait_ge(t_done, u + 1)
                for k in range(HT):
                    src = PS[:, 4 + u % 4, 4 * HA * k:4 * HA * (k + 1)].rearrange("p (s e) -> p s e", s=4)
                    last = dve.tensor_copy(history(AEXT, HA, k, 4 * i, 4), src)
                last.then_inc(t_free, 1)

            def to_ext(tile, h, k, c, op):
                lo, hi = c * C, min((c + 1) * C, TP)
                last = op(prompt_cols(tile, h, k, lo, hi), slice(0, hi - lo), False)
                if (c + 1) * C > TP:
                    last = op(sample_cols(tile, h, k), slice(TP - lo, C), True)
                return last

            def product(par, s_tile):
                def op(out, cols, seq):
                    a, b = PS[:, 2 * par + 1, cols], s_tile[:, par, cols]
                    return dve.tensor_tensor(out, by_seq(a) if seq else a, by_seq(b) if seq else b, ALU.mult)
                return op

            def plain(par):
                def op(out, cols, seq):
                    a = PS[:, 2 * par + 1, cols]
                    return dve.tensor_copy(out, by_seq(a) if seq else a)
                return op

            def taps():
                steps = 0
                for k in range(HT):
                    dve.wait_ge(ext_zero, 1)
                    dve.wait_ge(gu_free, 2 + 3 * (k + 1))
                    if k:
                        dve.wait_ge(conv_done, k)
                    for j in range(CW):
                        if steps:
                            dve.wait_ge(acc_step, steps)
                        acc_p, acc_s = CACC[:, 0:TP], by_seq(CACC[:, TP:T])
                        in_p, in_s = prompt_cols(AEXT, HA, k, 0, TP, HA - j), sample_cols(AEXT, HA, k, HA - j)
                        if j == 0:
                            for acc, src in ((acc_p, in_p), (acc_s, in_s)):
                                dve.tensor_scalar(acc, src, row(k, R_DW), row(k, R_BDW), ALU.mult, ALU.add).then_inc(acc_step, 1)
                            steps += 2
                        elif j < CW - 1:
                            for acc, src in ((acc_p, in_p), (acc_s, in_s)):
                                dve.scalar_tensor_tensor(acc, src, row(k, R_DW + j), acc, ALU.mult, ALU.add).then_inc(acc_step, 1)
                            steps += 2
                        else:
                            dve.scalar_tensor_tensor(acc_p, in_p, row(k, R_DW + j), acc_p, ALU.mult, ALU.add)
                            dve.scalar_tensor_tensor(acc_s, in_s, row(k, R_DW + j), acc_s, ALU.mult, ALU.add).then_inc(acc_done, 1)
                        yield

            conv = taps()
            for k in range(HT):
                split_stage(k + 1)
                for c in range(NC):
                    n = 3 * k + c
                    dve.wait_ge(s_ready, n + 1)
                    to_ext(AEXT, HA, k, c, product(n % 2, S)).then_inc(gu_free, 1)
                    for _ in range(3 if k else 0):
                        next(conv)
            dve.wait_ge(wf_hi, 1)
            low(WFL[:], WFR[:], WFH[:]).then_inc(wf_lo, 1)
            for u, tile, rows in ((TU_A, STA, HA), (TU_A + 1, STB, NS * NQ)):
                dve.wait_ge(t_done, u + 1)
                dve.tensor_copy(tile[:], PS[0:rows, 4 + u % 4, :]).then_inc(t_free, 1)

            for q in range(6):
                split_stage(ST_QKV + q + 1)
                if q == 5:
                    dve.wait_ge(sta_sent, 16 * (1 + NS))
                for c in range(NC):
                    n = 3 * q + c
                    dve.wait_ge(s_ready, GU_QKV + n + 1)
                    dve.tensor_copy(QKV[:, 2 * q + 1, chunk(c)], PS[:, 2 * (n % 2) + 1, 0:C]).then_inc(gu_free, 1)
                    for _ in range(TAPS):
                        next(conv, None)
            for _ in conv:
                pass
            dve.wait_ge(f_act, NC + 3)
            dve.scalar_tensor_tensor(LFZ[:, 2, :], LFZ[:, 0, :], 0.0, LFZ[:, 1, :], ALU.min, ALU.subtract).then_inc(lf_ready, 1)
            dve.wait_ge(lf_ready, 1)
            dve.tensor_tensor_scan(LFC[:], CST[0:NH, K_ONE:K_ONE + 1].to_broadcast([NH, TP]), LFZ[:, 2, 0:TP], 0.0,
                                   ALU.mult, ALU.add).then_inc(c_ready, 1)
            dve.wait_ge(c_hi, 1)
            low(LCL[:], LFC[:], LCH[:]).then_inc(c_lo, 1)
            for n in range(2 * NTT):
                u = TU_KV + n
                dve.wait_ge(t_done, u + 1)
                if n >= 4:
                    dve.wait_ge(stg_sent[n % 4], 16 * (n // 4))
                rows = tw[n // 2]
                dve.tensor_copy(STG[0:rows, n % 4, :], PS[0:rows, 4 + u % 4, :]).then_inc(t_free, 1)
            u = TU_LF
            dve.wait_ge(t_done, u + 1)
            dve.tensor_copy(LFO[:, 0:8, :], PS[:, 4 + u % 4, 0:8 * NH].rearrange("p (b h) -> p b h", b=8))
            dve.tensor_copy(LFO[0:tw[8], 8, :], PS[0:tw[8], 4 + u % 4, 8 * NH:9 * NH]).then_inc(t_free, 1)

            def peak(it, a, h2, j, i, m, n, na, nb):
                base = (0, 3)[a % 2]
                dve.wait_ge(qk_done, 36 * it + a + 1)
                src = PS[0:m, base:base + (n + 511) // 512, :].rearrange("p b n -> p (b n)")[:, 0:n]
                dve.tensor_reduce(ST4[0:m, 0, a:a + 1], src, AX_X, ALU.max, negate=True).then_inc(nm_ready, 1)

            def inverse(it, a, h2, j, i, m, n, na, nb):
                dve.wait_ge(exp_done, 36 * it + a + 3)
                dve.reciprocal(ST4[0:m, 2, a:a + 1], ST4[0:m, 1, a:a + 1]).then_inc(rc_ready, 1)

            def turned(it, a, h2, j, i, m, n, na, nb):
                bank = PS[:, 5, :].rearrange("p (k n) -> p k n", k=4)
                dve.wait_ge(ta_done, NA * it + na + 1)
                w = min(4, i + 1)
                dve.tensor_copy(PT[:, a % 2, 0:w, 0:m], bank[:, 0:w, 0:m]).then_inc(pta_ready, 1)
                if i == 8:
                    dve.wait_ge(ta_done, NA * it + na + 2)
                    dve.tensor_copy(PT[0:META, a % 2, 8, 0:m], PS[0:META, 5, 0:m]).then_inc(pta_ready, 1)

            dve.wait_ge(ab_open, 1)
            def head_low(it, x, part):
                h2 = x % 2
                own, other = slice(HD * h2, HD * (h2 + 1)), slice(HD * (1 - h2), HD * (2 - h2))
                if part == 0:
                    dve.wait_ge(qk_hi, 16 * it + 4 * x + 1)
                    src = QKV[own, bass.ds(2 * it + x // 2 + HT, 1), 0:TP].rearrange("p a n -> p (a n)")
                    low(KS2[0:HD, h2, :], src, KS1[own, h2, :]).then_inc(qk_lo, 1)
                elif part == 1:
                    dve.wait_ge(qk_hi, 16 * it + 4 * x + 2)
                    src = QKV[own, bass.ds(2 * it + x // 2, 1), 0:TP].rearrange("p a n -> p (a n)")
                    dve.scalar_tensor_tensor(QS1[other, h2, :], src, HD ** -0.5, f32(QS1[own, h2, :]), ALU.mult, ALU.subtract).then_inc(qk_lo, 1)
                else:
                    dve.tensor_scalar(QS2[64:96, h2, :], QBA[:], CST[0:32, bass.ds(K_MSK + 4 * it + x, 1)], None, ALU.mult).then_inc(qk_lo, 1)

            with dve.Fori(0, 2) as it:
                for part in range(3):
                    head_low(it, 0, part)
                for n in range(36 + 2):
                    if n < 27 and n % 9 in (4, 5, 6):
                        head_low(it, n // 9 + 1, n % 9 - 4)
                    if 1 <= n < 37:
                        inverse(it, *ATT[n - 1])
                    if n < 36:
                        peak(it, *ATT[n])
                    if n >= 2:
                        turned(it, *ATT[n - 2])

            dve.wait_ge(t_done, TU_LFS + 1)
            dve.tensor_copy(LFS[:, 0:PAST], PS[0:64, 6, :]).then_inc(t_free, 1)
            dve.wait_ge(t_free, 4 + TU_LFS + 1)
            dve.wait_ge(lfs_in, 16)
            dve.tensor_tensor_scan(KBS[0:64, :], CST[0:64, K_ONE:K_ONE + 1].to_broadcast([64, KS]), LFS[:], 0.0,
                                   ALU.mult, ALU.add).then_inc(cs_ready, 1)
            dve.wait_ge(sel_in, 16)
            dve.wait_ge(cq_ready, 1)
            half = SELC[64:128].rearrange("p s h q -> p (s h) q")
            dve.tensor_tensor(half, half, CQ2[64:128, :].unsqueeze(1).to_broadcast([64, NS * NH, NQ]), ALU.mult).then_inc(sel_ready, 1)
            with dve.Fori(0, NS // 2) as it:
                for j in range(2):
                    s = 2 * it + j
                    dve.wait_ge(sqk_done, s + 1)
                    dve.tensor_reduce(ST5[:, j, 0:1], PS[0:64, 4:6, :].rearrange("p b n -> p (b n)")[:, 0:KS], AX_X, ALU.max,
                                      negate=True).then_inc(snm, 1)
                    dve.wait_ge(sexp, s + 2)
                    dve.reciprocal(ST5[:, j, 2:3], ST5[:, j, 1:2]).then_inc(src_, 1)
                    dve.wait_ge(src_, s + 1)
                    dve.tensor_scalar(PSA[:, j, :], PSA[:, j, :], ST5[:, j, 2:3], None, ALU.mult).then_inc(spn, 1)

            for c in range(NC):
                cc = chunk(c)
                dve.wait_ge(la_mean, c + 1)
                for q in range(2):
                    qs = slice(2 * q, 2 * q + 2)
                    dve.tensor_tensor(YCA[:, qs, :], AEXT[:, qs, cc], two(PS[:, 7, 0:C]), ALU.subtract).then_inc(la_cen, 1)
                dve.wait_ge(la_sd, c + 1)
                dve.reciprocal(RSA[:], RSA[:]).then_inc(la_rs, 1)
                dve.wait_ge(la_rs, c + 1)
                for q in range(2):
                    qs = slice(2 * q, 2 * q + 2)
                    dve.tensor_tensor(YCA[:, qs, :], YCA[:, qs, :], two(RSA[:]), ALU.mult).then_inc(la_nrm, 1)
                for q in range(2):
                    qs, ks = slice(2 * q, 2 * q + 2), slice(HT + 2 * q, HT + 2 * q + 2)
                    dve.wait_ge(la_hi, 4 * c + q + 1)
                    low(AL[:, ks, cc], QKV[:, qs, cc], AH[:, ks, cc]).then_inc(m_ready, 1)
                for q in range(2):
                    qs = slice(2 * q, 2 * q + 2)
                    dve.wait_ge(la_hi, 4 * c + 2 + q + 1)
                    low(AL[:, qs, cc], SQA[:, qs, :], AH[:, qs, cc]).then_inc(m_ready, 1)

            def centre(ln, c, qs=range(4)):
                k, cc = 3 * ln + c, chunk(c)
                for q in qs:
                    ts = slice(2 * q, 2 * q + 2)
                    dve.wait_ge(ln_mean, k + 1)
                    dve.tensor_tensor(Y[:, ts, cc], Y[:, ts, cc], two(PS[:, 7, 0:C]), ALU.subtract).then_inc(ln_cen, 1)

            def normalise(ln, c):
                k, cc, rs = 3 * ln + c, chunk(c), RSD[:, c % 2, :]
                dve.wait_ge(ln_sd, k + 1)
                dve.reciprocal(rs, rs).then_inc(ln_rs, 1)
                dve.wait_ge(ln_rs, k + 1)
                for q in range(4):
                    ts = slice(2 * q, 2 * q + 2)
                    dve.wait_ge(ln_sq, 4 * k + q + 1)
                    dve.tensor_tensor(Y[:, ts, cc], Y[:, ts, cc], two(rs), ALU.mult).then_inc(ln_nrm, 1)

            def x_low(ln, c):
                k, cc = 3 * ln + c, chunk(c)
                for q in range(4):
                    ts = slice(2 * q, 2 * q + 2)
                    dve.wait_ge(ln_hi, 4 * k + q + 1)
                    low(AL[:, ts, cc], Y[:, ts, cc], AH[:, ts, cc]).then_inc(x_ready, 1)

            def head(ln, split_next, unit, split_after):
                split_next()
                normalise(ln, 0)
                x_low(ln, 0)
                centre(ln, 1)
                for c in range(NC):
                    unit(0, c)
                    if c == 2:
                        split_after()
                    if c < 2:
                        normalise(ln, c + 1)
                        x_low(ln, c + 1)
                    unit(1, c)
                    if c == 0:
                        centre(ln, 2)

            def out_product(layer, st, dn):
                for q in range(4):
                    split_stage(st + q + 1)
                    for c in range(NC):
                        for w in range(2):
                            n, o = 6 * q + 2 * c + w, 2 * q + w
                            if q == 3 and c == 2:
                                centre(2 * layer, 0, (2 * w, 2 * w + 1))
                            if c == 0:
                                dve.wait_ge(y_in[o], 16 * (layer + 1))
                            dve.wait_ge(d_done, dn + n + 1)
                            y = Y[:, o, chunk(c)]
                            dve.scalar_tensor_tensor(y, y, ALPHA, PS[:, 4 + n % 3, 0:C], ALU.mult, ALU.add).then_inc(d_free, 1)

            def hidden(g, f, gu, j, c, u=None):
                u = 3 * j + c if u is None else u
                unit, v, par = gu + 6 * g + u, 66 * f + 6 * g + u, u % 2
                dve.wait_ge(s_ready, unit + 1)
                dve.tensor_tensor(HF[:, par, :], S[:, par, :], PS[:, 2 * par + 1, 0:C], ALU.mult).then_inc(gu_free, 1)
                dve.wait_ge(hh_ready, v + 1)
                low(HL[:, j, chunk(c)], HF[:, par, :], HH[:, j, chunk(c)]).then_inc(h_ready, 1)

            def down(g, f, dn, split_slot, first=False, last=False):
                for c in range(NC):
                    for o in range(KT):
                        n = 8 * c + o
                        if last and c == 2 and o % 2 == 0:
                            centre(2 * f + 1, 0, (o // 2,))
                        dve.wait_ge(d_done, dn + 24 * g + n + 1)
                        y = Y[:, o, chunk(c)]
                        if first:
                            dve.scalar_tensor_tensor(y, y, ALPHA, PS[:, 4 + n % 3, 0:C], ALU.mult, ALU.add).then_inc(d_free, 1)
                        else:
                            dve.tensor_tensor(y, y, PS[:, 4 + n % 3, 0:C], ALU.add).then_inc(d_free, 1)
                        if n in (4, 9):
                            split_slot(n // 9)

            def ffn(f):
                st, gu, dn = ffn_units(f)
                head(2 * f, lambda: split_stage(st + 1), lambda j, c: hidden(0, f, gu, j, c, 2 * c + j), lambda: split_stage(st + 2))
                down(0, f, dn, lambda j: split_slot(2 * (st + 3), 2 * (st + 3) % 4, j), first=True)

                def group(it, par, last=False):
                    g = 2 * it + (1 if par else 2)
                    s0 = st + (3 if par else 6)
                    for j in range(2):
                        split(2 * (s0 + j + 1) + 12 * it, 2 * (s0 + j + 1) % 4)
                        for c in range(NC):
                            hidden(g, f, gu, j, c)
                    down(g, f, dn, lambda j: None if last and f == 1 else split_slot(2 * (s0 + 3) + 12 * it, 2 * (s0 + 3) % 4, j), last=last)

                with dve.Fori(0, NG // 2 - 1) as it:
                    group(it, 1)
                    group(it, 0)
                group(NG // 2 - 1, 1)
                group(NG // 2 - 1, 0, last=True)

            out_product(0, ST_OUT0, DN_OUT0)
            ffn(0)

            steps = [0]

            def step(ins):
                steps[0] += 1
                ins.then_inc(tap, 1)
                dve.wait_ge(tap, steps[0])

            def new_rows(i):
                dve.wait_ge(ot_done, i + 1)
                cs = slice(i * P, (i + 1) * P)
                dve.tensor_copy(OSA[0:NS * NQ, cs], PS[0:NS * NQ, 7, 0:P])
                dve.tensor_copy(OSA[64:64 + HS, cs], PS[0:HS, 7, P:2 * P])
                dve.tensor_copy(OSA[96:96 + HP, cs], PS[0:HP, 7, 2 * P:3 * P])
                dve.tensor_copy(OSB[:, cs], PS[0:NS * HS, 7, 3 * P:4 * P]).then_inc(ot_free, 1)

            def odd_unit(i, n, j, c):
                dve.wait_ge(s_ready, GU_ODD + 6 * i + n + 1)
                if j == 0:
                    to_ext(YEXT, HS, i, c, product(n % 2, S)).then_inc(gu_free, 1)
                else:
                    to_ext(PEXT, HP, i, c, plain(n % 2)).then_inc(gu_free, 1)

            head(1, lambda: split_stage(ST_ODD + 1), lambda j, c: odd_unit(0, 2 * c + j, j, c), lambda: split_stage(ST_ODD + 2))
            dve.wait_ge(xt_spill, 48)
            for u, bank, tile, h in ((TU_ST, 7, YEXT, HS), (TU_ST + 1, 4, PEXT, HP)):
                dve.wait_ge(t_done, u + 1)
                for k in range(HT):
                    last = dve.tensor_copy(history(tile, h, k, 0, NS), by_seq(PS[:, bank, NS * h * k:NS * h * (k + 1)]))
                last.then_inc(t_free, 1)
            dve.wait_ge(od_zero, 2)
            for i in range(HT):
                for j in range(2 if i else 0):
                    split_stage(ST_ODD + 2 * i + j + 1)
                    for c in range(NC):
                        odd_unit(i, 3 * j + c, j, c)
                if i == 0:
                    dve.wait_ge(wm_hi, 1)
                    low(WML[:], WMR[:], WMH[:]).then_inc(wm_lo, 1)
                    dve.wait_ge(t_free, 4 + TU_ST + 2)
                if i:
                    dve.wait_ge(ot_done, i)
                dve.wait_ge(gu_free, 2 + GU_ODD + 6 * (i + 1))
                y_new, p_new = sample_cols(YEXT, HS, i), sample_cols(PEXT, HP, i)
                dve.tensor_copy(by_seq(CMP[:, 0:NS * HS]), y_new[:, :, NQ - HS:])
                dve.tensor_copy(by_seq(CMP[:, NS * HS:]), p_new).then_inc(cmp_ready, 1)
                if i:
                    dve.wait_ge(dh_ready, i)
                    new_rows(i - 1)
                for j in range(SW):
                    for acc, src in ((T1[:, 0:TP], prompt_cols(YEXT, HS, i, 0, TP, HS - j)),
                                     (by_seq(T1[:, TP:T]), sample_cols(YEXT, HS, i, HS - j))):
                        if j == 0:
                            step(dve.tensor_scalar(acc, src, row(i, R_SC), None, ALU.mult))
                        else:
                            step(dve.scalar_tensor_tensor(acc, src, row(i, R_SC + j), acc, ALU.mult, ALU.add))
                dve.tensor_tensor(BG[:, i, :], BG[:, i, :], T1[:, 0:T], ALU.mult).then_inc(oc_done, 1)
                src, lo = PEXT[:, i, :], 0
                for d in range(i + 1):
                    w, dst = 1 << d, (T2, T1)[d % 2]
                    step(dve.tensor_tensor(dst[:, lo + w:EP], src[:, lo + w:EP], src[:, lo:EP - w], ALU.add))
                    src, lo = dst, lo + w
                w, df = 2 << i, DF[i]
                first = src[:, HP:HP + PW]
                step(dve.tensor_tensor(first, first, CST[:, K_CNT + PW * i:K_CNT + PW * (i + 1)], ALU.mult))
                dve.tensor_tensor(df[:, 0:PW], first, PEXT[:, i, HP:HP + PW], ALU.subtract)
                dve.scalar_tensor_tensor(df[:, PW:TP], src[:, HP + PW:HP + TP], 1.0 / w, PEXT[:, i, HP + PW:HP + TP], ALU.mult, ALU.subtract)
                sums = src[:, HP + TP:EP].rearrange("p (s e) -> p s e", s=NS)[:, :, HP:]
                dve.scalar_tensor_tensor(by_seq(df[:, TP:T]), sums, 1.0 / w, p_new, ALU.mult, ALU.subtract).then_inc(df_ready, 1)
                dve.wait_ge(dh_ready, i + 1)
                if i:
                    dve.wait_ge(mix_done, 3 * i)
                low(DL[:], df[:, 0:T], DH[:]).then_inc(dl_ready, 1)
            new_rows(HT - 1)
            for c in range(NC):
                for q in range(4):
                    src = BG if q < 2 else YEXT
                    dve.wait_ge(la_hi, 12 + 4 * c + q + 1)
                    qs = slice(2 * q, 2 * q + 2)
                    low(AL[:, qs, chunk(c)], src[:, 2 * q % 4:2 * q % 4 + 2, chunk(c)], AH[:, qs, chunk(c)]).then_inc(m_ready, 1)
            out_product(1, ST_OUT1, DN_OUT1)
            ffn(1)

            def y_rows(c):
                n = sum(len(YPIECES[x]) for x in range(c))
                for a, w in YPIECES[c]:
                    for h in range(2):
                        u = 2 * n + h
                        dve.wait_ge(t_done, TU_Y + u + 1)
                        if n >= 4:
                            dve.wait_ge(yo_sent[n % 4], 16 * (n // 4))
                        dve.tensor_copy(YO[0:w, n % 4, h * HALF:(h + 1) * HALF], PS[0:w, u % 4, :]).then_inc(t_free, 1)
                    n += 1

            normalise(3, 0)
            centre(3, 1)
            y_rows(0)
            normalise(3, 1)
            centre(3, 2)
            y_rows(1)
            normalise(3, 2)
            y_rows(2)


_INS = ["x_prompt", "x_sample", "cache_k", "cache_v", "cache_logf", "page_table", "state_conv_a", "state_sconv", "state_pool",
        "meta_tokens", "w_in_even", "b_forget", "w_dw_a", "b_dw_a", "ln_a_g", "ln_a_b", "w_out_even", "w_in_odd", "w_sconv",
        "w_pool_mix", "pool_scale", "w_out_odd", "ln_mix_g", "ln_mix_b", "w_ffn_gate", "w_ffn_up", "w_ffn_down", "ln_ffn_g",
        "ln_ffn_b"]
_OUTS = [("y_prompt", (1, SEQ, D)), ("y_sample", (NS, NQ, D)), ("k_prompt", (1, 1, TP, NH, HD)), ("v_prompt", (1, 1, TP, NH, HD)),
         ("logf_prompt", (1, 1, TP, NH)), ("conv_a_prompt", (1, 1, HA, HALF)), ("sconv_prompt", (1, 1, HS, HALF)),
         ("pool_prompt", (1, 1, HP, HALF)), ("k_sample", (NS, 1, NQ, NH, HD)), ("v_sample", (NS, 1, NQ, NH, HD)),
         ("logf_sample", (NS, 1, NQ, NH)), ("conv_a_sample", (NS, 1, HA, HALF)), ("sconv_sample", (NS, 1, HS, HALF)),
         ("pool_sample", (NS, 1, HP, HALF))]


def kernel(**inputs):
    import concourse.bacc as bacc
    from concourse.bass_utils import run_bass_kernel_spmd

    nc = bacc.Bacc("TRN2", target_bir_lowering=False, num_devices=1)
    arrays, aps = {}, {}
    for name in _INS + ["consts"]:
        a = constants() if name == "consts" else np.ascontiguousarray(inputs[name])
        arrays[f"in_{name}"] = a
        aps[name] = nc.dram_tensor(f"in_{name}", a.shape, mybir.dt.from_np(a.dtype), kind="ExternalInput").ap()
    for name, shape in _OUTS:
        aps[name] = nc.dram_tensor(f"out_{name}", shape, F32, kind="ExternalOutput").ap()
    build(nc, aps)
    r = run_bass_kernel_spmd(nc, [arrays], core_ids=[0])
    return tuple(r.results[0][f"out_{name}"] for name, _ in _OUTS)
```

```python
from contextlib import ExitStack

import numpy as np

import concourse.bass as bass
from concourse import mybir

F32 = mybir.dt.float32
F32R = mybir.dt.float32r
I32 = mybir.dt.int32
ALU = mybir.AluOpType
ACT = mybir.ActivationFunctionType
AX_X = mybir.AxisListType.X

P = 128
D = 1024
KT = D // P
META, SEQ = 16, 1024
TP = META + SEQ
NS, NQ = 8, 8
T = TP + NS * NQ
NC = 3
C = T // NC
HALF = D // 2
HT = HALF // P
NH, HD = 8, 64
CW, SW, PW = 31, 3, 16
HA, HS, HP = CW - 1, SW - 1, PW - 1
FF = 2816
NG = FF // P // 2
PAGE, NPAGE = 128, 4
PAST = PAGE * NPAGE
KS = PAST + NQ
ALPHA = float(4 ** 0.25)
EPS = 1e-5
NEG = -float(2 ** 100)
NTT = (T + P - 1) // P
EA, ES, EP = HA + TP + NS * (HA + NQ), HS + TP + NS * (HS + NQ), HP + TP + NS * (HP + NQ)

R_DW, R_BDW, R_LAG, R_LAB, R_SC, R_PS = 0, 31, 32, 33, 34, 37
R_MG, R_MB, R_FG, R_FB, R_ALL = 38, 42, 46, 50, 54

K_ID, K_O1024, K_O512, K_MASK, K_MS, K_MSK, K_CNT, K_ONE, K_SEL, K_ALL = 0, 128, 256, 384, 512, 520, 528, 592, 600, 1112

ST_UG, ST_QKV, ST_OUT0, ST_FF0 = 0, 4, 10, 14
ST_ODD = ST_FF0 + 3 * NG
ST_OUT1 = ST_ODD + 8
ST_FF1 = ST_OUT1 + 4
ST_END = ST_FF1 + 3 * NG
GU_UG, GU_QKV, GU_FF0 = 0, 12, 30
GU_ODD = GU_FF0 + 6 * NG
GU_FF1 = GU_ODD + 24
DN_OUT0, DN_FF0 = 0, 24
DN_OUT1 = DN_FF0 + 24 * NG
DN_FF1 = DN_OUT1 + 24
TU_X, TU_PAR, TU_SA, TU_A, TU_KV, TU_LF, TU_LFS, TU_ST, TU_Y = 0, 18, 19, 21, 23, 41, 42, 43, 45
TAPS = 4
XB, TB = 6, 4
MEAN_BANK = (7, 3, 7)
PV0 = 64 * (NPAGE + 1)
ORDER = (tuple(range(9)), (0, 8, 1, 2, 3, 4, 5, 6, 7))


def constants():
    k = np.zeros((P, K_ALL), np.float32)
    k[:, K_ID:K_ID + P] = np.eye(P)
    k[:, K_O1024:K_O1024 + P] = 1.0 / D
    k[:, K_O512:K_O512 + P] = 1.0 / HALF
    i = np.arange(P)
    k[:, K_MASK:K_MASK + P] = np.where(i[None, :] > i[:, None], NEG, 0.0)
    q = np.arange(64) % NQ
    k[:64, K_MS:K_MS + NQ] = np.where(np.arange(NQ)[None, :] > q[:, None], NEG, 0.0)
    k[:32, K_MSK:K_MSK + NH] = np.arange(NH)[None, :] == (np.arange(32) % NH)[:, None]
    for g, w in enumerate((2, 4, 8, 16)):
        k[:, K_CNT + PW * g:K_CNT + PW * (g + 1)] = 1.0 / np.minimum(w, np.arange(PW) + 1.0)
    k[:, K_ONE] = 1.0
    sel = np.zeros((NS, NH, NS, NH, NQ), np.float32)
    for s in range(NS):
        for h in range(NH):
            sel[s, h, s, h, :] = 1.0
    sel = sel.reshape(64, NS * 64)
    k[:64, K_SEL:] = -sel
    k[64:, K_SEL:] = sel
    return k


def build(nc, t):
    ctx = ExitStack()
    with ctx:
        def at(name, off, shape, dt=F32):
            n = int(np.prod(shape[1:])) * 4
            assert off % 32 == 0 and off + n <= 229344, (name, off, n)
            return nc.alloc_sbuf_tensor_at(name, shape, dt, offset=off), (off + n + 31) // 32 * 32

        def sem(name):
            return ctx.enter_context(nc.semaphore(name))

        CST, o = at("CST", 16512, [P, K_SEL])
        PRT, o = at("PRT", o, [P, HT, R_ALL])
        PTB, o = at("PTB", o, [1, NS * NPAGE], I32)
        BF, o = at("BF", o, [NH, 8])
        assert o <= 21120
        RAW, o = at("RAW", 21120, [P, 4, D])
        WHI, o = at("WHI", o, [P, 4, D], F32R)
        WLO, A0 = at("WLO", o, [P, 4, D], F32R)
        AH, o = at("AH", A0, [P, KT, T], F32R)
        AL, B0 = at("AL", o, [P, KT, T], F32R)
        R0 = B0 + 12 * T * 4
        QKV, _ = at("QKV", B0, [P, 12, T])
        AEXT, o = at("AEXT", R0, [P, HT, EA])
        CACC, _ = at("CACC", o, [P, T])
        STA, o = at("STA", B0 + 11 * T * 4, [HA, HALF])
        STB, _ = at("STB", o, [NS * NQ, HALF])
        S, o = at("S", R0 + 26400, [P, 2, C])
        HF, _ = at("HF", o, [P, 2, C])
        ACMP, _ = at("ACMP", o, [P, HT, NS, NQ])
        SELC, _ = at("SELC", o, [P, NS, NH, NQ])
        WFR, o = at("WFR", R0 + 32288, [P, KT, NH])
        WFH, o = at("WFH", o, [P, KT, NH], F32R)
        WFL, o = at("WFL", o, [P, KT, NH], F32R)
        LFR, o = at("LFR", o, [P, NPAGE, NS, NH])
        HH, o = at("HH", B0, [P, 2, T], F32R)
        HL, o = at("HL", o, [P, 2, T], F32R)
        Y, o = at("Y", o, [P, KT, T])
        SQ, o = at("SQ", R0, [P, KT, C])
        RSD, o = at("RSD", o, [P, 2, C])
        YSM, o = at("YSM", o, [P, 2, C])
        YSV, o = at("YSV", o, [P, 2, C])
        YCA, o = at("YCA", B0 + 8 * T * 4, [P, HT, C])
        SQA, o = at("SQA", o, [P, HT, C])
        YSA, o = at("YSA", o, [P, 2, C])
        RSA, o = at("RSA", o, [P, C])
        assert o <= R0
        XIN, o = at("XIN", B0, [P, XB, D])
        XTT, o = at("XTT", o, [P, TB, KT, P])
        PIN, o = at("PIN", o, [R_ALL, HALF])
        SIN, o = at("SIN", o, [P, 2, HALF])
        assert o <= B0 + 11 * T * 4
        STG, o = at("STG", A0, [P, 4, HALF])
        LFZ, o = at("LFZ", o, [NH, 3, T])
        LFC, o = at("LFC", o, [NH, TP])
        LCH, o = at("LCH", o, [NH, TP], F32R)
        LCL, o = at("LCL", o, [NH, TP], F32R)
        stage_end = o
        QS1, o = at("QS1", A0, [P, 2, TP], F32R)
        KS1, o = at("KS1", o, [P, 2, TP], F32R)
        QS2, o = at("QS2", o, [96, 2, TP], F32R)
        PB, o = at("PB", o, [P, 3, TP])
        assert o >= stage_end
        VP, o = at("VP", o, [P, 2, NTT, P])
        PT, o = at("PT", o, [P, 2, NTT, P])
        KS2, o = at("KS2", o, [96, 2, TP], F32R)
        QBA, o = at("QBA", o, [32, TP])
        IDR, o = at("IDR", o, [P, P], F32R)
        MKR, o = at("MKR", o, [P, P], F32R)
        ST4, o = at("ST4", o, [P, 3, 36])
        LFO, o = at("LFO", o, [P, NTT, NH])
        assert o <= B0
        KR, o = at("KR", A0, [P, 2, NPAGE, HALF])
        VR, o = at("VR", o, [P, 2, NPAGE + 1, HALF])
        KTS, o = at("KTS", o, [P, 2, HT, KS])
        PSA, o = at("PSA", o, [64, 2, KS])
        PTS, o = at("PTS", o, [P, 2, NPAGE + 1, 64])
        QBD, o = at("QBD", o, [P, 2, 328])
        LFS, o = at("LFS", o, [64, KS])
        KBS, o = at("KBS", o, [P, KS])
        SLS, o = at("SLS", o, [P, 2, 64])
        CQ2, o = at("CQ2", o, [P, NQ])
        ST5, o = at("ST5", o, [64, 2, 8])
        assert o <= B0
        MIX, o = at("MIX", B0, [P, HT, ES + T + EP])
        YEXT, BG, PEXT = MIX[:, :, 0:ES], MIX[:, :, ES:ES + T], MIX[:, :, ES + T:]
        assert (ES + T + EP) * 4 <= 4 * T * 4
        T1, o = at("T1", o, [P, EP + 1])
        T2, o = at("T2", o, [P, EP + 1])
        DH, o = at("DH", o, [P, T], F32R)
        WMR, _ = at("WMR", o, [P, HT, P])
        DL, o = at("DL", o, [P, T], F32R)
        OSA, o = at("OSA", o, [P, HALF])
        OSB, o = at("OSB", o, [NS * HS, HALF])
        CMP, o = at("CMP", o, [P, NS * HS + NS * NQ])
        assert o <= R0 + 26400
        WMH, o = at("WMH", R0 + 29344, [P, HT, P], F32R)
        WML, o = at("WML", o, [P, HT, P], F32R)
        DF = (T1, T2, T1, T2)
        YO, _ = at("YO", A0, [P, 4, D])
        PS = ctx.enter_context(nc.psum_tensor("PS", [P, 8, 512], F32))
        XT = nc.dram_tensor("x_spill", [P, KT, T], F32, kind="Internal").ap()
        LFD = nc.dram_tensor("lf_spill", [NS * NH, NQ], F32, kind="Internal").ap()
        IDN = CST[:, K_ID:K_ID + P]
        ONES_D, ONES_H = CST[:, K_O1024:K_O1024 + P], CST[:, K_O512:K_O512 + P]

        def prompt_cols(tile, h, k, lo, hi, shift=0):
            return tile[:, k, h + lo - shift:h + hi - shift]

        def sample_cols(tile, h, k, shift=0):
            v = tile[:, k, h + TP:h + TP + NS * (h + NQ)].rearrange("p (s e) -> p s e", s=NS)
            return v[:, :, h - shift:h - shift + NQ]

        def history(tile, h, k, s0, n):
            v = tile[:, k, h + TP:h + TP + NS * (h + NQ)].rearrange("p (s e) -> p s e", s=NS)
            return v[:, s0:s0 + n, 0:h]

        def by_seq(ap):
            return ap.rearrange("p (s e) -> p s e", s=NS)

        def row(k, r):
            return PRT[:, k % HT, r + k // HT:r + k // HT + 1]

        s_cst, s_par, s_xin = sem("s_cst"), sem("s_par"), [sem(f"s_xin{i}") for i in range(XB)]
        s_sin, s_bf, s_wf, s_ptb, ext_zero = sem("s_sin"), sem("s_bf"), sem("s_wf"), sem("s_ptb"), sem("ext_zero")
        w_loaded = [sem(f"w_loaded{i}") for i in range(4)]
        w_hi, w_lo = sem("w_hi"), sem("w_lo")
        t_done, t_free = sem("t_done"), sem("t_free")
        xt_copy = sem("xt_copy")
        xt_sent = [sem(f"xt_sent{i}") for i in range(TB)]
        gu_done, s_ready, gu_free = sem("gu_done"), sem("s_ready"), sem("gu_free")
        hh_ready, h_ready = sem("hh_ready"), sem("h_ready")
        d_done, d_free = sem("d_done"), sem("d_free")
        acmp_ready, sta_sent, acc_step, acc_done, conv_done = (sem("acmp_ready"), sem("sta_sent"), sem("acc_step"),
                                                              sem("acc_done"), sem("conv_done"))
        wf_hi, wf_lo, f_done, f_act, lf_ready = sem("wf_hi"), sem("wf_lo"), sem("f_done"), sem("f_act"), sem("lf_ready")
        c_ready, c_hi, c_lo, kb_sent, kb_fill, lfd_sent = (sem("c_ready"), sem("c_hi"), sem("c_lo"), sem("kb_sent"),
                                                           sem("kb_fill"), sem("lfd_sent"))
        stg_sent, ab_open = [sem(f"stg_sent{i}") for i in range(4)], sem("ab_open")
        idr_ready, qk_hi, qk_lo = sem("idr_ready"), sem("qk_hi"), sem("qk_lo")
        vp_ready = [sem("vp_ready0"), sem("vp_ready1")]
        qk_done, nm_ready, exp_done, rc_ready, pn_ready = (sem("qk_done"), sem("nm_ready"), sem("exp_done"),
                                                           sem("rc_ready"), sem("pn_ready"))
        ta_done, tb_done, pta_ready, ptb_ready = sem("ta_done"), sem("tb_done"), sem("pta_ready"), sem("ptb_ready")
        pv_done, att_evac = sem("pv_done"), sem("att_evac")
        lfr_in, lfs_in, sel_in, cs_ready, cq_ready, sel_ready = (
            sem("lfr_in"), sem("lfs_in"), sem("sel_in"), sem("cs_ready"), sem("cq_ready"), sem("sel_ready"))
        kr_in, vr_in = [sem("kr_in0"), sem("kr_in1")], [sem("vr_in0"), sem("vr_in1")]
        sk_done, kt_ready, kt_new, qbd_zero, qbd_ready, sls_ready = (sem("sk_done"), sem("kt_ready"), sem("kt_new"),
                                                                     sem("qbd_zero"), sem("qbd_ready"), sem("sls_ready"))
        sqk_done, snm, sexp, s_inverse, spn = sem("sqk_done"), sem("snm"), sem("sexp"), sem("s_inverse"), sem("spn")
        spt_done, spt_ready, spv_done, satt = sem("spt_done"), sem("spt_ready"), sem("spv_done"), sem("satt")
        la_sum, la_mean, la_cen, la_sq, la_sum2, la_var, la_sd, la_rs, la_nrm, la_act, la_hi = (
            sem("la_sum"), sem("la_mean"), sem("la_cen"), sem("la_sq"), sem("la_sum2"), sem("la_var"), sem("la_sd"),
            sem("la_rs"), sem("la_nrm"), sem("la_act"), sem("la_hi"))
        m_ready, y_in = sem("m_ready"), [sem(f"y_in{i}") for i in range(KT)]
        ln_part, ln_sum, ln_mean, ln_cen, ln_sq, ln_sum2, ln_var, ln_sd, ln_rs, ln_nrm = (
            sem("ln_part"), sem("ln_sum"), sem("ln_mean"), sem("ln_cen"), sem("ln_sq"), sem("ln_sum2"), sem("ln_var"),
            sem("ln_sd"), sem("ln_rs"), sem("ln_nrm"))
        ln_xf, ln_hi, x_ready, xt_spill = sem("ln_xf"), sem("ln_hi"), sem("x_ready"), sem("xt_spill")
        od_in, od_zero, wm_in, wm_hi, wm_lo = sem("od_in"), sem("od_zero"), sem("wm_in"), sem("wm_hi"), sem("wm_lo")
        cmp_ready, ot_done, ot_free, os_sent, df_ready, dh_ready, dl_ready, mix_done, mix_evac, tap = (
            sem("cmp_ready"), sem("ot_done"), sem("ot_free"), sem("os_sent"), sem("df_ready"), sem("dh_ready"),
            sem("dl_ready"), sem("mix_done"), sem("mix_evac"), sem("tap"))
        oc_done, pool_step, lf_out = sem("oc_done"), sem("pool_step"), sem("lf_out")
        yo_sent, pool_out = [sem("yo_sent0"), sem("yo_sent1"), sem("yo_sent2"), sem("yo_sent3")], sem("pool_out")

        w_ug = t["w_in_even"][0].rearrange("(k p) n -> p k n", p=P)
        w_odd = t["w_in_odd"][0].rearrange("(k p) n -> p k n", p=P)
        w_out = [t[n][0].rearrange("(k p) n -> p k n", p=P) for n in ("w_out_even", "w_out_odd")]
        w_g = [t["w_ffn_gate"][i].rearrange("(k p) n -> p k n", p=P) for i in range(2)]
        w_u = [t["w_ffn_up"][i].rearrange("(k p) n -> p k n", p=P) for i in range(2)]
        w_d = [t["w_ffn_down"][i] for i in range(2)]

        def raw_cols(pos):
            return RAW[:, pos, :].rearrange("p (k m) -> p k m", k=KT)

        def token_pieces(i):
            lo, hi = i * P, min((i + 1) * P, T)
            spans = [(0, META, "meta_tokens"), (META, TP, "x_prompt"), (TP, T, "x_sample")]
            return [(max(lo, a) - lo, min(hi, b) - max(lo, a), n, max(lo, a) - a)
                    for a, b, n in spans if max(lo, a) < min(hi, b)]

        xsrc = {"meta_tokens": t["meta_tokens"], "x_prompt": t["x_prompt"][0],
                "x_sample": t["x_sample"].rearrange("s q d -> (s q) d")}
        xin_count = [16 * sum(len(token_pieces(j)) for j in range(i % XB, i + 1, XB)) for i in range(NTT)]
        tw = [min(P, T - i * P) for i in range(NTT)]
        YPIECES = [[(16, 112), (128, 128), (256, 112)], [(368, 128), (496, 128), (624, 112)],
                   [(736, 128), (864, 128), (992, 48), (1040, 64)]]
        STG_ALL = (6, 6, 4, 4)

        def att_units():
            na = nb = 0
            for a in range(36):
                i = ORDER[(a // 9) % 2][a % 9]
                groups = (i + 4) // 4
                yield a, (a // 9) % 2, a // 18, i, (P if i < 8 else META), min(P * (i + 1), TP), na, nb
                na += 1 + (groups > 2)
                nb += groups > 1

        ATT = list(att_units())
        NA = ATT[-1][6] + 1 + (ATT[-1][3] == 8)
        NB = ATT[-1][7] + (ATT[-1][3] > 3)

        def chunk(c):
            return slice(c * C, (c + 1) * C)

        def ffn_units(f):
            return (ST_FF0, GU_FF0, DN_FF0) if f == 0 else (ST_FF1, GU_FF1, DN_FF1)

        LN_DONE = [[3 + b + 18 + 2 * c + 2 for c in range(NC)] if f is None else
                   [3 + b + 24 * (NG - 1) + 8 * (c + 1) for c in range(NC)]
                   for b, f in ((DN_OUT0, None), (DN_FF0, 0), (DN_OUT1, None), (DN_FF1, 1))]
        block = ctx.enter_context(nc.Block())

        @block.sync
        def _(sp):
            def load(n, pos, src):
                sp.wait_ge(w_lo, n - 3)
                sp.dma_start(raw_cols(pos) if len(src.shape) == 3 else RAW[:, pos, :], src).then_inc(w_loaded[pos], 16)

            def cols(w, m):
                return w[:, :, bass.ds(m * P, P)]

            sp.dma_start(CST[:], t["consts"][:, 0:K_SEL]).then_inc(s_cst, 16)
            for i in range(NTT):
                if i >= XB:
                    sp.wait_ge(t_done, 2 * (i - XB + 1))
                for r, n, name, first in token_pieces(i):
                    sp.dma_start(XIN[r:r + n, i % XB, :], xsrc[name][first:first + n, :]).then_inc(s_xin[i % XB], 16)
                if i in (2, 5):
                    for n in (0, 1) if i == 2 else (2, 3):
                        sp.dma_start(raw_cols(n), cols(w_ug, (1 - n % 2) * HT + n // 2)).then_inc(w_loaded[n], 16)
            for n in range(4, 8):
                load(n, n % 4, cols(w_ug, (1 - n % 2) * HT + n // 2))
            with sp.Fori(0, 3) as it:
                for n in range(4):
                    load(2 * ST_QKV + 4 * it + n, n, cols(w_ug, 4 * it + n + 2 * HT))
            for n in range(4):
                load(2 * ST_OUT0 + n, (2 * ST_OUT0 + n) % 4, w_out[0][:, :, n * P:(n + 1) * P])
            kv = [t[n][0, 0].rearrange("t h d -> t (h d)") for n in ("k_prompt", "v_prompt")]
            kvs = [t[n].rearrange("s a q h d -> (s a q) (h d)") for n in ("k_sample", "v_sample")]
            for i in range(NTT):
                for j in range(2):
                    u = 2 * i + j
                    sp.wait_ge(t_free, 4 + TU_KV + u + 1)
                    if i < 8:
                        sp.dma_start(kv[j][i * P:(i + 1) * P, :], STG[:, u % 4, :]).then_inc(stg_sent[u % 4], 16)
                    else:
                        sp.dma_start(kv[j][i * P:TP, :], STG[0:META, u % 4, :]).then_inc(stg_sent[u % 4], 16)
                        sp.dma_start(kvs[j], STG[META:META + NS * NQ, u % 4, :]).then_inc(stg_sent[u % 4], 16)
            vd = t["v_prompt"][0, 0].rearrange("t h d -> t (h d)")
            for i in range(4):
                sp.wait_ge(stg_sent[i], 16 * STG_ALL[i])
            with sp.Fori(0, 2) as it:
                sp.wait_ge(pv_done, 1 + 36 * it)
                for j in range(2):
                    c = bass.ds((2 * it + j) * P, P)
                    sp.dma_start(VP[:, j, 0:8, :], vd[0:8 * P].rearrange("(b p) n -> p b n", p=P)[:, :, c]).then_inc(vp_ready[j], 16)
                    sp.dma_start(VP[0:META, j, 8, :], vd[8 * P:TP, c]).then_inc(vp_ready[j], 16)
            sp.wait_ge(s_ptb, 16)
            sp.wait_ge(att_evac, 1 + 72)
            vs = t["v_sample"].rearrange("s a q h d -> (s a) q (h d)")

            def pages(s, j, wait):
                rows = [sp.value_load(PTB[0:1, bass.ds(s * NPAGE + g, 1)], min_val=0, max_val=t["cache_k"].shape[0] - 1)
                        for g in range(NPAGE)]
                if wait:
                    sp.wait_ge(sk_done, 4 * s - 4)
                for g, r in enumerate(rows):
                    sp.dma_start(KR[:, j, g, :], t["cache_k"][bass.ds(r, 1)].rearrange("a e p h d -> (a e p) (h d)")).then_inc(kr_in[j], 16)
                if wait:
                    sp.wait_ge(spv_done, s)
                for g, r in enumerate(rows):
                    sp.dma_start(VR[:, j, g, :], t["cache_v"][bass.ds(r, 1)].rearrange("a e p h d -> (a e p) (h d)")).then_inc(vr_in[j], 16)
                sp.dma_start(VR[0:NQ, j, NPAGE, :], vs[bass.ds(s, 1)].rearrange("s q n -> (s q) n")).then_inc(vr_in[j], 16)

            for j in range(2):
                pages(j, j, False)
            with sp.Fori(0, NS // 2 - 1) as it:
                for j in range(2):
                    pages(2 * it + 2 + j, j, True)

            def residual(layer):
                sp.wait_ge(m_ready, 12 * (layer + 1))
                for k in range(KT):
                    sp.dma_start(Y[:, k, :], XT[:, k, :]).then_inc(y_in[k], 16)

            def ffn_weights(f):
                st = ffn_units(f)[0]

                def group(n, g, par):
                    for j in range(2):
                        load(n + 2 * j, (par + 2 * j) % 4, cols(w_g[f], 2 * g + j))
                        load(n + 2 * j + 1, (par + 2 * j + 1) % 4, cols(w_u[f], 2 * g + j))
                    for j in range(2):
                        load(n + 4 + j, (par + j) % 4, w_d[f][bass.ds((2 * g + j) * P, P), :])

                with sp.Fori(0, NG // 2) as it:
                    group(2 * st + 12 * it, 2 * it, 2 * st)
                    group(2 * st + 12 * it + 6, 2 * it + 1, 2 * st + 6)
                group(2 * st + 6 * (NG - 1), NG - 1, 2 * st + 6 * (NG - 1))

            for i in range(TB):
                sp.wait_ge(xt_sent[i], 16 * len(range(i, NTT, TB)))
            residual(0)
            for n in range(4, 8):
                load(2 * ST_OUT0 + n, (2 * ST_OUT0 + n) % 4, w_out[0][:, :, n * P:(n + 1) * P])
            ffn_weights(0)
            for i in range(HT):
                for j, m in enumerate((HT + i, 3 * HT + i, 2 * HT + i, i)):
                    load(2 * ST_ODD + 4 * i + j, (2 * ST_ODD + j) % 4, w_odd[:, :, m * P:(m + 1) * P])
            for n in range(4):
                load(2 * ST_OUT1 + n, (2 * ST_OUT1 + n) % 4, w_out[1][:, :, n * P:(n + 1) * P])
            residual(1)
            for n in range(4, 8):
                load(2 * ST_OUT1 + n, (2 * ST_OUT1 + n) % 4, w_out[1][:, :, n * P:(n + 1) * P])
            ffn_weights(1)

        @block.gpsimd
        def _(gp):
            for r, name, n in ((R_DW, "w_dw_a", CW), (R_BDW, "b_dw_a", 1), (R_LAG, "ln_a_g", 1), (R_LAB, "ln_a_b", 1),
                               (R_SC, "w_sconv", SW), (R_PS, "pool_scale", 1)):
                gp.dma_start(PIN[r:r + n, :], t[name][0] if n > 1 else t[name]).then_inc(s_par, 16)
            for r, name in ((R_MG, "ln_mix_g"), (R_MB, "ln_mix_b"), (R_FG, "ln_ffn_g"), (R_FB, "ln_ffn_b")):
                gp.dma_start(PIN[r:r + 4, :], t[name].rearrange("l (a n) -> (l a) n", a=2)).then_inc(s_par, 16)
            sca = t["state_conv_a"].rearrange("s a e n -> (s a e) n")
            for i in range(2):
                gp.dma_start(SIN[0:4 * HA, i, :], sca[4 * HA * i:4 * HA * (i + 1), :]).then_inc(s_sin, 16)
            gp.dma_start(PTB[:], t["page_table"].rearrange("(a s) g -> a (s g)", a=1)).then_inc(s_ptb, 16)
            with nc.allow_non_contiguous_dma(reason="eight biases, one per partition"):
                gp.dma_start(BF[:, 0:1], t["b_forget"].rearrange("a h -> h a")).then_inc(s_bf, 16)
            gp.dma_start(WFR[:], w_ug[:, :, 5 * HALF:5 * HALF + NH]).then_inc(s_wf, 16)
            gp.memset(AEXT[:, :, 0:HA], 0.0).then_inc(ext_zero, 1)
            gp.dma_start(t["conv_a_sample"][:, 0, 0:HA - NQ, :], t["state_conv_a"][:, 0, NQ:HA, :]).then_inc(pool_out, 16)
            gp.dma_start(t["pool_sample"][:, 0, 0:HP - NQ, :], t["state_pool"][:, 0, NQ:HP, :]).then_inc(pool_out, 16)
            for i in range(NTT):
                gp.wait_ge(xt_copy, 2 * (i + 1))
                gp.dma_start(XT[:, :, i * P:i * P + tw[i]], XTT[:, i % TB, :, 0:tw[i]]).then_inc(xt_sent[i % TB], 16)
            gp.wait_ge(s_ptb, 16)
            with gp.Fori(0, NS) as s:
                for g in range(NPAGE):
                    r = gp.value_load(PTB[0:1, bass.ds(s * NPAGE + g, 1)], min_val=0, max_val=t["cache_logf"].shape[0] - 1)
                    gp.dma_start(LFR[:, g, bass.ds(s, 1), :].rearrange("p a h -> p (a h)"),
                                 t["cache_logf"][bass.ds(r, 1)].rearrange("a e p h -> (a e p) h")).then_inc(lfr_in, 16)
            gp.wait_ge(gu_free, 2 + GU_QKV)
            for k in range(HT):
                gp.tensor_copy(ACMP[:, k, :, :], sample_cols(AEXT, HA, k)).then_inc(acmp_ready, 1)
            gp.wait_ge(t_free, 4 + TU_A + 1)
            gp.dma_start(t["conv_a_prompt"][0, 0], STA[:]).then_inc(sta_sent, 16)
            gp.wait_ge(t_free, 4 + TU_A + 2)
            for s in range(NS):
                gp.dma_start(t["conv_a_sample"][s, 0, HA - NQ:HA, :], STB[s * NQ:(s + 1) * NQ, :]).then_inc(sta_sent, 16)
            k, acc, tmp, steps = HT - 1, HF[:].rearrange("p b n -> p (b n)"), S[:].rearrange("p b n -> p (b n)"), [0]

            def pool_op(ins):
                steps[0] += 1
                ins.then_inc(pool_step, 1)
                gp.wait_ge(pool_step, steps[0])

            for lo, hi in ((0, TP // 2), (TP // 2, TP)):
                m = hi - lo
                pieces = [(acc[:, 0:m], tmp[:, 0:m], lambda j: prompt_cols(AEXT, HA, k, lo, hi, HA - j))]
                if hi == TP:
                    pieces.append((by_seq(acc[:, m:m + NS * NQ]), by_seq(tmp[:, m:m + NS * NQ]), lambda j: sample_cols(AEXT, HA, k, HA - j)))
                for j in range(CW):
                    for out, part, src in pieces:
                        if j == 0:
                            pool_op(gp.tensor_scalar(out, src(j), row(k, R_DW), row(k, R_BDW), ALU.mult, ALU.add))
                        else:
                            pool_op(gp.tensor_scalar(part, src(j), row(k, R_DW + j), 1.0, ALU.mult, ALU.mult))
                            pool_op(gp.tensor_tensor(out, out, part, ALU.add))
                n = m + (NS * NQ if hi == TP else 0)
                pool_op(gp.tensor_copy(AEXT[:, k, lo:lo + n], acc[:, 0:n]))
            gp.wait_ge(kb_sent, 96)
            gp.wait_ge(lfd_sent, 16)
            for i in range(4):
                gp.wait_ge(stg_sent[i], 16 * STG_ALL[i])
            gp.sem_inc(ab_open, 1)

            with gp.Fori(0, 2) as it:
                for a, h2, j, i, m, n, _, _ in ATT:
                    gp.wait_ge(rc_ready, 36 * it + a + 1)
                    gp.nop(nofuse=True)
                    gp.tensor_scalar(PB[0:m, a % 3, 0:n], PB[0:m, a % 3, 0:n], ST4[0:m, 2, a:a + 1], 1.0,
                                     ALU.mult, ALU.mult).then_inc(pn_ready, 1)
            gp.wait_ge(att_evac, 1 + 72)
            gp.wait_ge(lf_out, 16 * 3)
            gp.dma_start(SELC[:].rearrange("p s h q -> p (s h q)"), t["consts"][:, K_SEL:K_ALL]).then_inc(sel_in, 16)
            gp.dma_start(LFS[:, PAST:KS], LFD).then_inc(lfs_in, 16)
            gp.memset(QBD[:], 0.0).then_inc(qbd_zero, 1)
            gp.wait_ge(qbd_zero, 1)
            gp.memset(KBS[64:128, :], 1.0).then_inc(qbd_zero, 1)
            gp.wait_ge(qbd_zero, 2)
            gp.wait_ge(sel_ready, 1)
            gp.wait_ge(conv_done, HT - 1)
            assert NC == NS // 2 - 1

            def new_keys(s, j):
                gp.tensor_copy(SLS[:, j, :], SELC[:, bass.ds(s, 1), :, :].rearrange("p a h q -> p (a h q)")).then_inc(sls_ready, 1)
                gp.tensor_copy(KTS[:, j, :, PAST:KS], QKV[:, HT:2 * HT, bass.ds(TP + s * NQ, NQ)]).then_inc(kt_new, 1)

            for j in range(2):
                new_keys(j, j)
            with gp.Fori(0, NC) as it:
                cc = bass.ds(it * C, C)
                gp.wait_ge(la_var, it + 1)
                gp.tensor_tensor(YSA[:], AEXT[:, 0:2, cc], AEXT[:, 2:4, cc], ALU.add).then_inc(la_sum, 1)
                gp.wait_ge(sqk_done, 2 * it + 1)
                new_keys(2 * it + 2, 0)
                gp.wait_ge(la_mean, it + 1)
                gp.wait_ge(la_sq, 2 * it + 2)
                gp.tensor_tensor(YSA[:], SQA[:, 0:2, :], SQA[:, 2:4, :], ALU.add).then_inc(la_sum2, 1)
                gp.wait_ge(sqk_done, 2 * it + 2)
                new_keys(2 * it + 3, 1)

            parts = [0]

            def partial(ins):
                parts[0] += 1
                ins.then_inc(ln_part, 1)
                gp.wait_ge(ln_part, parts[0])

            def mean_sums(ln, c):
                cc, k = chunk(c), 3 * ln + c
                gp.wait_ge(d_free, LN_DONE[ln][c])
                if k:
                    gp.wait_ge(ln_mean, k)
                partial(gp.tensor_tensor(YSM[:], Y[:, 0:2, cc], Y[:, 2:4, cc], ALU.add))
                partial(gp.tensor_tensor(YSM[:], YSM[:], Y[:, 4:6, cc], ALU.add))
                gp.tensor_tensor(YSM[:], YSM[:], Y[:, 6:8, cc], ALU.add).then_inc(ln_sum, 1)

            def square_sums(ln, c):
                k = 3 * ln + c
                if k:
                    gp.wait_ge(ln_var, k)
                gp.wait_ge(ln_sq, 4 * k + 2)
                partial(gp.tensor_tensor(YSV[:], SQ[:, 0:2, :], SQ[:, 2:4, :], ALU.add))
                gp.wait_ge(ln_sq, 4 * k + 4)
                partial(gp.tensor_tensor(YSV[:], YSV[:], SQ[:, 4:6, :], ALU.add))
                gp.tensor_tensor(YSV[:], YSV[:], SQ[:, 6:8, :], ALU.add).then_inc(ln_sum2, 1)

            def spill(c):
                gp.wait_ge(ln_xf, 4 * (3 + c) + 4)
                gp.dma_start(XT[:, :, chunk(c)], Y[:, :, chunk(c)]).then_inc(xt_spill, 16)

            def layer_norm(ln, after=lambda c: None):
                mean_sums(ln, 0)
                mean_sums(ln, 1)
                square_sums(ln, 0)
                square_sums(ln, 1)
                mean_sums(ln, 2)
                after(0)
                square_sums(ln, 2)
                after(1)
                after(2)

            layer_norm(0)
            layer_norm(1, spill)
            gp.wait_ge(xt_spill, 48)
            gp.wait_ge(x_ready, 24)
            gp.dma_start(OSB[:], t["state_sconv"].rearrange("s a e n -> (s a e) n")).then_inc(od_in, 16)
            gp.dma_start(OSA[0:NS * HP, :], t["state_pool"].rearrange("s a e n -> (s a e) n")).then_inc(od_in, 16)
            gp.dma_start(WMR[:], t["w_pool_mix"][0].rearrange("g c d -> c g d")).then_inc(wm_in, 16)
            gp.memset(YEXT[:, :, 0:HS], 0.0).then_inc(od_zero, 1)
            gp.memset(PEXT[:, :, 0:HP], 0.0).then_inc(od_zero, 1)
            gp.wait_ge(ot_free, 1 + HT)
            gp.dma_start(t["sconv_prompt"][0, 0], OSA[64:64 + HS, :]).then_inc(os_sent, 16)
            gp.dma_start(t["pool_prompt"][0, 0], OSA[96:96 + HP, :]).then_inc(os_sent, 16)
            gp.dma_start(t["sconv_sample"].rearrange("s a e n -> (s a e) n"), OSB[:]).then_inc(os_sent, 16)
            for s in range(NS):
                gp.dma_start(t["pool_sample"][s, 0, HP - NQ:HP, :], OSA[s * NQ:(s + 1) * NQ, :]).then_inc(os_sent, 16)
            gp.wait_ge(os_sent, 16 * (3 + NS))
            layer_norm(2)

            def store_y(c):
                n = sum(len(YPIECES[x]) for x in range(c))
                for a, w in YPIECES[c]:
                    gp.wait_ge(t_free, 4 + TU_Y + 2 * (n + 1))
                    dst = t["y_prompt"][0, a - META:a - META + w, :] if a < TP else t["y_sample"].rearrange("s q d -> (s q) d")
                    gp.dma_start(dst, YO[0:w, n % 4, :]).then_inc(yo_sent[n % 4], 16)
                    n += 1

            layer_norm(3, store_y)
            for i in range(4):
                gp.wait_ge(yo_sent[i], 16 * len(range(i, sum(map(len, YPIECES)), 4)))
            gp.wait_ge(sta_sent, 16 * (1 + NS))
            gp.wait_ge(pool_out, 16 * 2)
            gp.wait_ge(lf_out, 16 * 3)

        @block.tensor
        def _(pe):
            pe.sem_inc(pv_done, 1)
            pe.sem_inc(spv_done, 1)
            pe.sem_inc(la_var, 1)

            def mm3(out, wh, wl, xh, xl, first, last):
                pe.matmul(out, wh, xh, start=first, stop=False)
                pe.matmul(out, wh, xl, start=False, stop=False)
                return pe.matmul(out, wl, xh, start=False, stop=last)

            def transposes(u, bank, pieces):
                pe.wait_ge(t_free, u + 1)
                for out, src, idn in pieces:
                    m = pe.transpose(out, src, idn)
                m.then_inc(t_done, 1)

            def gu_stage(stage, pos, unit, par, before=None):
                pe.wait_ge(w_lo, 2 * stage + 2)
                for c in range(NC):
                    if before:
                        before(c)
                    pe.wait_ge(gu_free, unit + c + 1)
                    for w in range(2):
                        out = PS[:, 2 * ((par + c) % 2) + w, 0:C]
                        for k in range(KT):
                            ks = slice(k * P, (k + 1) * P)
                            m = mm3(out, WHI[:, pos + w, ks], WLO[:, pos + w, ks], AH[:, k, chunk(c)], AL[:, k, chunk(c)],
                                    k == 0, k == KT - 1)
                    m.then_inc(gu_done, 1)

            def norm_product(ones, ys, s_in, s_res, k, bank=7):
                pe.wait_ge(s_in, k + 1)
                pe.matmul(PS[:, bank, 0:C], ones, ys[:, 0, :], start=True, stop=False)
                pe.matmul(PS[:, bank, 0:C], ones, ys[:, 1, :], start=False, stop=True).then_inc(s_res, 1)

            def mean(ln, c):
                k = 3 * ln + c
                if k and c != 1:
                    pe.wait_ge(ln_sd, k)
                norm_product(ONES_D, YSM, ln_sum, ln_mean, k, MEAN_BANK[c])

            def variance(ln, c):
                k = 3 * ln + c
                if c == 1:
                    pe.wait_ge(ln_sd, k)
                norm_product(ONES_D, YSV, ln_sum2, ln_var, k)

            def gu_unit(pos, unit, par, c):
                pe.wait_ge(gu_free, unit + 1)
                for w in range(2):
                    for k in range(KT):
                        ks = slice(k * P, (k + 1) * P)
                        m = mm3(PS[:, 2 * par + w, 0:C], WHI[:, pos + w, ks], WLO[:, pos + w, ks], AH[:, k, chunk(c)], AL[:, k, chunk(c)],
                                k == 0, k == KT - 1)
                m.then_inc(gu_done, 1)

            def gu_stage(stage, pos, unit, par, before=None):
                pe.wait_ge(w_lo, 2 * stage + 2)
                for c in range(NC):
                    if before:
                        before(c)
                    gu_unit(pos, unit + c, (par + c) % 2, c)

            def head(ln, st, unit):
                mean(ln, 1)
                variance(ln, 0)
                variance(ln, 1)
                for c in range(NC):
                    pe.wait_ge(x_ready, 12 * ln + 4 * (c + 1))
                    for j in range(2):
                        pe.wait_ge(w_lo, 2 * (st + j) + 2)
                        gu_unit(2 * (st + j) % 4, unit + 2 * c + j, j, c)
                        if j == 0 and c == 0:
                            mean(ln, 2)
                        if j == 0 and c == 1:
                            variance(ln, 2)

            pe.wait_ge(s_cst, 16)
            def x_turn(i):
                pe.wait_ge(s_xin[i % XB], xin_count[i])
                for h in range(2):
                    u = 2 * i + h
                    transposes(u, 4 + u % 4, [(PS[:, 4 + u % 4, P * j:P * j + tw[i]], XIN[0:tw[i], i % XB, (4 * h + j) * P:(4 * h + j + 1) * P],
                                               IDN[0:tw[i], 0:tw[i]]) for j in range(4)])

            for c in range(NC):
                for i in range(3 * c, 3 * c + 3):
                    x_turn(i)
                if c == 0:
                    pe.wait_ge(w_lo, 2)
                pe.wait_ge(t_free, 4 + 6 * (c + 1))
                gu_unit(0, c, c % 2, c)
            pe.wait_ge(s_par, 160)
            u = TU_PAR
            transposes(u, 4 + u % 4, [(PS[:, 4 + u % 4, R_ALL * j:R_ALL * (j + 1)], PIN[:, j * P:(j + 1) * P], IDN[0:R_ALL, 0:R_ALL])
                                      for j in range(HT)])
            pe.wait_ge(s_sin, 32)
            for i in range(2):
                u, n = TU_SA + i, 4 * HA
                transposes(u, 4 + u % 4, [(PS[:, 4 + u % 4, n * j:n * (j + 1)], SIN[0:n, i, j * P:(j + 1) * P], IDN[0:n, 0:n])
                                          for j in range(HT)])
            for k in range(1, HT):
                gu_stage(k, 2 * k % 4, 3 * k, 3 * k)
            pe.wait_ge(gu_free, 2 + GU_QKV)
            u = TU_A
            transposes(u, 4 + u % 4, [(PS[0:HA, 4 + u % 4, k * P:(k + 1) * P], AEXT[:, k, TP:HA + TP], IDN) for k in range(HT)])
            pe.wait_ge(acmp_ready, HT)
            u = TU_A + 1
            transposes(u, 4 + u % 4, [(PS[0:NS * NQ, 4 + u % 4, k * P:(k + 1) * P], ACMP[:, k, :, :].rearrange("p s e -> p (s e)"), IDN)
                                      for k in range(HT)])
            with pe.Fori(0, 3) as it:
                for j in range(2):
                    gu_stage(ST_QKV + 2 * it + j, 2 * j, GU_QKV + 6 * it + 3 * j, 3 * j)
            pe.wait_ge(wf_lo, 1)
            pe.wait_ge(t_free, 4 + TU_KV)
            for c in range(NC):
                for k in range(KT):
                    m = mm3(PS[0:NH, 4 + c, 0:C], WFH[:, k, :], WFL[:, k, :], AH[:, k, chunk(c)], AL[:, k, chunk(c)], k == 0, k == KT - 1)
                m.then_inc(f_done, 1)
            pe.wait_ge(gu_free, 2 + GU_FF0)
            pe.wait_ge(f_act, NC)
            for i in range(NTT):
                for j in range(2):
                    u = TU_KV + 2 * i + j
                    transposes(u, 4 + u % 4, [(PS[0:tw[i], 4 + u % 4, k * P:(k + 1) * P], QKV[:, HT * (1 + j) + k, i * P:i * P + tw[i]], IDN)
                                              for k in range(HT)])
            pe.wait_ge(lf_ready, 1)
            u = TU_LF
            transposes(u, 4 + u % 4, [(PS[0:tw[i], 4 + u % 4, NH * i:NH * (i + 1)], LFZ[:, 2, i * P:i * P + tw[i]], IDN[0:NH, 0:NH])
                                      for i in range(NTT)])

            pe.wait_ge(t_free, 4 + TU_LF + 1)
            pe.wait_ge(idr_ready, 2)

            def scores(it, a, h2, j, i, m, n, na, nb):
                if a % 9 == 0:
                    pe.wait_ge(qk_hi, 16 * it + 4 * (a // 9) + 4)
                    pe.wait_ge(qk_lo, 12 * it + 3 * (a // 9) + 3)
                pe.wait_ge(exp_done, 36 * it + a + 1)
                if i == 8:
                    pe.nop(nofuse=True)
                base, ms = (0, 3)[a % 2], slice(i * P, i * P + m)
                for b in range((n + 511) // 512):
                    lo, hi = 512 * b, min(n, 512 * (b + 1))
                    diag = i * P >= lo and i * P < hi
                    out = PS[0:m, base + b, 0:hi - lo]
                    pe.matmul(out, QS1[:, h2, ms], KS1[:, h2, lo:hi], start=True, stop=False)
                    if diag:
                        pe.matmul(PS[0:m, base + b, i * P - lo:i * P - lo + m], IDR[:, 0:m], MKR[:, 0:m], start=False, stop=False,
                                  skip_group_check=True)
                    mm = pe.matmul(out, QS2[:, h2, ms], KS2[:, h2, lo:hi], start=False, stop=True)
                mm.then_inc(qk_done, 1)

            def turn(it, a, h2, j, i, m, n, na, nb):
                pe.wait_ge(pn_ready, 36 * it + a + 1)
                for g in range((i + 4) // 4):
                    if g == 1:
                        pe.wait_ge(ptb_ready, NB * it + nb + 1)
                    else:
                        pe.wait_ge(pta_ready, NA * it + na + g // 2 + 1)
                    if i == 8:
                        pe.nop(nofuse=True)
                    for jt in range(4 * g, min(4 * g + 4, i + 1)):
                        kw = min(P, TP - jt * P)
                        mm = pe.transpose(PS[0:kw, 5 + g % 2, (jt - 4 * g) * P:(jt - 4 * g) * P + m], PB[0:m, a % 3, jt * P:jt * P + kw],
                                          IDN[0:m, 0:m])
                    mm.then_inc(tb_done if g == 1 else ta_done, 1)

            def values(it, a, h2, j, i, m, n, na, nb):
                if a % 18 == 0:
                    pe.wait_ge(vp_ready[j], 32 * it + 32)
                pe.wait_ge(pta_ready, NA * it + na + (2 if i == 8 else 1) + 1)
                if i > 3:
                    pe.wait_ge(ptb_ready, NB * it + nb + 2)
                pe.wait_ge(att_evac, 36 * it + a + 1)
                for jt in range(i + 1):
                    kw = min(P, TP - jt * P)
                    mm = pe.matmul(PS[0:HD, 7, 0:m], VP[0:kw, j, jt, HD * h2:HD * (h2 + 1)], PT[0:kw, a % 2, jt, 0:m],
                                   start=(jt == 0), stop=(jt == i))
                mm.then_inc(pv_done, 1)

            with pe.Fori(0, 2) as it:
                for n in range(36 + 3):
                    if n < 36:
                        scores(it, *ATT[n])
                    if 2 <= n < 38:
                        turn(it, *ATT[n - 2])
                    if n >= 3:
                        values(it, *ATT[n - 3])

            pe.wait_ge(att_evac, 1 + 72)
            pe.wait_ge(lfr_in, 16 * NS * NPAGE)
            u = TU_LFS
            transposes(u, 6, [(PS[0:64, 6, g * P:(g + 1) * P], LFR[:, g, :, :].rearrange("p s h -> p (s h)"), IDN) for g in range(NPAGE)])
            pe.wait_ge(t_free, 4 + TU_LFS + 1)
            pe.wait_ge(qbd_zero, 2)

            def turn_keys(s, j, loads):
                pe.wait_ge(kr_in[j], 64 * loads)
                for c in range(HT):
                    pe.wait_ge(kt_ready, 4 * s + c + 1)
                    for g in range(NPAGE):
                        mm = pe.transpose(PS[:, c, g * P:(g + 1) * P], KR[:, j, g, c * P:(c + 1) * P], IDN)
                    mm.then_inc(sk_done, 1)

            def sample_scores(s, j):
                pe.wait_ge(kt_ready, 4 * s + 8)
                pe.wait_ge(kt_new, s + 1)
                pe.wait_ge(qbd_ready, 2 * s + 2)
                pe.wait_ge(sls_ready, s + 1)
                pe.wait_ge(sexp, s + 1)
                for b, lo, hi in ((4, 0, PAST), (5, PAST, KS)):
                    out = PS[0:64, b, 0:hi - lo]
                    for c in range(HT):
                        pe.matmul(out, QBD[:, j, 64 * c:64 * c + 64], KTS[:, j, c, lo:hi], start=(c == 0), stop=False)
                    mm = pe.matmul(out, SLS[:, j, :], KBS[:, lo:hi], start=False, stop=(b == 4))
                mm = pe.matmul(PS[0:64, 5, 0:NQ], IDN[0:64, 0:64], CST[0:64, K_MS:K_MS + NQ], start=False, stop=True)
                mm.then_inc(sqk_done, 1)

            def sample_values(s, j, loads):
                pe.wait_ge(spn, s + 1)
                pe.wait_ge(satt, s + 1)
                pe.nop(nofuse=True)
                for g in range(NPAGE + 1):
                    kw = P if g < NPAGE else NQ
                    mm = pe.transpose(PS[0:kw, 6, 64 * g:64 * g + 64], PSA[:, j, g * P:g * P + kw], IDN[0:64, 0:64])
                mm.then_inc(spt_done, 1)
                pe.wait_ge(spt_ready, s + 2)
                pe.wait_ge(vr_in[j], 80 * loads)
                for c in range(HT):
                    for g in range(NPAGE + 1):
                        kw = P if g < NPAGE else NQ
                        mm = pe.matmul(PS[:, 6, PV0 + 16 * c:PV0 + 16 * c + 16], VR[0:kw, j, g, c * P:(c + 1) * P], PTS[0:kw, j, g, 16 * c:16 * c + 16],
                                       start=(g == 0), stop=(g == NPAGE))
                mm.then_inc(spv_done, 1)

            turn_keys(0, 0, 1)
            sample_scores(0, 0)
            def sequence(s, j, it, beside=lambda: None):
                turn_keys(s + 1, 1 - j, it + 1 + j)
                sample_values(s, j, it + 1)
                beside()
                sample_scores(s + 1, 1 - j)

            with pe.Fori(0, NC) as it:
                sequence(2 * it, 0, it, lambda: norm_product(ONES_H, YSA, la_sum, la_mean, it))
                sequence(2 * it + 1, 1, it, lambda: norm_product(ONES_H, YSA, la_sum2, la_var, it))
            sequence(NS - 2, 0, NS // 2 - 1)
            sample_values(NS - 1, 1, NS // 2)

            def out_product(layer, st, dn):
                for q in range(4):
                    pos = 2 * (st + q) % 4
                    pe.wait_ge(w_lo, 2 * (st + q) + 2)
                    for c in range(NC):
                        pe.wait_ge(m_ready, 12 * layer + 4 * (c + 1))
                        if q == 3 and c == 2:
                            mean(2 * layer, 0)
                        for w in range(2):
                            n = 6 * q + 2 * c + w
                            pe.wait_ge(d_free, dn + n + 1)
                            for k in range(KT):
                                ks = slice(k * P, (k + 1) * P)
                                m = mm3(PS[:, 4 + n % 3, 0:C], WHI[:, pos + w, ks], WLO[:, pos + w, ks], AH[:, k, chunk(c)],
                                        AL[:, k, chunk(c)], k == 0, k == KT - 1)
                            m.then_inc(d_done, 1)

            def ffn(f):
                st, gu, dn = ffn_units(f)

                def h_need(g, c):
                    return 2 * c + 2 if isinstance(g, int) and g == 0 else 6 * g + 3 + c + 1

                def down(g, par, last=False):
                    pos = 2 * (st + 3 * par + 2) % 4
                    pe.wait_ge(w_lo, 2 * (st + 3 * g) + 6)
                    for c in range(NC):
                        if last and c == 2:
                            mean(2 * f + 1, 0)
                        pe.wait_ge(h_ready, 66 * f + h_need(g, c))
                        for o in range(KT):
                            n = 8 * c + o
                            pe.wait_ge(d_free, dn + 24 * g + n + 1)
                            for w in range(2):
                                os = slice(o * P, (o + 1) * P)
                                m = mm3(PS[:, 4 + n % 3, 0:C], WHI[:, pos + w, os], WLO[:, pos + w, os], HH[:, w, chunk(c)], HL[:, w, chunk(c)],
                                        w == 0, w == 1)
                            m.then_inc(d_done, 1)

                def group(g, par, last=False):
                    for j in range(2):
                        gu_stage(st + 3 * g + j, 2 * (st + 3 * par + j) % 4, gu + 6 * g + 3 * j, 3 * j)
                    down(g, par, last)

                head(2 * f, st, gu)
                down(0, 0)
                with pe.Fori(0, NG // 2 - 1) as it:
                    group(2 * it + 1, 1)
                    group(2 * it + 2, 0)
                group(NG - 2, 1)
                group(NG - 1, 0, last=True)

            out_product(0, ST_OUT0, DN_OUT0)
            ffn(0)
            def mix(i):
                pe.wait_ge(gu_free, 2 + GU_ODD + 6 * (i + 1))
                pe.wait_ge(cmp_ready, i + 1)
                pe.wait_ge(ot_free, i + 1)
                pe.transpose(PS[0:NS * NQ, 7, 0:P], CMP[:, NS * HS:], IDN)
                pe.transpose(PS[0:HS, 7, P:2 * P], prompt_cols(YEXT, HS, i, TP - HS, TP), IDN)
                pe.transpose(PS[0:HP, 7, 2 * P:3 * P], prompt_cols(PEXT, HP, i, TP - HP, TP), IDN)
                pe.transpose(PS[0:NS * HS, 7, 3 * P:4 * P], CMP[:, 0:NS * HS], IDN).then_inc(ot_done, 1)
                pe.wait_ge(dl_ready, i + 1)
                for c in range(NC):
                    pe.wait_ge(mix_evac, 3 * i + c + 1)
                    mm3(PS[:, 4 + c, 0:C], WMH[:, i, :], WML[:, i, :], DH[:, chunk(c)], DL[:, chunk(c)], True, True).then_inc(mix_done, 1)

            for i in range(HT):
                if i:
                    gu_stage(ST_ODD + 2 * i, 2 * ST_ODD % 4, GU_ODD + 6 * i, 0)
                else:
                    head(1, ST_ODD, GU_ODD)
                    pe.wait_ge(ln_sd, 6)
                    pe.wait_ge(d_free, 3 + DN_OUT1)
                    pe.wait_ge(od_in, 32)
                    transposes(TU_ST, 7, [(PS[:, 7, NS * HS * k:NS * HS * (k + 1)], OSB[:, k * P:(k + 1) * P], IDN[0:NS * HS, 0:NS * HS])
                                          for k in range(HT)])
                    n = NS * HP
                    transposes(TU_ST + 1, 4, [(PS[:, 4, n * k:n * (k + 1)], OSA[0:n, k * P:(k + 1) * P], IDN[0:n, 0:n])
                                              for k in range(HT)])
                    pe.wait_ge(wm_lo, 1)
                    pe.wait_ge(t_free, 4 + TU_ST + 2)
                if i:
                    mix(i - 1)
                    gu_stage(ST_ODD + 2 * i + 1, (2 * ST_ODD + 2) % 4, GU_ODD + 6 * i + 3, 1)
            mix(HT - 1)
            pe.wait_ge(mix_evac, 3 + 3 * HT)
            out_product(1, ST_OUT1, DN_OUT1)
            ffn(1)
            pe.wait_ge(gu_free, 2 + GU_FF1 + 6 * NG)
            u = TU_Y
            mean(3, 1)
            variance(3, 0)
            variance(3, 1)
            for c in range(NC):
                pe.wait_ge(ln_xf, 4 * (9 + c) + 4)
                for a, w in YPIECES[c]:
                    for h in range(2):
                        transposes(u, (u - TU_Y) % 4, [(PS[0:w, (u - TU_Y) % 4, k * P:(k + 1) * P], Y[:, 4 * h + k, a:a + w], IDN)
                                                       for k in range(4)])
                        u += 1
                if c == 0:
                    mean(3, 2)
                if c == 1:
                    variance(3, 2)

        @block.scalar
        def _(act):
            act.sem_inc(exp_done, 2)
            act.sem_inc(ptb_ready, 1)
            act.sem_inc(att_evac, 1)
            act.sem_inc(kt_ready, 4)
            act.sem_inc(sexp, 1)
            act.sem_inc(spt_ready, 1)
            act.sem_inc(satt, 1)
            act.sem_inc(mix_evac, 3)

            def split(stage, pos):
                for j in range(2):
                    n = 2 * stage + j
                    act.wait_ge(w_loaded[pos + j], 16 * (n // 4 + 1))
                    act.copy(WHI[:, pos + j, :], RAW[:, pos + j, :]).then_inc(w_hi, 1)

            def x_tile(i):
                for h in range(2):
                    u = 2 * i + h
                    act.wait_ge(t_done, u + 1)
                    src = PS[:, 4 + u % 4, :].rearrange("p (k n) -> p k n", k=4)[:, :, 0:tw[i]]
                    act.copy(AH[:, 4 * h:4 * h + 4, i * P:i * P + tw[i]], src)
                    if i >= TB:
                        act.wait_ge(xt_sent[i % TB], 16 * (i // TB))
                    act.copy(XTT[:, i % TB, 4 * h:4 * h + 4, 0:tw[i]], src).then_inc(xt_copy, 1)

            def gated(unit, par, func, s_tile, bank0_to=None):
                act.wait_ge(gu_done, unit + 1)
                act.activation(s_tile[:, par, :] if bank0_to is None else bank0_to, PS[:, 2 * par, 0:C], func).then_inc(s_ready, 1)

            for c in range(NC):
                for i in range(3 * c, 3 * c + 3):
                    x_tile(i)
                if c != 1:
                    split(c // 2, c)
                gated(c, c % 2, ACT.Sigmoid, S)
            for k in range(1, HT):
                split(k + 1, 2 * (k + 1) % 4)
                for c in range(NC):
                    gated(3 * k + c, (3 * k + c) % 2, ACT.Sigmoid, S)
            act.wait_ge(s_wf, 16)
            act.copy(WFH[:], WFR[:]).then_inc(wf_hi, 1)
            for i in range(TB):
                act.wait_ge(xt_sent[i], 16 * len(range(i, NTT, TB)))
            act.wait_ge(t_free, 4 + TU_A)
            for it in range(3):
                for j in range(2):
                    st = ST_QKV + 2 * it + j
                    split(st + 1, 2 * (1 - j))
                    for c in range(NC):
                        gated(GU_QKV + 6 * it + 3 * j + c, (3 * j + c) % 2, ACT.Copy, S, QKV[:, 4 * it + 2 * j, chunk(c)])
            act.wait_ge(f_done, NC)
            act.wait_ge(s_bf, 16)
            for c in range(NC):
                act.activation(LFZ[:, 0, chunk(c)], PS[0:NH, 4 + c, 0:C], ACT.Identity, bias=BF[:, 0:1]).then_inc(f_act, 1)
            act.wait_ge(f_act, NC)
            act.activation(LFZ[:, 1, :], LFZ[:, 0, :], ACT.Abs).then_inc(f_act, 1)
            act.wait_ge(f_act, NC + 1)
            act.activation(LFZ[:, 1, :], LFZ[:, 1, :], ACT.Exp, scale=-1.0).then_inc(f_act, 1)
            act.wait_ge(f_act, NC + 2)
            act.activation(LFZ[:, 1, :], LFZ[:, 1, :], ACT.Ln, bias=1.0).then_inc(f_act, 1)
            act.wait_ge(c_ready, 1)
            act.copy(LCH[:], LFC[:]).then_inc(c_hi, 1)
            act.wait_ge(kb_fill, 2)
            act.wait_ge(c_lo, 1)
            for j in range(2):
                act.dma_start(KS2[64:72, j, :].bitcast(F32), LCH[:].bitcast(F32)).then_inc(kb_sent, 16)
                act.dma_start(KS2[72:80, j, :].bitcast(F32), LCL[:].bitcast(F32)).then_inc(kb_sent, 16)
            act.dma_start(QBA[16:24, :], LCH[:].bitcast(F32)).then_inc(kb_sent, 16)
            act.dma_start(QBA[24:32, :], LCL[:].bitcast(F32)).then_inc(kb_sent, 16)
            act.dma_start(LFD.rearrange("(s h) q -> h s q", s=NS), LFZ[:, 2, TP:T].rearrange("p (s e) -> p s e", s=NS)).then_inc(lfd_sent, 16)
            act.wait_ge(t_free, 4 + TU_LF + 1)
            act.dma_start(t["logf_prompt"][0, 0, 0:8 * P].rearrange("(b p) h -> p b h", p=P), LFO[:, 0:8, :]).then_inc(lf_out, 16)
            act.dma_start(t["logf_prompt"][0, 0, 8 * P:TP], LFO[0:META, 8, :]).then_inc(lf_out, 16)
            act.dma_start(t["logf_sample"].rearrange("s a q h -> (s a q) h"), LFO[META:META + NS * NQ, 8, :]).then_inc(lf_out, 16)

            act.copy(IDR[:], IDN).then_inc(idr_ready, 1)
            act.copy(MKR[:], CST[:, K_MASK:K_MASK + P]).then_inc(idr_ready, 1)
            act.wait_ge(ab_open, 1)

            def expo(it, a, h2, j, i, m, n, na, nb):
                base = (0, 3)[a % 2]
                act.wait_ge(nm_ready, 36 * it + a + 1)
                src = PS[0:m, base:base + (n + 511) // 512, :].rearrange("p b n -> p (b n)")[:, 0:n]
                act.activation(PB[0:m, a % 3, 0:n], src, ACT.Exp, bias=ST4[0:m, 0, a:a + 1],
                               accum_out=ST4[0:m, 1, a:a + 1]).then_inc(exp_done, 1)

            def turned(it, a, h2, j, i, m, n, na, nb):
                if i > 3:
                    act.wait_ge(tb_done, NB * it + nb + 1)
                    w = min(i + 1, 8) - 4
                    act.copy(PT[:, a % 2, 4:4 + w, 0:m], PS[:, 6, :].rearrange("p (k n) -> p k n", k=4)[:, 0:w, 0:m]).then_inc(ptb_ready, 1)

            def result(it, a, h2, j, i, m, n, na, nb):
                act.wait_ge(pv_done, 36 * it + a + 2)
                act.nop(nofuse=True)
                act.activation(QKV[HD * h2:HD * (h2 + 1), bass.ds(2 * it + j, 1), i * P:i * P + m].rearrange("p a n -> p (a n)"),
                               PS[0:HD, 7, 0:m], ACT.Copy).then_inc(att_evac, 1)

            def head_high(it, x, part):
                h2 = x % 2
                if x >= 2 and part == 0:
                    act.wait_ge(qk_done, 36 * it + 9 * (x - 1))
                    act.nop(nofuse=True)
                own, other = slice(HD * h2, HD * (h2 + 1)), slice(HD * (1 - h2), HD * (2 - h2))
                tile, out, scale = ((HT, KS1[own, h2, :], 1.0), (0, QS1[own, h2, :], HD ** -0.5), (HT, KS1[other, h2, :], 1.0),
                                    (0, QS2[0:HD, h2, :], HD ** -0.5))[part]
                src = QKV[own, bass.ds(2 * it + x // 2 + tile, 1), 0:TP].rearrange("p a n -> p (a n)")
                act.activation(out, src, ACT.Copy, scale=scale).then_inc(qk_hi, 1)

            with act.Fori(0, 2) as it:
                act.wait_ge(pv_done, 1 + 36 * it)
                act.nop(nofuse=True)
                for part in range(4):
                    head_high(it, 0, part)
                for n in range(36 + 3):
                    if n < 36:
                        expo(it, *ATT[n])
                    if 2 <= n < 38:
                        turned(it, *ATT[n - 2])
                    if n >= 3:
                        result(it, *ATT[n - 3])
                    if n < 27 and n % 9 in (2, 3, 4, 5):
                        head_high(it, n // 9 + 1, n % 9 - 2)

            act.wait_ge(cs_ready, 1)
            act.copy(CQ2[64:128, :], KBS[0:64, PAST:KS]).then_inc(cq_ready, 1)
            act.wait_ge(qbd_zero, 1)

            def queries(s, j):
                act.nop(nofuse=True)
                for h2 in range(2):
                    dst = QBD[HD * h2:HD * (h2 + 1), j, 8 * h2:8 * h2 + 320].rearrange("p (c x) -> p c x", x=80)[:, :, 0:NQ]
                    act.mul(dst, QKV[HD * h2:HD * (h2 + 1), 0:HT, bass.ds(TP + s * NQ, NQ)], HD ** -0.5).then_inc(qbd_ready, 1)

            def keys(s, j, cs):
                for c in cs:
                    act.wait_ge(sk_done, 4 * s + c + 1)
                    act.copy(KTS[:, j, c, 0:PAST], PS[:, c, :]).then_inc(kt_ready, 1)

            def sample_exp(s, j):
                act.wait_ge(snm, s + 1)
                act.activation(PSA[:, j, :], PS[0:64, 4:6, :].rearrange("p b n -> p (b n)")[:, 0:KS], ACT.Exp,
                               bias=ST5[:, j, 0:1], accum_out=ST5[:, j, 1:2]).then_inc(sexp, 1)

            def sample_result(s, j):
                act.wait_ge(spt_done, s + 1)
                act.copy(PTS[:, j, 0:NPAGE, :], PS[:, 6, 0:256].rearrange("p (g n) -> p g n", g=NPAGE))
                act.copy(PTS[0:NQ, j, NPAGE, :], PS[0:NQ, 6, 256:320]).then_inc(spt_ready, 1)
                act.wait_ge(spv_done, s + 2)
                act.nop(nofuse=True)
                for h2 in range(2):
                    src = PS[HD * h2:HD * (h2 + 1), 6, PV0:PV0 + 64].rearrange("p (c x) -> p c x", x=16)[:, :, 8 * h2:8 * h2 + NQ]
                    mm = act.activation(QKV[HD * h2:HD * (h2 + 1), 0:HT, bass.ds(TP + s * NQ, NQ)], src, ACT.Copy)
                mm.then_inc(satt, 1)

            def sequence(s, j):
                queries(s + 1, 1 - j)
                keys(s + 1, 1 - j, (0, 1))
                sample_exp(s, j)
                keys(s + 1, 1 - j, (2, 3))
                sample_result(s, j)

            queries(0, 0)
            keys(0, 0, range(HT))
            with act.Fori(0, NC) as it:
                cc = bass.ds(it * C, C)
                sequence(2 * it, 0)
                for q in range(2):
                    act.wait_ge(la_cen, 2 * it + q + 1)
                    act.activation(SQA[:, 2 * q:2 * q + 2, :], YCA[:, 2 * q:2 * q + 2, :], ACT.Square).then_inc(la_sq, 1)
                sequence(2 * it + 1, 1)
                act.wait_ge(la_var, it + 2)
                act.activation(RSA[:], PS[:, 7, 0:C], ACT.Sqrt, bias=EPS).then_inc(la_sd, 1)
                act.wait_ge(la_nrm, 2 * it + 2)
                act.nop(nofuse=True)
                for k in range(HT):
                    act.activation(AEXT[:, k, cc], YCA[:, k, :], ACT.Silu, bias=row(k, R_LAB), scale=row(k, R_LAG)).then_inc(la_act, 1)
            sequence(NS - 2, 0)
            sample_exp(NS - 1, 1)
            sample_result(NS - 1, 1)

            act.wait_ge(satt, 1 + NS)
            act.wait_ge(la_act, HT * NC)
            for c in range(NC):
                for q in range(4):
                    src = AEXT if q < 2 else QKV
                    act.copy(AH[:, 2 * q:2 * q + 2, chunk(c)], src[:, 2 * q % 4:2 * q % 4 + 2, chunk(c)]).then_inc(la_hi, 1)

            def squares(ln, c):
                k = 3 * ln + c
                if k:
                    act.wait_ge(ln_sum2, k)
                for q in range(4):
                    act.wait_ge(ln_cen, 4 * k + q + 1)
                    act.activation(SQ[:, 2 * q:2 * q + 2, :], Y[:, 2 * q:2 * q + 2, chunk(c)], ACT.Square).then_inc(ln_sq, 1)

            def deviation(ln, c):
                k = 3 * ln + c
                act.wait_ge(ln_var, k + 1)
                act.activation(RSD[:, c % 2, :], PS[:, 7, 0:C], ACT.Sqrt, bias=EPS).then_inc(ln_sd, 1)

            def finish(ln, c):
                k, layer, cc = 3 * ln + c, ln // 2, chunk(c)
                g, b = ((R_MG, R_MB), (R_FG, R_FB))[ln % 2]
                for q in range(5):
                    if q < 4:
                        act.wait_ge(ln_nrm, 4 * k + q + 1)
                        for o in (2 * q, 2 * q + 1):
                            last = act.activation(Y[:, o, cc], Y[:, o, cc], ACT.Identity, bias=row(o, b + 2 * layer), scale=row(o, g + 2 * layer))
                        last.then_inc(ln_xf, 1)
                    if q and ln < 3:
                        act.wait_ge(ln_xf, 4 * k + q)
                        act.copy(AH[:, 2 * q - 2:2 * q, cc], Y[:, 2 * q - 2:2 * q, cc]).then_inc(ln_hi, 1)

            def head(ln, split_next, unit, split_after):
                squares(ln, 0)
                split_next()
                deviation(ln, 0)
                squares(ln, 1)
                finish(ln, 0)
                deviation(ln, 1)
                finish(ln, 1)
                for c in range(NC):
                    unit(0, c)
                    if c == 0:
                        squares(ln, 2)
                    if c == 1:
                        deviation(ln, 2)
                        finish(ln, 2)
                    if c == 2:
                        split_after()
                    unit(1, c)

            def out_product(st, dn):
                for q in range(4):
                    if q:
                        act.wait_ge(d_done, dn + 6 * q)
                    split(st + q + 1, 2 * (st + q + 1) % 4)

            def hidden(g, f, gu, j, c, u=None):
                u = 3 * j + c if u is None else u
                v, par = 66 * f + 6 * g + u, u % 2
                gated(gu + 6 * g + u, par, ACT.Silu, S)
                act.wait_ge(gu_free, 2 + gu + 6 * g + u + 1)
                act.copy(HH[:, j, chunk(c)], HF[:, par, :]).then_inc(hh_ready, 1)

            def ffn(f):
                st, gu, dn = ffn_units(f)

                def split_next():
                    act.wait_ge(d_done, dn)
                    split(st + 1, 2 * (st + 1) % 4)

                head(2 * f, split_next, lambda j, c: hidden(0, f, gu, j, c, 2 * c + j), lambda: split(st + 2, 2 * (st + 2) % 4))
                split(st + 3, 2 * (st + 3) % 4)

                def group(it, par, last=False):
                    g = 2 * it + (1 if par else 2)
                    for j in range(3):
                        s1 = st + (3 if par else 6) + j + 1
                        if j == 0:
                            act.wait_ge(d_done, dn + 24 * g)
                        for e in range(0 if last and j == 2 else 2):
                            act.wait_ge(w_loaded[2 * s1 % 4 + e], 16 * (s1 // 2 + 1) + 48 * it)
                            act.copy(WHI[:, 2 * s1 % 4 + e, :], RAW[:, 2 * s1 % 4 + e, :]).then_inc(w_hi, 1)
                        if j < 2:
                            for c in range(NC):
                                hidden(g, f, gu, j, c)

                with act.Fori(0, NG // 2 - 1) as it:
                    group(it, 1)
                    group(it, 0)
                group(NG // 2 - 1, 1)
                group(NG // 2 - 1, 0, last=f == 1)

            def mixed(i):
                for c in range(NC):
                    act.wait_ge(mix_done, 3 * i + c + 1)
                    act.activation(PEXT[:, i, chunk(c)], PS[:, 4 + c, 0:C], ACT.Identity, scale=row(i, R_PS)).then_inc(mix_evac, 1)

            out_product(ST_OUT0, DN_OUT0)
            ffn(0)
            def odd_unit(i, n, j, c):
                if j == 0:
                    gated(GU_ODD + 6 * i + n, n % 2, ACT.Copy, S, BG[:, i, chunk(c)])
                else:
                    gated(GU_ODD + 6 * i + n, n % 2, ACT.Copy, S)

            def odd_next():
                act.wait_ge(d_done, DN_OUT1)
                split(ST_ODD + 1, (2 * ST_ODD + 2) % 4)

            head(1, odd_next, lambda j, c: odd_unit(0, 2 * c + j, j, c), lambda: split(ST_ODD + 2, 2 * ST_ODD % 4))
            act.wait_ge(xt_spill, 48)
            def pooled_high(i):
                act.wait_ge(df_ready, i + 1)
                if i:
                    act.wait_ge(mix_done, 3 * i)
                act.copy(DH[:], DF[i][:, 0:T]).then_inc(dh_ready, 1)

            act.wait_ge(wm_in, 16)
            act.copy(WMH[:], WMR[:]).then_inc(wm_hi, 1)
            pooled_high(0)
            for i in range(1, HT):
                split(ST_ODD + 2 * i + 1, 2 * (ST_ODD + 1) % 4)
                for c in range(NC):
                    odd_unit(i, c, 0, c)
                split(ST_ODD + 2 * i + 2, 2 * ST_ODD % 4)
                mixed(i - 1)
                odd_unit(i, 3, 1, 0)
                pooled_high(i)
                odd_unit(i, 4, 1, 1)
                odd_unit(i, 5, 1, 2)
            mixed(HT - 1)
            act.wait_ge(gu_done, GU_FF1)
            act.wait_ge(mix_evac, 3 + 3 * HT)
            for c in range(NC):
                for q in (2, 3, 0, 1):
                    if c == 0 and q == 0:
                        act.wait_ge(oc_done, HT)
                    src = BG if q < 2 else PEXT
                    act.copy(AH[:, 2 * q:2 * q + 2, chunk(c)], src[:, 2 * q % 4:2 * q % 4 + 2, chunk(c)]).then_inc(la_hi, 1)
            out_product(ST_OUT1, DN_OUT1)
            ffn(1)
            squares(3, 0)
            deviation(3, 0)
            squares(3, 1)
            finish(3, 0)
            deviation(3, 1)
            finish(3, 1)
            squares(3, 2)
            deviation(3, 2)
            finish(3, 2)

        @block.vector
        def _(dve):
            dve.sem_inc(t_free, 4)
            dve.sem_inc(gu_free, 2)
            dve.sem_inc(d_free, 3)
            dve.sem_inc(pta_ready, 1)
            dve.sem_inc(ot_free, 1)

            def f32(ap):
                return ap.bitcast(F32)

            def two(ap):
                return ap.unsqueeze(1).to_broadcast([P, 2, C])

            def low(out, x, hi):
                return dve.tensor_tensor(out, x, f32(hi), ALU.subtract)

            def split_slot(n, pos, j):
                dve.wait_ge(w_hi, n + j + 1)
                low(WLO[:, pos + j, :], RAW[:, pos + j, :], WHI[:, pos + j, :]).then_inc(w_lo, 1)

            def split(n, pos):
                for j in range(2):
                    split_slot(n, pos, j)

            def split_stage(s):
                split(2 * s, 2 * s % 4)

            def x_tile(i):
                for h in range(2):
                    u, cols = 2 * i + h, slice(i * P, i * P + tw[i])
                    dve.wait_ge(xt_copy, u + 1)
                    src = PS[:, 4 + u % 4, :].rearrange("p (k n) -> p k n", k=4)[:, :, 0:tw[i]]
                    low(AL[:, 4 * h:4 * h + 4, cols], src, AH[:, 4 * h:4 * h + 4, cols]).then_inc(t_free, 1)

            def to_ext(tile, h, k, c, op):
                lo, hi = c * C, min((c + 1) * C, TP)
                last = op(prompt_cols(tile, h, k, lo, hi), slice(0, hi - lo), False)
                if (c + 1) * C > TP:
                    last = op(sample_cols(tile, h, k), slice(TP - lo, C), True)
                return last

            def product(par, s_tile):
                def op(out, cols, seq):
                    a, b = PS[:, 2 * par + 1, cols], s_tile[:, par, cols]
                    return dve.tensor_tensor(out, by_seq(a) if seq else a, by_seq(b) if seq else b, ALU.mult)
                return op

            def plain(par):
                def op(out, cols, seq):
                    a = PS[:, 2 * par + 1, cols]
                    return dve.tensor_copy(out, by_seq(a) if seq else a)
                return op

            def gated_a(k, c):
                n = 3 * k + c
                dve.wait_ge(s_ready, n + 1)
                to_ext(AEXT, HA, k, c, product(n % 2, S)).then_inc(gu_free, 1)

            for c in range(NC):
                for i in range(3 * c, 3 * c + 3):
                    x_tile(i)
                if c != 1:
                    split_stage(c // 2)
                gated_a(0, c)
            u = TU_PAR
            dve.wait_ge(t_done, u + 1)
            dve.tensor_copy(PRT[:], PS[:, 4 + u % 4, 0:HT * R_ALL].rearrange("p (k n) -> p k n", k=HT)).then_inc(t_free, 1)
            for i in range(2):
                u = TU_SA + i
                dve.wait_ge(t_done, u + 1)
                for k in range(HT):
                    src = PS[:, 4 + u % 4, 4 * HA * k:4 * HA * (k + 1)].rearrange("p (s e) -> p s e", s=4)
                    last = dve.tensor_copy(history(AEXT, HA, k, 4 * i, 4), src)
                last.then_inc(t_free, 1)

            def taps():
                steps = 0
                for k in range(HT - 1):
                    dve.wait_ge(ext_zero, 1)
                    dve.wait_ge(t_free, 4 + TU_A)
                    dve.wait_ge(gu_free, 2 + 3 * (k + 1))
                    if k:
                        dve.wait_ge(conv_done, k)
                    for j in range(CW):
                        if steps:
                            dve.wait_ge(acc_step, steps)
                        acc_p, acc_s = CACC[:, 0:TP], by_seq(CACC[:, TP:T])
                        in_p, in_s = prompt_cols(AEXT, HA, k, 0, TP, HA - j), sample_cols(AEXT, HA, k, HA - j)
                        if j == 0:
                            for acc, src in ((acc_p, in_p), (acc_s, in_s)):
                                dve.tensor_scalar(acc, src, row(k, R_DW), row(k, R_BDW), ALU.mult, ALU.add).then_inc(acc_step, 1)
                            steps += 2
                        elif j < CW - 1:
                            for acc, src in ((acc_p, in_p), (acc_s, in_s)):
                                dve.scalar_tensor_tensor(acc, src, row(k, R_DW + j), acc, ALU.mult, ALU.add).then_inc(acc_step, 1)
                            steps += 2
                        else:
                            dve.scalar_tensor_tensor(acc_p, in_p, row(k, R_DW + j), acc_p, ALU.mult, ALU.add)
                            dve.scalar_tensor_tensor(acc_s, in_s, row(k, R_DW + j), acc_s, ALU.mult, ALU.add).then_inc(acc_done, 1)
                            dve.wait_ge(acc_done, k + 1)
                            dve.tensor_copy(AEXT[:, k, 0:T], CACC[:]).then_inc(conv_done, 1)
                        yield

            conv = taps()
            for k in range(1, HT):
                split_stage(k + 1)
                for c in range(NC):
                    gated_a(k, c)
                    for _ in range(3):
                        next(conv)
            dve.wait_ge(wf_hi, 1)
            low(WFL[:], WFR[:], WFH[:]).then_inc(wf_lo, 1)
            for u, tile, rows in ((TU_A, STA, HA), (TU_A + 1, STB, NS * NQ)):
                dve.wait_ge(t_done, u + 1)
                dve.tensor_copy(tile[:], PS[0:rows, 4 + u % 4, :]).then_inc(t_free, 1)

            for q in range(6):
                split_stage(ST_QKV + q + 1)
                if q == 5:
                    dve.wait_ge(sta_sent, 16 * (1 + NS))
                for c in range(NC):
                    n = 3 * q + c
                    dve.wait_ge(s_ready, GU_QKV + n + 1)
                    dve.tensor_copy(QKV[:, 2 * q + 1, chunk(c)], PS[:, 2 * (n % 2) + 1, 0:C]).then_inc(gu_free, 1)
                    for _ in range(TAPS):
                        next(conv, None)
            for _ in conv:
                pass
            dve.wait_ge(f_done, NC)
            dve.memset(KS2[64:96, :, :].bitcast(F32), 1.0).then_inc(kb_fill, 1)
            dve.memset(QBA[:], -1.0).then_inc(kb_fill, 1)

            def kv_rows(ns):
                for n in ns:
                    u = TU_KV + n
                    dve.wait_ge(t_done, u + 1)
                    if n >= 4:
                        dve.wait_ge(stg_sent[n % 4], 16 * (n // 4))
                    rows = tw[n // 2]
                    dve.tensor_copy(STG[0:rows, n % 4, :], PS[0:rows, 4 + u % 4, :]).then_inc(t_free, 1)

            kv_rows(range(8))
            dve.wait_ge(f_act, NC + 3)
            dve.scalar_tensor_tensor(LFZ[:, 2, :], LFZ[:, 0, :], 0.0, LFZ[:, 1, :], ALU.min, ALU.subtract).then_inc(lf_ready, 1)
            dve.wait_ge(lf_ready, 1)
            dve.tensor_tensor_scan(LFC[:], CST[0:NH, K_ONE:K_ONE + 1].to_broadcast([NH, TP]), LFZ[:, 2, 0:TP], 0.0,
                                   ALU.mult, ALU.add).then_inc(c_ready, 1)
            dve.wait_ge(c_hi, 1)
            low(LCL[:], LFC[:], LCH[:]).then_inc(c_lo, 1)
            kv_rows(range(8, 2 * NTT))
            u = TU_LF
            dve.wait_ge(t_done, u + 1)
            dve.tensor_copy(LFO[:, 0:8, :], PS[:, 4 + u % 4, 0:8 * NH].rearrange("p (b h) -> p b h", b=8))
            dve.tensor_copy(LFO[0:tw[8], 8, :], PS[0:tw[8], 4 + u % 4, 8 * NH:9 * NH]).then_inc(t_free, 1)

            def peak(it, a, h2, j, i, m, n, na, nb):
                base = (0, 3)[a % 2]
                dve.wait_ge(qk_done, 36 * it + a + 1)
                src = PS[0:m, base:base + (n + 511) // 512, :].rearrange("p b n -> p (b n)")[:, 0:n]
                dve.tensor_reduce(ST4[0:m, 0, a:a + 1], src, AX_X, ALU.max, negate=True).then_inc(nm_ready, 1)

            def inverse(it, a, h2, j, i, m, n, na, nb):
                dve.wait_ge(exp_done, 36 * it + a + 3)
                dve.reciprocal(ST4[0:m, 2, a:a + 1], ST4[0:m, 1, a:a + 1]).then_inc(rc_ready, 1)

            def turned(it, a, h2, j, i, m, n, na, nb):
                bank = PS[:, 5, :].rearrange("p (k n) -> p k n", k=4)
                dve.wait_ge(ta_done, NA * it + na + 1)
                w = min(4, i + 1)
                dve.tensor_copy(PT[:, a % 2, 0:w, 0:m], bank[:, 0:w, 0:m]).then_inc(pta_ready, 1)
                if i == 8:
                    dve.wait_ge(ta_done, NA * it + na + 2)
                    dve.tensor_copy(PT[0:META, a % 2, 8, 0:m], PS[0:META, 5, 0:m]).then_inc(pta_ready, 1)

            dve.wait_ge(ab_open, 1)
            def head_low(it, x, part):
                h2 = x % 2
                own, other = slice(HD * h2, HD * (h2 + 1)), slice(HD * (1 - h2), HD * (2 - h2))
                if part == 0:
                    dve.wait_ge(qk_hi, 16 * it + 4 * x + 1)
                    src = QKV[own, bass.ds(2 * it + x // 2 + HT, 1), 0:TP].rearrange("p a n -> p (a n)")
                    low(KS2[0:HD, h2, :], src, KS1[own, h2, :]).then_inc(qk_lo, 1)
                elif part == 1:
                    dve.wait_ge(qk_hi, 16 * it + 4 * x + 2)
                    src = QKV[own, bass.ds(2 * it + x // 2, 1), 0:TP].rearrange("p a n -> p (a n)")
                    dve.scalar_tensor_tensor(QS1[other, h2, :], src, HD ** -0.5, f32(QS1[own, h2, :]), ALU.mult, ALU.subtract).then_inc(qk_lo, 1)
                else:
                    dve.tensor_scalar(QS2[64:96, h2, :], QBA[:], CST[0:32, bass.ds(K_MSK + 4 * it + x, 1)], None, ALU.mult).then_inc(qk_lo, 1)

            with dve.Fori(0, 2) as it:
                for part in range(3):
                    head_low(it, 0, part)
                for n in range(36 + 2):
                    if 1 <= n < 37:
                        inverse(it, *ATT[n - 1])
                    if n < 36:
                        peak(it, *ATT[n])
                    if n >= 2:
                        turned(it, *ATT[n - 2])
                    if n < 27 and n % 9 in (4, 5, 6):
                        head_low(it, n // 9 + 1, n % 9 - 4)

            dve.wait_ge(t_done, TU_LFS + 1)
            dve.tensor_copy(LFS[:, 0:PAST], PS[0:64, 6, :]).then_inc(t_free, 1)
            dve.wait_ge(t_free, 4 + TU_LFS + 1)
            dve.wait_ge(lfs_in, 16)
            dve.tensor_tensor_scan(KBS[0:64, :], CST[0:64, K_ONE:K_ONE + 1].to_broadcast([64, KS]), LFS[:], 0.0,
                                   ALU.mult, ALU.add).then_inc(cs_ready, 1)
            dve.wait_ge(sel_in, 16)
            dve.wait_ge(cq_ready, 1)
            half = SELC[64:128].rearrange("p s h q -> p (s h) q")
            dve.tensor_tensor(half, half, CQ2[64:128, :].unsqueeze(1).to_broadcast([64, NS * NH, NQ]), ALU.mult).then_inc(sel_ready, 1)

            def softmax(s, j):
                dve.wait_ge(sqk_done, s + 1)
                dve.tensor_reduce(ST5[:, j, 0:1], PS[0:64, 4:6, :].rearrange("p b n -> p (b n)")[:, 0:KS], AX_X, ALU.max,
                                  negate=True).then_inc(snm, 1)
                dve.wait_ge(sexp, s + 2)
                dve.reciprocal(ST5[:, j, 2:3], ST5[:, j, 1:2]).then_inc(s_inverse, 1)
                dve.wait_ge(s_inverse, s + 1)
                dve.tensor_scalar(PSA[:, j, :], PSA[:, j, :], ST5[:, j, 2:3], None, ALU.mult).then_inc(spn, 1)

            with dve.Fori(0, NC) as it:
                softmax(2 * it, 0)
                dve.wait_ge(la_mean, it + 1)
                for q in range(2):
                    qs = slice(2 * q, 2 * q + 2)
                    dve.tensor_tensor(YCA[:, qs, :], AEXT[:, qs, bass.ds(it * C, C)], two(PS[:, 7, 0:C]), ALU.subtract).then_inc(la_cen, 1)
                softmax(2 * it + 1, 1)
                dve.wait_ge(la_sd, it + 1)
                dve.reciprocal(RSA[:], RSA[:]).then_inc(la_rs, 1)
                dve.wait_ge(la_rs, it + 1)
                for q in range(2):
                    qs = slice(2 * q, 2 * q + 2)
                    dve.tensor_tensor(YCA[:, qs, :], YCA[:, qs, :], two(RSA[:]), ALU.mult).then_inc(la_nrm, 1)
            softmax(NS - 2, 0)
            softmax(NS - 1, 1)

            for c in range(NC):
                for q in range(4):
                    src, qs = AEXT if q < 2 else QKV, slice(2 * q, 2 * q + 2)
                    dve.wait_ge(la_hi, 4 * c + q + 1)
                    low(AL[:, qs, chunk(c)], src[:, 2 * q % 4:2 * q % 4 + 2, chunk(c)], AH[:, qs, chunk(c)]).then_inc(m_ready, 1)

            def centre(ln, c, qs=range(4)):
                k, cc = 3 * ln + c, chunk(c)
                for q in qs:
                    ts = slice(2 * q, 2 * q + 2)
                    dve.wait_ge(ln_mean, k + 1)
                    dve.tensor_tensor(Y[:, ts, cc], Y[:, ts, cc], two(PS[:, MEAN_BANK[c], 0:C]), ALU.subtract).then_inc(ln_cen, 1)

            def normalise(ln, c):
                k, cc, rs = 3 * ln + c, chunk(c), RSD[:, c % 2, :]
                dve.wait_ge(ln_sd, k + 1)
                dve.reciprocal(rs, rs).then_inc(ln_rs, 1)
                dve.wait_ge(ln_rs, k + 1)
                for q in range(4):
                    ts = slice(2 * q, 2 * q + 2)
                    dve.wait_ge(ln_sq, 4 * k + q + 1)
                    dve.tensor_tensor(Y[:, ts, cc], Y[:, ts, cc], two(rs), ALU.mult).then_inc(ln_nrm, 1)

            def x_low(ln, c):
                k, cc = 3 * ln + c, chunk(c)
                for q in range(4):
                    ts = slice(2 * q, 2 * q + 2)
                    dve.wait_ge(ln_hi, 4 * k + q + 1)
                    low(AL[:, ts, cc], Y[:, ts, cc], AH[:, ts, cc]).then_inc(x_ready, 1)

            def head(ln, split_next, unit, split_after):
                split_next()
                centre(ln, 1)
                normalise(ln, 0)
                x_low(ln, 0)
                normalise(ln, 1)
                x_low(ln, 1)
                for c in range(NC):
                    unit(0, c)
                    if c == 0:
                        centre(ln, 2)
                    if c == 1:
                        normalise(ln, 2)
                        x_low(ln, 2)
                    if c == 2:
                        split_after()
                    unit(1, c)

            def out_product(layer, st, dn):
                for q in range(4):
                    split_stage(st + q + 1)
                    for c in range(NC):
                        for w in range(2):
                            n, o = 6 * q + 2 * c + w, 2 * q + w
                            if q == 3 and c == 2:
                                centre(2 * layer, 0, (2 * w, 2 * w + 1))
                            if c == 0:
                                dve.wait_ge(y_in[o], 16 * (layer + 1))
                            dve.wait_ge(d_done, dn + n + 1)
                            y = Y[:, o, chunk(c)]
                            dve.scalar_tensor_tensor(y, y, ALPHA, PS[:, 4 + n % 3, 0:C], ALU.mult, ALU.add).then_inc(d_free, 1)

            def hidden(g, f, gu, j, c, u=None):
                u = 3 * j + c if u is None else u
                unit, v, par = gu + 6 * g + u, 66 * f + 6 * g + u, u % 2
                dve.wait_ge(s_ready, unit + 1)
                dve.tensor_tensor(HF[:, par, :], S[:, par, :], PS[:, 2 * par + 1, 0:C], ALU.mult).then_inc(gu_free, 1)
                dve.wait_ge(hh_ready, v + 1)
                low(HL[:, j, chunk(c)], HF[:, par, :], HH[:, j, chunk(c)]).then_inc(h_ready, 1)

            def down(g, f, dn, split_slot, first=False, last=False):
                for c in range(NC):
                    for o in range(KT):
                        n = 8 * c + o
                        if last and c == 2 and o % 2 == 0:
                            centre(2 * f + 1, 0, (o // 2,))
                        dve.wait_ge(d_done, dn + 24 * g + n + 1)
                        y = Y[:, o, chunk(c)]
                        if first:
                            dve.scalar_tensor_tensor(y, y, ALPHA, PS[:, 4 + n % 3, 0:C], ALU.mult, ALU.add).then_inc(d_free, 1)
                        else:
                            dve.tensor_tensor(y, y, PS[:, 4 + n % 3, 0:C], ALU.add).then_inc(d_free, 1)
                        if n in (4, 9):
                            split_slot(n // 9)

            def ffn(f):
                st, gu, dn = ffn_units(f)
                head(2 * f, lambda: split_stage(st + 1), lambda j, c: hidden(0, f, gu, j, c, 2 * c + j), lambda: split_stage(st + 2))
                down(0, f, dn, lambda j: split_slot(2 * (st + 3), 2 * (st + 3) % 4, j), first=True)

                def group(it, par, last=False):
                    g = 2 * it + (1 if par else 2)
                    s0 = st + (3 if par else 6)
                    for j in range(2):
                        split(2 * (s0 + j + 1) + 12 * it, 2 * (s0 + j + 1) % 4)
                        for c in range(NC):
                            hidden(g, f, gu, j, c)
                    down(g, f, dn, lambda j: None if last and f == 1 else split_slot(2 * (s0 + 3) + 12 * it, 2 * (s0 + 3) % 4, j), last=last)

                with dve.Fori(0, NG // 2 - 1) as it:
                    group(it, 1)
                    group(it, 0)
                group(NG // 2 - 1, 1)
                group(NG // 2 - 1, 0, last=True)

            out_product(0, ST_OUT0, DN_OUT0)
            ffn(0)

            steps = [0]

            def step(ins):
                steps[0] += 1
                ins.then_inc(tap, 1)
                dve.wait_ge(tap, steps[0])

            def new_rows(i):
                dve.wait_ge(ot_done, i + 1)
                cs = slice(i * P, (i + 1) * P)
                dve.tensor_copy(OSA[0:NS * NQ, cs], PS[0:NS * NQ, 7, 0:P])
                dve.tensor_copy(OSA[64:64 + HS, cs], PS[0:HS, 7, P:2 * P])
                dve.tensor_copy(OSA[96:96 + HP, cs], PS[0:HP, 7, 2 * P:3 * P])
                dve.tensor_copy(OSB[:, cs], PS[0:NS * HS, 7, 3 * P:4 * P]).then_inc(ot_free, 1)

            def odd_unit(i, n, j, c):
                dve.wait_ge(s_ready, GU_ODD + 6 * i + n + 1)
                if j == 0:
                    to_ext(PEXT, HP, i, c, plain(n % 2)).then_inc(gu_free, 1)
                else:
                    to_ext(YEXT, HS, i, c, product(n % 2, S)).then_inc(gu_free, 1)

            head(1, lambda: split_stage(ST_ODD + 1), lambda j, c: odd_unit(0, 2 * c + j, j, c), lambda: split_stage(ST_ODD + 2))
            dve.wait_ge(xt_spill, 48)
            for u, bank, tile, h in ((TU_ST, 7, YEXT, HS), (TU_ST + 1, 4, PEXT, HP)):
                dve.wait_ge(t_done, u + 1)
                for k in range(HT):
                    last = dve.tensor_copy(history(tile, h, k, 0, NS), by_seq(PS[:, bank, NS * h * k:NS * h * (k + 1)]))
                last.then_inc(t_free, 1)
            dve.wait_ge(od_zero, 2)
            def pooling(i):
                if i:
                    dve.wait_ge(oc_done, i)
                src, lo = PEXT[:, i, :], 0
                for d in range(i + 1):
                    w, dst = 1 << d, (T2, T1)[d % 2]
                    step(dve.tensor_tensor(dst[:, lo + w:EP], src[:, lo + w:EP], src[:, lo:EP - w], ALU.add))
                    src, lo = dst, lo + w
                w, df = 2 << i, DF[i]
                first = src[:, HP:HP + PW]
                step(dve.tensor_tensor(first, first, CST[:, K_CNT + PW * i:K_CNT + PW * (i + 1)], ALU.mult))
                dve.tensor_tensor(df[:, 0:PW], first, PEXT[:, i, HP:HP + PW], ALU.subtract)
                dve.scalar_tensor_tensor(df[:, PW:TP], src[:, HP + PW:HP + TP], 1.0 / w, PEXT[:, i, HP + PW:HP + TP], ALU.mult, ALU.subtract)
                sums = src[:, HP + TP:EP].rearrange("p (s e) -> p s e", s=NS)[:, :, HP:]
                dve.scalar_tensor_tensor(by_seq(df[:, TP:T]), sums, 1.0 / w, sample_cols(PEXT, HP, i), ALU.mult, ALU.subtract).then_inc(df_ready, 1)

            def pooled_low(i):
                dve.wait_ge(dh_ready, i + 1)
                low(DL[:], DF[i][:, 0:T], DH[:]).then_inc(dl_ready, 1)

            def short_conv(i):
                if i:
                    dve.wait_ge(ot_done, i)
                dve.wait_ge(gu_free, 2 + GU_ODD + 6 * (i + 1))
                dve.tensor_copy(by_seq(CMP[:, 0:NS * HS]), sample_cols(YEXT, HS, i)[:, :, NQ - HS:])
                dve.tensor_copy(by_seq(CMP[:, NS * HS:]), sample_cols(PEXT, HP, i)).then_inc(cmp_ready, 1)
                dve.wait_ge(dl_ready, i + 1)
                for j in range(SW):
                    for acc, src in ((T1[:, 0:TP], prompt_cols(YEXT, HS, i, 0, TP, HS - j)),
                                     (by_seq(T1[:, TP:T]), sample_cols(YEXT, HS, i, HS - j))):
                        if j == 0:
                            step(dve.tensor_scalar(acc, src, row(i, R_SC), None, ALU.mult))
                        else:
                            step(dve.scalar_tensor_tensor(acc, src, row(i, R_SC + j), acc, ALU.mult, ALU.add))
                dve.tensor_tensor(BG[:, i, :], BG[:, i, :], T1[:, 0:T], ALU.mult).then_inc(oc_done, 1)

            dve.wait_ge(wm_hi, 1)
            low(WML[:], WMR[:], WMH[:]).then_inc(wm_lo, 1)
            dve.wait_ge(t_free, 4 + TU_ST + 2)
            pooling(0)
            pooled_low(0)
            short_conv(0)
            for i in range(1, HT):
                split_stage(ST_ODD + 2 * i + 1)
                for c in range(NC):
                    odd_unit(i, c, 0, c)
                split_stage(ST_ODD + 2 * i + 2)
                dve.wait_ge(gu_free, 2 + GU_ODD + 6 * i + 3)
                pooling(i)
                odd_unit(i, 3, 1, 0)
                new_rows(i - 1)
                pooled_low(i)
                odd_unit(i, 4, 1, 1)
                odd_unit(i, 5, 1, 2)
                short_conv(i)
            new_rows(HT - 1)
            for c in range(NC):
                for n, q in enumerate((2, 3, 0, 1)):
                    src = BG if q < 2 else PEXT
                    dve.wait_ge(la_hi, 12 + 4 * c + n + 1)
                    qs = slice(2 * q, 2 * q + 2)
                    low(AL[:, qs, chunk(c)], src[:, 2 * q % 4:2 * q % 4 + 2, chunk(c)], AH[:, qs, chunk(c)]).then_inc(m_ready, 1)
            out_product(1, ST_OUT1, DN_OUT1)
            ffn(1)

            def y_rows(c):
                n = sum(len(YPIECES[x]) for x in range(c))
                for a, w in YPIECES[c]:
                    for h in range(2):
                        u = 2 * n + h
                        dve.wait_ge(t_done, TU_Y + u + 1)
                        if n >= 4:
                            dve.wait_ge(yo_sent[n % 4], 16 * (n // 4))
                        dve.tensor_copy(YO[0:w, n % 4, h * HALF:(h + 1) * HALF], PS[0:w, u % 4, :]).then_inc(t_free, 1)
                    n += 1

            centre(3, 1)
            normalise(3, 0)
            normalise(3, 1)
            y_rows(0)
            centre(3, 2)
            y_rows(1)
            normalise(3, 2)
            y_rows(2)


_INS = ["x_prompt", "x_sample", "cache_k", "cache_v", "cache_logf", "page_table", "state_conv_a", "state_sconv", "state_pool",
        "meta_tokens", "w_in_even", "b_forget", "w_dw_a", "b_dw_a", "ln_a_g", "ln_a_b", "w_out_even", "w_in_odd", "w_sconv",
        "w_pool_mix", "pool_scale", "w_out_odd", "ln_mix_g", "ln_mix_b", "w_ffn_gate", "w_ffn_up", "w_ffn_down", "ln_ffn_g",
        "ln_ffn_b"]
_OUTS = [("y_prompt", (1, SEQ, D)), ("y_sample", (NS, NQ, D)), ("k_prompt", (1, 1, TP, NH, HD)), ("v_prompt", (1, 1, TP, NH, HD)),
         ("logf_prompt", (1, 1, TP, NH)), ("conv_a_prompt", (1, 1, HA, HALF)), ("sconv_prompt", (1, 1, HS, HALF)),
         ("pool_prompt", (1, 1, HP, HALF)), ("k_sample", (NS, 1, NQ, NH, HD)), ("v_sample", (NS, 1, NQ, NH, HD)),
         ("logf_sample", (NS, 1, NQ, NH)), ("conv_a_sample", (NS, 1, HA, HALF)), ("sconv_sample", (NS, 1, HS, HALF)),
         ("pool_sample", (NS, 1, HP, HALF))]


def kernel(**inputs):
    import concourse.bacc as bacc
    from concourse.bass_utils import run_bass_kernel_spmd

    nc = bacc.Bacc("TRN2", target_bir_lowering=False, num_devices=1)
    arrays, aps = {}, {}
    for name in _INS + ["consts"]:
        a = constants() if name == "consts" else np.ascontiguousarray(inputs[name])
        arrays[f"in_{name}"] = a
        aps[name] = nc.dram_tensor(f"in_{name}", a.shape, mybir.dt.from_np(a.dtype), kind="ExternalInput").ap()
    for name, shape in _OUTS:
        aps[name] = nc.dram_tensor(f"out_{name}", shape, F32, kind="ExternalOutput").ap()
    build(nc, aps)
    r = run_bass_kernel_spmd(nc, [arrays], core_ids=[0])
    return tuple(r.results[0][f"out_{name}"] for name, _ in _OUTS)
```
